# Optimizing a Trainium2 kernel written in Bass

```python
import math
import jax, jax.numpy as jnp
from jax import lax
import numpy as np

D_MODEL = 1024
BATCH = 1
SEQ = 512
DEPTH = 2

N_EVEN = (DEPTH + 1) // 2
N_ODD = DEPTH // 2
D_FF = 256 * ((8 * D_MODEL // 3 + 255) // 256)
NORM_EPS = 1e-6
SC_WIDTH = D_MODEL // 2
SC_KERNEL = 3
ATT_HEAD_DIM = 64
ATT_HEADS = D_MODEL // 128
ATT_WIDTH = ATT_HEADS * ATT_HEAD_DIM
IDX_HEADS = D_MODEL // 128
IDX_DIM = ATT_HEAD_DIM
TOPK_MAX = 256
Q_BLOCK = 128
EV_MIX_WIDTH = SC_WIDTH + ATT_WIDTH
EV_PROJ = 3 * SC_WIDTH + 3 * ATT_WIDTH + IDX_HEADS * IDX_DIM + IDX_DIM + IDX_HEADS
DN_HEAD_DIM = 128
DN_HEADS = D_MODEL // 128
DN_WIDTH = DN_HEADS * DN_HEAD_DIM
DN_KERNEL = 4
CHUNK = 64
OD_PROJ = 4 * DN_WIDTH + 2 * DN_HEADS
ROPE_THETA = 500000.0
ROPE_DIM = ATT_HEAD_DIM // 4

kernel_name = "hybrid_conv_dsa_gdn_macaron"

def rmsnorm(x, gain):
    xf = x.astype(jnp.float32)
    y = xf * lax.rsqrt(jnp.mean(xf * xf, axis=-1, keepdims=True) + NORM_EPS)
    return (y * gain.astype(jnp.float32)).astype(x.dtype)

def l2norm(x):
    xf = x.astype(jnp.float32)
    return (xf * lax.rsqrt(jnp.sum(xf * xf, axis=-1, keepdims=True) + NORM_EPS)).astype(x.dtype)

def split_cols(t, sizes):
    return jnp.split(t, np.cumsum(sizes)[:-1].tolist(), axis=-1)

def swiglu(h, w_gate, w_up, w_down):
    return (jax.nn.silu(h @ w_gate) * (h @ w_up)) @ w_down

def rope_tables(positions):
    inv_freq = ROPE_THETA ** (-jnp.arange(0, ROPE_DIM, 2, dtype=jnp.float32) / ROPE_DIM)
    ang = positions.astype(jnp.float32)[..., None] * inv_freq
    return jnp.cos(ang), jnp.sin(ang)

def apply_partial_rope(x, cos, sin):
    half = ROPE_DIM // 2
    c = cos[:, :, None, :].astype(x.dtype)
    s = sin[:, :, None, :].astype(x.dtype)
    x1, x2, rest = x[..., :half], x[..., half:ROPE_DIM], x[..., ROPE_DIM:]
    return jnp.concatenate([x1 * c - x2 * s, x2 * c + x1 * s, rest], axis=-1)

def causal_depthwise_conv(u, w):
    width, seq = w.shape[0], u.shape[1]
    up = jnp.pad(u, ((0, 0), (width - 1, 0), (0, 0)))
    out = up[:, 0:seq] * w[0]
    for j in range(1, width):
        out = out + up[:, j:j + seq] * w[j]
    return out

def dsa_attention(q, k, v, q_idx, k_idx, w_idx, top_k):
    bsz, seq, heads, hd = q.shape
    n_blocks = seq // Q_BLOCK
    key_pos = jnp.arange(seq, dtype=jnp.int32)
    scale = hd ** -0.5
    gather = jax.vmap(lambda t, i: t[i])

    def blocks(t):
        return jnp.moveaxis(t.reshape((bsz, n_blocks, Q_BLOCK) + t.shape[2:]), 1, 0)

    def one_block(args):
        start, qb, qib, wb = args
        tpos = start + jnp.arange(Q_BLOCK, dtype=jnp.int32)
        admissible = key_pos[None, :] <= tpos[:, None]
        score = jax.nn.relu(jnp.einsum('bthd,bsd->bths', qib, k_idx))
        score = jnp.einsum('bths,bth->bts', score, wb).astype(jnp.float32)
        score = jnp.where(admissible[None], score, -jnp.inf)
        _, sel = lax.top_k(score, top_k)
        k_sel = gather(k, sel)
        v_sel = gather(v, sel)
        logits = jnp.einsum('bthd,btkhd->bthk', qb, k_sel).astype(jnp.float32) * scale
        valid = (sel <= tpos[None, :, None])[:, :, None, :]
        probs = jax.nn.softmax(jnp.where(valid, logits, -jnp.inf), axis=-1).astype(v.dtype)
        return jnp.einsum('bthk,btkhd->bthd', probs, v_sel)

    starts = jnp.arange(n_blocks, dtype=jnp.int32) * Q_BLOCK
    out = lax.map(one_block, (starts, blocks(q), blocks(q_idx), blocks(w_idx)))
    return jnp.moveaxis(out, 0, 1).reshape(bsz, seq, heads * hd)

def conv_sparse_attn_mixer(h, cos, sin, w_in, conv_w, w_out, top_k):
    bsz, seq, _ = h.shape
    parts = split_cols(h @ w_in, [SC_WIDTH] * 3 + [ATT_WIDTH] * 3 + [IDX_HEADS * IDX_DIM, IDX_DIM, IDX_HEADS])
    sc_b, sc_c, sc_x, q, k, v, q_idx, k_idx, w_idx = parts
    y_conv = sc_b * causal_depthwise_conv(sc_c * sc_x, conv_w)
    q = apply_partial_rope(q.reshape(bsz, seq, ATT_HEADS, ATT_HEAD_DIM), cos, sin)
    k = apply_partial_rope(k.reshape(bsz, seq, ATT_HEADS, ATT_HEAD_DIM), cos, sin)
    v = v.reshape(bsz, seq, ATT_HEADS, ATT_HEAD_DIM)
    q_idx = apply_partial_rope(q_idx.reshape(bsz, seq, IDX_HEADS, IDX_DIM), cos, sin)
    k_idx = apply_partial_rope(k_idx[:, :, None, :], cos, sin)[:, :, 0]
    w_idx = w_idx * (IDX_HEADS * IDX_DIM) ** -0.5
    y_attn = dsa_attention(q, k, v, q_idx, k_idx, w_idx, top_k)
    return jnp.concatenate([y_conv, y_attn], axis=-1) @ w_out

def gated_delta_rule(q, k, v, g, beta):
    bsz, seq, heads, dk = q.shape
    dv = v.shape[-1]
    n_chunks = seq // CHUNK

    def chunks(t):
        t = jnp.moveaxis(t, 2, 1).astype(jnp.float32)
        return t.reshape(t.shape[:2] + (n_chunks, CHUNK) + t.shape[3:])

    q, k, v, g, beta = (chunks(t) for t in (q, k, v, g, beta))
    g = jnp.cumsum(g, axis=-1)
    causal = jnp.tril(jnp.ones((CHUNK, CHUNK), dtype=bool))
    strict = jnp.tril(jnp.ones((CHUNK, CHUNK), dtype=bool), k=-1)
    diff = g[..., :, None] - g[..., None, :]
    decay = jnp.where(causal, jnp.exp(jnp.where(causal, diff, 0.0)), 0.0)
    k_beta = k * beta[..., None]
    a_mat = jnp.where(strict, jnp.einsum('bhnid,bhnjd->bhnij', k_beta, k) * decay, 0.0)
    eye = jnp.eye(CHUNK, dtype=jnp.float32)
    t_inv = lax.linalg.triangular_solve(a_mat + eye, jnp.broadcast_to(eye, a_mat.shape),
                                        left_side=True, lower=True, unit_diagonal=True)
    u = jnp.einsum('bhnij,bhnjd->bhnid', t_inv, v * beta[..., None])
    w = jnp.einsum('bhnij,bhnjd->bhnid', t_inv, k_beta * jnp.exp(g)[..., None])
    intra = jnp.einsum('bhnid,bhnjd->bhnij', q, k) * decay
    q_dec = q * jnp.exp(g)[..., None]
    k_dec = k * jnp.exp(g[..., -1:] - g)[..., None]
    chunk_decay = jnp.exp(g[..., -1])
    xs = tuple(jnp.moveaxis(t, 2, 0) for t in (u, w, intra, q_dec, k_dec, chunk_decay))

    def step(state, inp):
        u_n, w_n, intra_n, q_n, k_n, d_n = inp
        v_new = u_n - jnp.einsum('bhcd,bhde->bhce', w_n, state)
        out = jnp.einsum('bhcd,bhde->bhce', q_n, state) + jnp.einsum('bhij,bhje->bhie', intra_n, v_new)
        state = state * d_n[..., None, None] + jnp.einsum('bhcd,bhce->bhde', k_n, v_new)
        return state, out

    state0 = jnp.zeros((bsz, heads, dk, dv), jnp.float32)
    _, out = lax.scan(step, state0, xs)
    out = jnp.moveaxis(out, 0, 2).reshape(bsz, heads, seq, dv)
    return jnp.moveaxis(out, 1, 2)

def gated_deltanet_mixer(h, w_in, conv_w, a_log, dt_bias, o_gain, w_out):
    bsz, seq, _ = h.shape
    qkv, z, b_raw, a_raw = split_cols(h @ w_in, [3 * DN_WIDTH, DN_WIDTH, DN_HEADS, DN_HEADS])
    qkv = jax.nn.silu(causal_depthwise_conv(qkv, conv_w))
    q, k, v = (t.reshape(bsz, seq, DN_HEADS, DN_HEAD_DIM) for t in jnp.split(qkv, 3, axis=-1))
    q = l2norm(q) * DN_HEAD_DIM ** -0.5
    k = l2norm(k)
    beta = jax.nn.sigmoid(b_raw.astype(jnp.float32))
    g = -jnp.exp(a_log.astype(jnp.float32)) * jax.nn.softplus(a_raw.astype(jnp.float32) + dt_bias.astype(jnp.float32))
    o = gated_delta_rule(q, k, v, g, beta).astype(h.dtype)
    o = rmsnorm(o, o_gain) * jax.nn.silu(z.reshape(bsz, seq, DN_HEADS, DN_HEAD_DIM))
    return o.reshape(bsz, seq, DN_WIDTH) @ w_out

def setup_inputs(seed: int = 0) -> dict:
    key = jax.random.key(seed)
    ks = jax.random.split(key, 16)
    f32 = jnp.float32

    def nrm(k, shape, fan_in):
        return jax.random.normal(k, shape, f32) * fan_in ** -0.5

    x = jax.random.normal(ks[0], (BATCH, SEQ, D_MODEL), f32)
    positions = jnp.broadcast_to(jnp.arange(SEQ, dtype=jnp.int32), (BATCH, SEQ))
    norm_gain = 1.0 + 0.02 * jax.random.normal(ks[1], (DEPTH, 3, D_MODEL), f32)
    ffn_w_gate = nrm(ks[2], (DEPTH, 2, D_MODEL, D_FF), D_MODEL)
    ffn_w_up = nrm(ks[3], (DEPTH, 2, D_MODEL, D_FF), D_MODEL)
    ffn_w_down = nrm(ks[4], (DEPTH, 2, D_FF, D_MODEL), D_FF)
    ev_w_in = nrm(ks[5], (N_EVEN, D_MODEL, EV_PROJ), D_MODEL)
    ev_conv_w = nrm(ks[6], (N_EVEN, SC_KERNEL, SC_WIDTH), SC_KERNEL)
    ev_w_out = nrm(ks[7], (N_EVEN, EV_MIX_WIDTH, D_MODEL), EV_MIX_WIDTH)
    od_w_in = nrm(ks[8], (N_ODD, D_MODEL, OD_PROJ), D_MODEL)
    od_conv_w = nrm(ks[9], (N_ODD, DN_KERNEL, 3 * DN_WIDTH), DN_KERNEL)
    od_a_log = jnp.log(jax.random.uniform(ks[10], (N_ODD, DN_HEADS), f32, 1.0, 16.0))
    dt = jnp.exp(jax.random.uniform(ks[11], (N_ODD, DN_HEADS), f32, math.log(1e-3), math.log(1e-1)))
    od_dt_bias = dt + jnp.log(-jnp.expm1(-dt))
    od_o_gain = 1.0 + 0.02 * jax.random.normal(ks[12], (N_ODD, DN_HEAD_DIM), f32)
    od_w_out = nrm(ks[13], (N_ODD, DN_WIDTH, D_MODEL), DN_WIDTH)
    final_gain = 1.0 + 0.02 * jax.random.normal(ks[14], (D_MODEL,), f32)
    return {"x": x, "positions": positions, "norm_gain": norm_gain,
            "ffn_w_gate": ffn_w_gate, "ffn_w_up": ffn_w_up, "ffn_w_down": ffn_w_down,
            "ev_w_in": ev_w_in, "ev_conv_w": ev_conv_w, "ev_w_out": ev_w_out,
            "od_w_in": od_w_in, "od_conv_w": od_conv_w, "od_a_log": od_a_log,
            "od_dt_bias": od_dt_bias, "od_o_gain": od_o_gain, "od_w_out": od_w_out,
            "final_gain": final_gain}

def reference(x, positions, norm_gain, ffn_w_gate, ffn_w_up, ffn_w_down, ev_w_in, ev_conv_w, ev_w_out,
              od_w_in, od_conv_w, od_a_log, od_dt_bias, od_o_gain, od_w_out, final_gain):
    top_k = min(TOPK_MAX, x.shape[1] // 4)
    cos, sin = rope_tables(positions)
    for layer in range(DEPTH):
        i = layer // 2
        x = x + 0.5 * swiglu(rmsnorm(x, norm_gain[layer, 0]), ffn_w_gate[layer, 0], ffn_w_up[layer, 0], ffn_w_down[layer, 0])
        h = rmsnorm(x, norm_gain[layer, 1])
        if layer % 2 == 0:
            x = x + conv_sparse_attn_mixer(h, cos, sin, ev_w_in[i], ev_conv_w[i], ev_w_out[i], top_k)
        else:
            x = x + gated_deltanet_mixer(h, od_w_in[i], od_conv_w[i], od_a_log[i], od_dt_bias[i], od_o_gain[i], od_w_out[i])
        x = x + 0.5 * swiglu(rmsnorm(x, norm_gain[layer, 2]), ffn_w_gate[layer, 1], ffn_w_up[layer, 1], ffn_w_down[layer, 1])
    return rmsnorm(x, final_gain)


_drawn_inputs = setup_inputs


def setup_inputs(seed=0):
    import zlib

    import numpy as np

    out = dict(_drawn_inputs(seed))
    spreads = {}
    factors = {}
    for name, (base, spread) in spreads.items():
        noise = np.random.default_rng([zlib.crc32(name.encode()), seed]).standard_normal(out[name].shape)
        drawn = base * np.exp(spread * noise) if base else spread * noise
        out[name] = __import__('jax').numpy.asarray(drawn.astype(out[name].dtype))
    for name, factor in factors.items():
        out[name] = (out[name] * factor).astype(out[name].dtype)
    return out
```

```python
from contextlib import ExitStack

import numpy as np

import concourse.bass as bass
from concourse import mybir

F32 = mybir.dt.float32
F32R = mybir.dt.float32r
I32 = mybir.dt.int32
ALU = mybir.AluOpType
ACT = mybir.ActivationFunctionType
AX = mybir.AxisListType

P = 128
D = 1024
T = 512
KT = D // P
TT = T // P
DFF = 2816
FT = DFF // P
HALF = FT // 2
NFFN = 4
EPS = 1e-6
HEADS = 8
HD = 64
TOPK = T // 4
ROUNDS = TOPK // 8
LEVELS = 7
NEG = -3.0e38
MARK = -3.3e38
SPLIT = -3.15e38

EV_UNITS = [("ik", 0)] + [("iq", m) for m in range(4)] + [("k", m) for m in range(4)] + [("q", m) for m in range(4)] \
    + [("v", m) for m in range(4)] + [(w, m) for m in range(4) for w in "cxb"]
OD_UNITS = [("ba", 0)] + [(w, h) for h in range(HEADS) for w in "qkvz"]
ROPED = ("iq", "k", "q")

FFN_UNITS, FFN_STEPS = 2 * FT + 2 * KT, FT + KT
EV_N, EV_S = FFN_UNITS, FFN_STEPS
EVO_N, EVO_S = EV_N + len(EV_UNITS), EV_S + len(EV_UNITS)
F1_N, F1_S = EVO_N + KT, EVO_S + KT
F2_N, F2_S = F1_N + FFN_UNITS, F1_S + FFN_STEPS
OD_N, OD_S = F2_N + FFN_UNITS, F2_S + FFN_STEPS
ODO_N, ODO_S = OD_N + len(OD_UNITS), OD_S + len(OD_UNITS)
F3_N, F3_S = ODO_N + KT, ODO_S + KT
FFN_AT = [(0, 0), (F1_N, F1_S), (F2_N, F2_S), (F3_N, F3_S)]
N_END = F3_N + FFN_UNITS
GU0, EV0 = 0, 2 * FT
EVO0 = EV0 + len(EV_UNITS)
GU1 = EVO0 + KT
GU2 = GU1 + 2 * FT
OD0 = GU2 + 2 * FT
ODO0 = OD0 + len(OD_UNITS)
GU3 = ODO0 + KT
GU_ROW = [GU0, GU1, GU2, GU3]
ROWS8 = GU3 + 2 * FT

CONSTS = ["ident", "ones", "tri", "neg_future", "rot", "dup", "dup_rot"] + [f"level{l}" for l in range(1, LEVELS + 1)]


def unit_width(n):
    for n0, _ in FFN_AT:
        if n0 + 2 * FT <= n < n0 + FFN_UNITS:
            return HALF * P
    return KT * P


def ev_extras():
    out = {u: [] for u in range(len(EV_UNITS))}
    idx = [("idx", b, h) for b in range(1, TT) for h in range(HEADS)]
    top = [("top", b, r) for b in range(1, TT) for r in range(ROUNDS)]
    for u in range(len(EV_UNITS)):
        if u >= 6:
            take = 3 if u < 20 else 4
            if idx:
                out[u] += idx[:3]
                del idx[:3]
            done_b = 4 if not idx else idx[0][1]
            while take and top and top[0][1] < done_b:
                out[u].append(top.pop(0))
                take -= 1
    assert not idx
    out["rest"] = top
    return out


STAGES = ["norm", "decay", "gram", "turn1"] + [f"{w}{l}" for l in range(2, LEVELS + 1) for w in ("y", "t")] \
    + ["w"] + [f"{w}{t}" for t in range(TT) for w in ("new", "out")] + ["fin"]


SHIFT = 3
TU = 2 * LEVELS - 1
N_SIDE = 17
Q_ITEMS = TT * HEADS


def norm_of(f):
    return (0, 2, 3, 5)[f]


def pi_parts(value, count, bits=7):
    parts = []
    for _ in range(count):
        scale = 2.0 ** (np.floor(np.log2(value)) - bits + 1)
        parts.append(float(np.floor(value / scale) * scale))
        value -= parts[-1]
    return parts


def program(nc, A, out):
    with ExitStack() as ctx:
        def sem(name):
            return ctx.enter_context(nc.semaphore(name))

        def sb(name, shape, dt=F32):
            return nc.alloc_sbuf_tensor(name, [P] + shape, dt)

        x = sb("x", [KT, T])
        h_hi, h_lo = sb("h_hi", [KT, T], F32R), sb("h_lo", [KT, T], F32R)
        raw = sb("raw", [4, HALF * P])
        w_hi, w_lo = sb("w_hi", [2, HALF * P], F32R), sb("w_lo", [2, HALF * P], F32R)
        consts = sb("consts", [len(CONSTS), P])
        gains = sb("gains", [7, KT])
        eps = sb("eps", [1])
        silu_g = sb("silu_g", [2, T])
        act_f = sb("act_f", [2, T])
        sq = sb("sq", [2, T])
        rstd = sb("rstd", [T])
        lnv = sb("lnv", [T])
        hf = sb("hf", [2, T])
        const = {name: consts[:, i, :] for i, name in enumerate(CONSTS)}

        region = nc.sbuf_base
        region_end = nc.sbuf_usable_end

        class Plan:
            def __init__(self):
                self.at = (region + 31) // 32 * 32

            def __call__(self, name, shape, dt=F32):
                t = nc.alloc_sbuf_tensor_at(name, [P] + shape, dt, offset=self.at)
                self.at += int(np.prod(shape)) * 4
                self.at = (self.at + 31) // 32 * 32
                assert self.at <= region_end, (name, self.at, region_end)
                return t

        io = Plan()
        x_rows = io("x_rows", [TT, D])
        ffn = Plan()
        a_hi, a_lo = ffn("a_hi", [FT, T], F32R), ffn("a_lo", [FT, T], F32R)

        ev = Plan()
        emix_hi, emix_lo = ev("emix_hi", [KT, T], F32R), ev("emix_lo", [KT, T], F32R)
        iq, qT, kT = ev("iq", [4, T]), ev("qT", [4, T]), ev("kT", [4, T])
        ik = ev("ik", [T])
        vtok = ev("vtok", [TT, 4, P])
        y_f = iq
        cosT, sinT = ev("cosT", [T]), ev("sinT", [T])
        roped_in = hf
        cbuf, ubuf = ev("cbuf", [T]), ev("ubuf", [T])
        score = ev("score", [TT, T])
        relu_s = ev("relu_s", [2, T])
        probs = silu_g
        probsT = act_f[:].rearrange("p b (t c) -> p b t c", t=TT)
        w_idx = ev("w_idx", [TT, HEADS])
        top8 = ev("top8", [8])
        amax, asum = ev("amax", [2]), ev("asum", [2])
        amax_n, arcp = ev("amax_n", [2]), ev("arcp", [2])
        ev_conv = ev("ev_conv", [4, 3])
        freq = ev("freq", [1])

        od = Plan()
        omix_hi, omix_lo = od("omix_hi", [KT, T], F32R), od("omix_lo", [KT, T], F32R)
        qc, kc, vc, zs = (od(n, [2, T]) for n in ("qc", "kc", "vc", "zs"))
        kn = od("kn", [TT, P])
        g_b, e_row = od("g_b", [TT, P]), od("e_row", [TT, P])
        dec_t, dec_a = od("dec_t", [TT, P]), od("dec_a", [TT, P])
        a_mat = od("a_mat", [TT, P])
        intra_t = od("intra_t", [TT, P])
        b_lvl = od("b_lvl", [2, TT, P])
        t_inv, u_inv, y_lvl = od("t_inv", [TT, P]), od("u_inv", [TT, P]), od("y_lvl", [TT, P])
        v_beta, k_beg, k_dec = od("v_beta", [TT, P]), od("k_beg", [TT, P]), od("k_dec", [TT, P])
        neg_w, q_dec = od("neg_w", [TT, P]), od("q_dec", [TT, P])
        state, v_new = od("state", [2, P]), od("v_new", [2, P])
        g_tok, g_cum = od("g_tok", [TT, HEADS]), od("g_cum", [TT, HEADS])
        beta, beg = od("beta", [TT, HEADS]), od("beg", [TT, HEADS])
        ba_tok = od("ba_tok", [TT, 2 * HEADS])
        gt1, gt2 = od("gt1", [TT, HEADS]), od("gt2", [TT, HEADS])
        alog, dtb = od("alog", [HEADS]), od("dtb", [HEADS])
        od_conv = od("od_conv", [3 * HEADS, 4])
        o_gain = od("o_gain", [1])

        fin = Plan()
        y_out = fin("y_out", [KT, T])
        y_rows = fin("y_rows", [2, D])

        prod = nc.alloc_psum_tensor("prod", [P, 4, T], F32)
        misc = nc.alloc_psum_tensor("misc", [P, 4, T], F32)

        def tiles(ap):
            return ap.rearrange("p (t c) -> p t c", t=TT)

        setup_in = sem("setup_in")
        raw_in = [sem(f"raw_in{i}") for i in range(4)]
        hi_ready, lo_ready, unit_done, evac = sem("hi_ready"), sem("lo_ready"), sem("unit_done"), sem("evac")
        x_turned, x_in = sem("x_turned"), sem("x_in")
        sq_ready, sum_done, ln_done, rstd_ready = sem("sq_ready"), sem("sum_done"), sem("ln_done"), sem("rstd_ready")
        hf_ready, hhi_ready, h_ready = sem("hf_ready"), sem("hhi_ready"), sem("h_ready")
        silu_done, ahi_ready, a_ready = sem("silu_done"), sem("ahi_ready"), sem("a_ready")
        act_seq, dve_seq, pool_seq = sem("act_seq"), sem("dve_seq"), sem("pool_seq")
        ev_in, od_in = sem("ev_in"), sem("od_in")
        ang_ready, trig_ready = sem("ang_ready"), sem("trig_ready")
        took, rot_done, cos_part, roped = sem("took"), sem("rot_done"), sem("cos_part"), sem("roped")
        idx_mm, relu_done, idx_added = sem("idx_mm"), sem("relu_done"), sem("idx_added")
        emhi, emix_ready = sem("emhi"), sem("emix_ready")
        logit_mm, masked, exp_done, probs_ready = sem("logit_mm"), sem("masked"), sem("exp_done"), sem("probs_ready")
        turned, probsT_ready, pv_done, y_taken = sem("turned"), sem("probsT_ready"), sem("pv_done"), sem("y_taken")
        act_done, state_mm = sem("act_done"), sem("state_mm")
        ba_taken, ba_turned, ba_tok_in, gate_exp = sem("ba_taken"), sem("ba_turned"), sem("ba_tok_in"), sem("gate_exp")
        g_ready, gcum_mm, g_cum_in, gate_in = sem("g_ready"), sem("gcum_mm"), sem("g_cum_in"), sem("gate_in")
        qk_sq, qk_sum, qk_rstd, qk_ready = sem("qk_sq"), sem("qk_sum"), sem("qk_rstd"), sem("qk_ready")
        gb_ready, grow_mm, dif_ready, dec_exp = sem("gb_ready"), sem("grow_mm"), sem("dif_ready"), sem("dec_exp")
        dec_ready, gram_mm, a_made = sem("dec_ready"), sem("gram_mm"), sem("a_made")
        b_made, b1_turned, tu_ready = sem("b_made"), sem("b1_turned"), sem("tu_ready")
        y_mm, y_ready, t_mm = sem("y_mm"), sem("y_ready"), sem("t_mm")
        w_mm, w_ready = sem("w_mm"), sem("w_ready")
        vnew_mm, vnew_ready, out_mm, state_ready = sem("vnew_mm"), sem("vnew_ready"), sem("out_mm"), sem("state_ready")
        o_sq, o_sum, o_rstd, o_f, ohi, omix_ready = (sem(n) for n in ("o_sq", "o_sum", "o_rstd", "o_f", "ohi", "omix_ready"))
        qdec_ready, e_row_ready = sem("qdec_ready"), sem("e_row_ready")
        y_turned, y_rows_in, stored = sem("y_turned"), sem("y_rows_in"), [sem("stored0"), sem("stored1")]
        SETUP = 4

        block = ctx.enter_context(nc.Block())
        extras = ev_extras()

        @block.sync
        def _(sp):
            def load(n, src, i=0):
                if n >= 4:
                    sp.wait_ge(lo_ready, n - 3 + 4 * i)
                sp.dma_start(raw[:, n % 4, 0:unit_width(n)], src).then_inc(raw_in[n % 4], 16)

            def ffn_loads(f):
                n0, row0 = FFN_AT[f][0], GU_ROW[f]
                for u in range(4):
                    load(n0 + u, A["w8"][row0 + u])
                with sp.Fori(1, 2 * FT // 4) as i:
                    for u in range(4):
                        row = i * 4 + (row0 + u)
                        sp.wait_ge(lo_ready, i * 4 + (n0 + u - 3))
                        sp.dma_start(raw[:, (n0 + u) % 4, 0:KT * P],
                                     A["w8"][bass.ds(row, 1)].rearrange("a p c -> (a p) c")).then_inc(raw_in[(n0 + u) % 4], 16)
                with sp.Fori(0, 2 * KT // 4) as i:
                    for u in range(4):
                        n = n0 + 2 * FT + u
                        row = i * 4 + (f * 2 * KT + u)
                        sp.wait_ge(lo_ready, i * 4 + (n - 3))
                        sp.dma_start(raw[:, n % 4, :],
                                     A["wd"][bass.ds(row, 1)].rearrange("a p c -> (a p) c")).then_inc(raw_in[n % 4], 16)

            sp.dma_start(x_rows[:], A["x"].rearrange("(t p) d -> p t d", p=P)).then_inc(setup_in, 16)
            sp.dma_start(consts[:], A["consts"]).then_inc(setup_in, 16)
            sp.dma_start(gains[:], A["gains"]).then_inc(setup_in, 16)
            sp.dma_start(eps[:], A["eps"]).then_inc(setup_in, 16)
            ffn_loads(0)
            for u in range(4):
                load(EV_N + u, A["w8"][EV0 + u])
            sp.wait_ge(evac, FFN_STEPS)
            sp.dma_start(ev_conv[:], A["ev_conv"]).then_inc(ev_in, 16)
            sp.dma_start(freq[:], A["freq"]).then_inc(ev_in, 16)
            sp.dma_start(cbuf[:].bitcast(I32), A["pos"].broadcast_to([P, T])).then_inc(ev_in, 16)
            for u in range(4, len(EV_UNITS) + KT):
                load(EV_N + u, A["w8"][EV0 + u])
            ffn_loads(1)
            ffn_loads(2)
            for u in range(4):
                load(OD_N + u, A["w8"][OD0 + u])
            sp.wait_ge(evac, OD_S)
            sp.dma_start(alog[:], A["alog"].broadcast_to([P, HEADS])).then_inc(od_in, 16)
            sp.dma_start(dtb[:], A["dtb"].broadcast_to([P, HEADS])).then_inc(od_in, 16)
            sp.dma_start(od_conv[:], A["od_conv"]).then_inc(od_in, 16)
            sp.dma_start(o_gain[:], A["o_gain"]).then_inc(od_in, 16)
            for u in range(4, len(OD_UNITS) + KT):
                load(OD_N + u, A["w8"][OD0 + u])
            ffn_loads(3)
            for t in range(TT):
                sp.wait_ge(y_rows_in, t + 1)
                sp.dma_start(out[t * P:(t + 1) * P, :], y_rows[:, t % 2, :]).then_inc(stored[t % 2], 16)
            sp.wait_ge(stored[0], 16 * TT // 2)
            sp.wait_ge(stored[1], 16 * TT // 2)

        @block.tensor
        def _(pe):
            def unit(n, bank, k0, acts, first, last, i=0, between=None, wait_k=None):
                pe.wait_ge(lo_ready, n + 1 + 4 * i)
                tiles_n = unit_width(n) // P
                for k in range(tiles_n):
                    if wait_k is not None:
                        wait_k(k)
                    hi, lo = acts(k0 + k)
                    wh = w_hi[:, n % 2, k * P:(k + 1) * P]
                    wl = w_lo[:, n % 2, k * P:(k + 1) * P]
                    pe.matmul(bank, wh, hi, start=first and k == 0, stop=False)
                    pe.matmul(bank, wh, lo, start=False, stop=False)
                    ins = pe.matmul(bank, wl, hi, start=False, stop=last and k == tiles_n - 1)
                    if k == tiles_n - 1:
                        ins.then_inc(unit_done, 1)
                    if between is not None:
                        between(k)

            def h_act(k):
                return h_hi[:, k, :], h_lo[:, k, :]

            def a_act(k):
                return a_hi[:, k, :], a_lo[:, k, :]

            def bank_free(s, i=0):
                if not isinstance(i, int):
                    pe.wait_ge(evac, i * 2 + (s - 1))
                elif s >= 2:
                    pe.wait_ge(evac, s - 1)

            def square_sum(r, m, c=None):
                pe.wait_ge(sq_ready, 8 * r + m + 1)
                pe.matmul(misc[:, 0, :], const["ones"], sq[:, m % 2, :], start=m == 0, stop=m == KT - 1)\
                    .then_inc(sum_done, 1)

            def ffn_pe(f):
                n0, s0 = FFN_AT[f]

                def h_wait(k):
                    pe.wait_ge(h_ready, 8 * norm_of(f) + k + 1)

                def pairs(i, first):
                    for u in range(4):
                        s = s0 + u // 2
                        if u % 2 == 0:
                            bank_free(s, i)
                        unit(n0 + u, prod[:, 2 * (s % 2) + u % 2, :], 0, h_act, True, True, i,
                             wait_k=h_wait if first and u == 0 else None)

                pairs(0, True)
                with pe.Fori(1, FT // 2) as i:
                    pairs(i, False)
                pe.wait_ge(a_ready, FT * (f + 1))
                for m in range(KT):
                    s = s0 + FT + m
                    bank_free(s)
                    for half in range(2):
                        unit(n0 + 2 * FT + 2 * m + half, prod[:, 2 * (s % 2), :], half * HALF, a_act,
                             half == 0, half == 1)
                    if m >= 1:
                        square_sum(norm_of(f) + 1, m - 1)
                square_sum(norm_of(f) + 1, KT - 1)

            def out_pe(n0, s0, r, acts, ready, total):
                pe.wait_ge(ready, total)
                for m in range(KT):
                    bank_free(s0 + m)
                    unit(n0 + m, prod[:, 2 * ((s0 + m) % 2), :], 0, acts, True, True)
                    if m >= 1:
                        square_sum(r, m - 1)
                square_sum(r, KT - 1)

            pe.wait_ge(setup_in, 16 * SETUP)
            for k in range(KT):
                if k >= 4:
                    pe.wait_ge(x_in, k - 3)
                for t in range(TT):
                    ins = pe.transpose(prod[:, k % 4, t * P:(t + 1) * P], x_rows[:, t, k * P:(k + 1) * P], const["ident"])
                ins.then_inc(x_turned, 1)
            for k in range(KT):
                square_sum(0, k)
            pe.wait_ge(x_in, KT)
            ffn_pe(0)

            def idx_pe(b, h):
                q = (b - 1) * HEADS + h
                if b == 1 and h == 0:
                    pe.wait_ge(roped, 5)
                if q >= 2:
                    pe.wait_ge(relu_done, q - 1)
                r = slice(HD * (h % 2), HD * (h % 2) + HD)
                w = (b + 1) * P
                pe.matmul(misc[:, 2 + q % 2, 0:w], iq[r, h // 2, b * P:(b + 1) * P], ik[r, 0:w],
                          start=True, stop=True).then_inc(idx_mm, 1)

            def ev_extra_pe(u):
                for kind, b, j in extras[u]:
                    if kind == "idx":
                        idx_pe(b, j)

            def ev_side_pe(u):
                kind, m = EV_UNITS[u]
                if kind == "ik":
                    pe.wait_ge(took, 1)
                    pe.matmul(misc[:, 0, :], const["dup"], roped_in[:, 0, :], start=True, stop=True)
                    pe.matmul(misc[:, 1, :], const["dup_rot"], roped_in[:, 0, :], start=True, stop=True)
                    for t in range(TT):
                        ins = pe.matmul(misc[:, 2, t * HEADS:(t + 1) * HEADS], roped_in[:, 0, t * P:(t + 1) * P],
                                        const["ident"][:, HD:HD + HEADS], start=True, stop=True)
                    ins.then_inc(rot_done, 1)
                elif kind in ROPED:
                    pe.wait_ge(took, u + 1)
                    pe.wait_ge(roped, u)
                    pe.matmul(misc[:, 0, :], const["rot"], roped_in[:, u % 2, :], start=True, stop=True)\
                        .then_inc(rot_done, 1)
                elif kind == "v":
                    pe.wait_ge(took, u + 1)
                    pe.wait_ge(roped, u)
                    for t in range(TT):
                        ins = pe.transpose(misc[:, 0, t * P:(t + 1) * P], roped_in[:, u % 2, t * P:(t + 1) * P],
                                           const["ident"])
                    ins.then_inc(rot_done, 1)

            pe.wait_ge(evac, EV_S)
            for u in range(len(EV_UNITS)):
                s = EV_S + u
                bank_free(s)
                unit(EV_N + u, prod[:, 2 * (s % 2), :], 0, h_act, True, True,
                     wait_k=(lambda k: pe.wait_ge(h_ready, 8 + k + 1)) if u == 0 else None)
                if u >= 1:
                    ev_side_pe(u - 1)
                    ev_extra_pe(u - 1)
            ev_extra_pe(len(EV_UNITS) - 1)

            def att(q):
                return q // HEADS, q % HEADS, slice(HD * (q % 2), HD * (q % 2) + HD)

            def att_logits(q):
                b, h, r = att(q)
                if q >= 2:
                    pe.wait_ge(masked, q - 1)
                w = (b + 1) * P
                pe.matmul(misc[:, q % 2, 0:w], qT[r, h // 2, b * P:(b + 1) * P], kT[r, h // 2, 0:w],
                          start=True, stop=True).then_inc(logit_mm, 1)

            def att_turn(q):
                b = q // HEADS
                pe.wait_ge(probs_ready, q + 1)
                if q >= 1:
                    pe.wait_ge(probsT_ready, q)
                for c in range(b + 1):
                    ins = pe.transpose(misc[:, 2, c * P:(c + 1) * P], probs[:, q % 2, c * P:(c + 1) * P], const["ident"])
                ins.then_inc(turned, 1)

            def att_pv(q):
                b, h, r = att(q)
                pe.wait_ge(probsT_ready, q + 1)
                if q >= 1:
                    pe.wait_ge(y_taken, q)
                for c in range(b + 1):
                    ins = pe.matmul(misc[r, 3, 0:P], vtok[:, c, h // 2, r.start:r.stop], probsT[:, q % 2, c, :],
                                    start=c == 0, stop=c == b)
                ins.then_inc(pv_done, 1)

            pe.wait_ge(evac, EVO_S)
            pe.wait_ge(roped, N_SIDE)
            pe.wait_ge(idx_added, HEADS * (TT - 1))
            Q = TT * HEADS
            for q in range(Q + 2):
                if q < Q:
                    att_logits(q)
                if 1 <= q <= Q:
                    att_turn(q - 1)
                if q >= 2:
                    att_pv(q - 2)
            out_pe(EVO_N, EVO_S, 2, lambda k: (emix_hi[:, k, :], emix_lo[:, k, :]), emix_ready, 5)
            ffn_pe(1)
            ffn_pe(2)

            def prep_pe(j):
                if j == 2:
                    pe.wait_ge(ba_taken, 1)
                    for t in range(TT):
                        ins = pe.matmul(misc[:, 0, t * 16:(t + 1) * 16], hf[:, 0, t * P:(t + 1) * P],
                                        const["ident"][:, 0:16], start=True, stop=True)
                    ins.then_inc(ba_turned, 1)
                if j == 12:
                    pe.wait_ge(g_ready, 1)
                    pe.matmul(misc[:, 1, 0:TT * HEADS], const["tri"], g_tok[:].rearrange("p t h -> p (t h)"),
                              start=True, stop=True).then_inc(gcum_mm, 1)

            def each(dst, lhs, rhs, start=True, stop=True):
                for t in range(TT):
                    ins = pe.matmul(dst[:, t, :], lhs[:, t, :], rhs[:, t, :], start=start, stop=stop)
                return ins

            M = [tiles(misc[:, i, :]) for i in range(4)]

            def stage_pe(g, name):
                tri4 = const["tri"]
                L = g * (LEVELS - 1)
                if name == "norm":
                    pe.wait_ge(qk_sq, g + 1)
                    if g >= 1:
                        pe.wait_ge(omix_ready, g)
                    pe.matmul(misc[:, 0, :], const["ones"], sq[:, 0, :], start=True, stop=True)
                    pe.matmul(misc[:, 1, :], const["ones"], sq[:, 1, :], start=True, stop=True).then_inc(qk_sum, 1)
                elif name == "decay":
                    pe.wait_ge(gb_ready, g + 1)
                    for t in range(TT):
                        ins = pe.matmul(M[2][:, t, :], g_b[:, t, :], tri4, start=True, stop=True)
                    ins.then_inc(grow_mm, 1)
                elif name == "gram":
                    pe.wait_ge(qk_ready, g + 1)
                    pe.wait_ge(dec_exp, g + 1)
                    each(M[0], kn, kn)
                    each(M[1], kn, tiles(qc[:, g % 2, :]))
                    for t in range(TT):
                        pe.transpose(M[2][:, t, :], kn[:, t, :], const["ident"])
                    for t in range(TT):
                        ins = pe.transpose(M[3][:, t, :], vc[:, g % 2, t * P:(t + 1) * P], const["ident"])
                    ins.then_inc(gram_mm, 1)
                elif name == "turn1":
                    pe.wait_ge(b_made, LEVELS * g + 1)
                    pe.wait_ge(a_made, 5 * (g + 1))
                    for t in range(TT):
                        ins = pe.transpose(M[0][:, t, :], b_lvl[:, 1, t, :], const["ident"])
                    ins.then_inc(b1_turned, 1)
                elif name[0] == "y":
                    l = int(name[1:])
                    pe.wait_ge(b_made, LEVELS * g + l)
                    pe.wait_ge(tu_ready, TU * g + 2 * (l - 1))
                    each(M[3], b_lvl[:, l % 2], u_inv).then_inc(y_mm, 1)
                elif name[0] == "t":
                    l = int(name[1:])
                    pe.wait_ge(y_ready, L + l - 1)
                    if l < LEVELS:
                        each(M[1], y_lvl, t_inv)
                    each(M[2], t_inv, y_lvl).then_inc(t_mm, 1)
                elif name == "w":
                    pe.wait_ge(tu_ready, TU * (g + 1))
                    each(M[0], k_beg, u_inv).then_inc(w_mm, 1)
                elif name[:3] == "new":
                    t = int(name[3:])
                    if t == 0:
                        pe.wait_ge(w_ready, g + 1)
                    else:
                        pe.wait_ge(state_ready, (TT - 1) * g + t)
                    ins = pe.matmul(M[1][:, t, :], u_inv[:, t, :], v_beta[:, t, :], start=True, stop=t == 0)
                    if t:
                        ins = pe.matmul(M[1][:, t, :], neg_w[:, t, :], state[:, t % 2, :], start=False, stop=True)
                    ins.then_inc(vnew_mm, 1)
                elif name[:3] == "out":
                    t = int(name[3:])
                    pe.wait_ge(vnew_ready, TT * g + t + 1)
                    if t == 0:
                        pe.wait_ge(qdec_ready, g + 1)
                    if t < TT - 1:
                        pe.matmul(M[3][:, t, :], k_dec[:, t, :], v_new[:, t % 2, :], start=True, stop=True)\
                            .then_inc(state_mm, 1)
                    if t:
                        pe.matmul(M[2][:, t, :], state[:, t % 2, :], q_dec[:, t, :], start=True, stop=False)
                    pe.matmul(M[2][:, t, :], v_new[:, t % 2, :], intra_t[:, t, :], start=t == 0, stop=True)\
                        .then_inc(out_mm, 1)
                elif name == "fin":
                    pe.wait_ge(o_sq, g + 1)
                    pe.matmul(misc[:, 0, :], const["ones"], sq[:, 0, :], start=True, stop=True).then_inc(o_sum, 1)

            for u in range(len(OD_UNITS)):
                s = OD_S + u
                bank_free(s)
                head, part = divmod(u - 1, 4)

                def between(k, head=head, part=part, u=u):
                    slot = part * KT + k
                    if u == 0:
                        return
                    if head == 0:
                        prep_pe(slot)
                    elif 0 <= slot - SHIFT < len(STAGES):
                        stage_pe(head - 1, STAGES[slot - SHIFT])

                unit(OD_N + u, prod[:, 2 * (s % 2), :], 0, h_act, True, True, between=between,
                     wait_k=(lambda k: pe.wait_ge(h_ready, 8 * 4 + k + 1)) if u == 0 else None)
            for name in STAGES:
                stage_pe(HEADS - 1, name)
            out_pe(ODO_N, ODO_S, 5, lambda k: (omix_hi[:, k, :], omix_lo[:, k, :]), omix_ready, HEADS)
            ffn_pe(3)

            for t in range(TT):
                if t == 0:
                    pe.wait_ge(hf_ready, 8 * 7)
                if t >= 2:
                    pe.wait_ge(y_rows_in, t - 1)
                for k in range(KT):
                    ins = pe.transpose(prod[:, 2 * (t % 2) + k // 4, (k % 4) * P:(k % 4 + 1) * P],
                                       y_out[:, k, t * P:(t + 1) * P], const["ident"])
                ins.then_inc(y_turned, 1)

        @block.scalar
        def _(act):
            seq = [0]

            def link(ins):
                seq[0] += 1
                ins.then_inc(act_seq, 1)
                act.wait_ge(act_seq, seq[0])

            def split(n, i=0):
                if n >= N_END:
                    return
                act.wait_ge(raw_in[n % 4], 16 * (n // 4 + 1) + 16 * i)
                if n >= 2:
                    act.wait_ge(unit_done, n - 1 + 4 * i)
                w = unit_width(n)
                act.activation(w_hi[:, n % 2, 0:w], raw[:, n % 4, 0:w], ACT.Copy).then_inc(hi_ready, 1)

            def square(r, m, src, ready, count):
                act.wait_ge(ready, count)
                if 8 * r + m >= 2:
                    act.wait_ge(sum_done, 8 * r + m - 1)
                act.activation(sq[:, m % 2, :], src, ACT.Square).then_inc(sq_ready, 1)

            def norm(r, split_h=True):
                act.wait_ge(sum_done, 8 * (r + 1))
                link(act.activation(lnv[:], misc[:, 0, :], ACT.Ln, bias=eps[:], scale=1.0 / D))
                act.activation(rstd[:], lnv[:], ACT.Exp, scale=-0.5).then_inc(rstd_ready, 1)
                if split_h:
                    for k in range(KT):
                        act.wait_ge(hf_ready, 8 * r + k + 1)
                        act.activation(h_hi[:, k, :], hf[:, k % 2, :], ACT.Copy).then_inc(hhi_ready, 1)

            def ffn_act(f):
                n0, s0 = FFN_AT[f]

                def pair(i, tail=False):
                    for u in range(4):
                        n, s = n0 + u, s0 + u // 2
                        if tail:
                            split(n0 + 2 * FT - 4 + u + 2)
                            j = FT - 2 + u // 2
                            sem_i, jj = FT // 2 - 1, j
                        else:
                            split(n + 2, i)
                            sem_i = i
                            jj = None
                        if u % 2 == 1:
                            act.wait_ge(unit_done, n + 4 * sem_i)
                            act.activation(silu_g[:, s % 2, :], prod[:, 2 * (s % 2), :], ACT.Silu)\
                                .then_inc(silu_done, 1)
                            act.wait_ge(evac, s + 1 + 2 * sem_i)
                            dst = a_hi[:, jj, :] if tail else \
                                a_hi[:, bass.ds(i * 2 + u // 2, 1), :].rearrange("p a c -> p (a c)")
                            act.activation(dst, act_f[:, s % 2, :], ACT.Copy).then_inc(ahi_ready, 1)

                with act.Fori(0, FT // 2 - 1) as i:
                    pair(i)
                pair(0, tail=True)
                for m in range(KT):
                    for half in range(2):
                        split(n0 + 2 * FT + 2 * m + half + 2)
                    square(norm_of(f) + 1, m, x[:, m, :], evac, s0 + FT + m + 1)

            act.wait_ge(setup_in, 16 * SETUP)
            split(0)
            split(1)
            for k in range(KT):
                square(0, k, x[:, k, :], x_in, k + 1)
            norm(0)
            ffn_act(0)

            norm(1)
            for i in range(2):
                act.wait_ge(ang_ready, i + 1)
                act.activation((sinT, cosT)[i][:], (sinT, cosT)[i][:], ACT.Sin).then_inc(trig_ready, 1)

            def ev_extra_act(u):
                for kind, b, j in extras[u]:
                    if kind == "idx":
                        q = (b - 1) * HEADS + j
                        act.wait_ge(idx_mm, q + 1)
                        if q >= 2:
                            act.wait_ge(idx_added, q - 1)
                        act.activation(relu_s[:, q % 2, 0:(b + 1) * P], misc[:, 2 + q % 2, 0:(b + 1) * P], ACT.Relu)\
                            .then_inc(relu_done, 1)

            for u in range(len(EV_UNITS)):
                kind, m = EV_UNITS[u]
                split(EV_N + u + 2)
                if kind in ("ik", "iq", "k", "q", "v"):
                    act.wait_ge(unit_done, EV_N + u + 1)
                    if u >= 2:
                        act.wait_ge(rot_done, u - 1)
                        act.wait_ge(roped, u - 1)
                    act.activation(roped_in[:, u % 2, :], prod[:, 2 * ((EV_S + u) % 2), :], ACT.Copy).then_inc(took, 1)
                if kind == "b":
                    act.wait_ge(evac, EV_S + u + 1)
                    act.activation(emix_hi[:, m, :], act_f[:, m % 2, :], ACT.Copy).then_inc(emhi, 1)
                if u >= 1:
                    ev_extra_act(u - 1)
            ev_extra_act(len(EV_UNITS) - 1)
            Q = TT * HEADS
            for q in range(Q + 1):
                if q < Q:
                    act.wait_ge(masked, q + 1)
                    if q >= 2:
                        act.wait_ge(turned, q - 1)
                    w = (q // HEADS + 1) * P
                    act.activation(probs[:, q % 2, 0:w], relu_s[:, q % 2, 0:w], ACT.Exp, bias=amax_n[:, q % 2:q % 2 + 1],
                                   accum_out=asum[:, q % 2:q % 2 + 1]).then_inc(exp_done, 1)
                if q >= 1:
                    c = (q - 1) // HEADS + 1
                    act.wait_ge(turned, q)
                    if q >= 3:
                        act.wait_ge(pv_done, q - 2)
                    act.activation(probsT[:, (q - 1) % 2, 0:c, :], tiles(misc[:, 2, :])[:, 0:c, :], ACT.Copy)\
                        .then_inc(probsT_ready, 1)
            act.wait_ge(y_taken, Q)
            act.activation(emix_hi[:, 4:8, :], y_f[:], ACT.Copy).then_inc(emhi, 1)
            for m in range(KT):
                split(EVO_N + m + 2)
                square(2, m, x[:, m, :], evac, EVO_S + m + 1)
            norm(2)
            ffn_act(1)
            norm(3)
            ffn_act(2)
            norm(4)

            def prep_act(j):
                if j == 4:
                    act.wait_ge(ba_tok_in, 1)
                    act.activation(beta[:], ba_tok[:, :, 0:HEADS], ACT.Exp, scale=-1.0).then_inc(gate_exp, 1)
                    act.wait_ge(ba_tok_in, 2)
                    link(act.activation(gt1[:], gt1[:], ACT.Exp, scale=-1.0))
                    link(act.activation(gt1[:], gt1[:], ACT.Ln, bias=1.0))
                    act.activation(alog[:], alog[:], ACT.Exp).then_inc(gate_exp, 1)
                if j == 14:
                    act.wait_ge(g_cum_in, 1)
                    act.activation(beg[:], g_cum[:], ACT.Exp).then_inc(gate_exp, 1)

            M = [tiles(misc[:, i, :]) for i in range(4)]

            def stage_act(g, name):
                L = g * (LEVELS - 1)
                if name == "norm":
                    act.wait_ge(act_done, 4 * (g + 1))
                    if g >= 1:
                        act.wait_ge(omix_ready, g)
                    act.activation(sq[:, 0, :], qc[:, g % 2, :], ACT.Square)
                    act.activation(sq[:, 1, :], kc[:, g % 2, :], ACT.Square).then_inc(qk_sq, 1)
                    act.wait_ge(qk_sum, g + 1)
                    act.activation(silu_g[:, 0, :], misc[:, 0, :], ACT.Ln, bias=eps[:])
                    link(act.activation(silu_g[:, 1, :], misc[:, 1, :], ACT.Ln, bias=eps[:]))
                    act.activation(silu_g[:, 0, :], silu_g[:, 0, :], ACT.Exp, scale=-0.5)
                    act.activation(silu_g[:, 1, :], silu_g[:, 1, :], ACT.Exp, scale=-0.5).then_inc(qk_rstd, 1)
                elif name == "decay":
                    act.wait_ge(grow_mm, g + 1)
                    act.activation(e_row[:], M[2], ACT.Exp).then_inc(e_row_ready, 1)
                    act.wait_ge(dif_ready, g + 1)
                    act.activation(dec_t[:], dec_t[:], ACT.Exp)
                    act.activation(dec_a[:], dec_a[:], ACT.Exp, scale=-1.0).then_inc(dec_exp, 1)
                elif name[0] == "y":
                    l = int(name[1:])
                    act.wait_ge(y_mm, L + l - 1)
                    act.activation(y_lvl[:], M[3], ACT.Copy).then_inc(y_ready, 1)
                elif name == "w":
                    act.wait_ge(w_mm, g + 1)
                    act.activation(neg_w[:], M[0], ACT.Copy, scale=-1.0).then_inc(w_ready, 1)
                elif name == "fin":
                    act.wait_ge(out_mm, TT * (g + 1))
                    act.activation(sq[:, 0, :], misc[:, 2, :], ACT.Square).then_inc(o_sq, 1)
                    act.wait_ge(o_sum, g + 1)
                    link(act.activation(lnv[:], misc[:, 0, :], ACT.Ln, bias=eps[:], scale=1.0 / P))
                    act.activation(rstd[:], lnv[:], ACT.Exp, scale=-0.5).then_inc(o_rstd, 1)
                    act.wait_ge(o_f, g + 1)
                    act.activation(omix_hi[:, g, :], act_f[:, 0, :], ACT.Copy).then_inc(ohi, 1)

            for u in range(len(OD_UNITS)):
                head, part = divmod(u - 1, 4)
                if u >= 1:
                    for k in range(KT):
                        slot = part * KT + k
                        if head == 0:
                            prep_act(slot)
                        elif 0 <= slot - SHIFT < len(STAGES):
                            stage_act(head - 1, STAGES[slot - SHIFT])
                split(OD_N + u + 2)
                if u == 0:
                    act.wait_ge(unit_done, OD_N + 1)
                    act.activation(hf[:, 0, :], prod[:, 2 * (OD_S % 2), :], ACT.Copy).then_inc(ba_taken, 1)
                else:
                    kind, h = OD_UNITS[u]
                    dst = {"q": qc, "k": kc, "v": vc, "z": zs}[kind][:, h % 2, :]
                    act.wait_ge(evac, OD_S + u + 1)
                    act.activation(dst, dst, ACT.Silu).then_inc(act_done, 1)
            for name in STAGES:
                stage_act(HEADS - 1, name)
            for m in range(KT):
                split(ODO_N + m + 2)
                square(5, m, x[:, m, :], evac, ODO_S + m + 1)
            norm(5)
            ffn_act(3)
            norm(6, split_h=False)
            for t in range(TT):
                act.wait_ge(y_turned, t + 1)
                if t >= 2:
                    act.wait_ge(stored[t % 2], 16 * (t // 2))
                act.activation(y_rows[:, t % 2, :].rearrange("p (a c) -> p a c", a=2),
                               prod[:, 2 * (t % 2):2 * (t % 2) + 2, :], ACT.Copy).then_inc(y_rows_in, 1)

        @block.vector
        def _(dve):
            seq = [0]

            def link(ins):
                seq[0] += 1
                ins.then_inc(dve_seq, 1)
                dve.wait_ge(dve_seq, seq[0])

            def split(n, i=0):
                if n >= N_END:
                    return
                w = unit_width(n)
                dve.wait_ge(hi_ready, n + 1 + 4 * i)
                dve.tensor_tensor(w_lo[:, n % 2, 0:w], raw[:, n % 4, 0:w], w_hi[:, n % 2, 0:w].bitcast(F32),
                                  ALU.subtract).then_inc(lo_ready, 1)

            def norm(r, dst=None):
                dve.wait_ge(rstd_ready, r + 1)

                def lo(k):
                    dve.wait_ge(hhi_ready, 8 * r + k + 1)
                    dve.tensor_tensor(h_lo[:, k, :], hf[:, k % 2, :], h_hi[:, k, :].bitcast(F32), ALU.subtract)\
                        .then_inc(h_ready, 1)

                for k in range(KT):
                    to = hf[:, k % 2, :] if dst is None else dst[:, k, :]
                    if dst is None and k >= 2:
                        dve.wait_ge(h_ready, 8 * r + k - 1)
                    dve.scalar_tensor_tensor(to, x[:, k, :], gains[:, r, k:k + 1], rstd[:], ALU.mult, ALU.mult)\
                        .then_inc(hf_ready, 1)
                    if dst is None and k >= 1:
                        lo(k - 1)
                if dst is None:
                    lo(KT - 1)

            def residual(m, s, n_units, scale):
                dve.wait_ge(unit_done, n_units)
                dve.scalar_tensor_tensor(x[:, m, :], prod[:, 2 * (s % 2), :], scale, x[:, m, :], ALU.mult, ALU.add)\
                    .then_inc(evac, 1)

            def ffn_dve(f):
                n0, s0 = FFN_AT[f]

                def pair(i, tail=False):
                    for u in range(4):
                        n, s = n0 + u, s0 + u // 2
                        sem_i = FT // 2 - 1 if tail else i
                        if tail:
                            split(n0 + 2 * FT - 4 + u + 2)
                        else:
                            split(n + 2, i)
                        if u % 2 == 1:
                            j = FT * f + u // 2
                            dve.wait_ge(silu_done, j + 1 + 2 * sem_i)
                            dve.wait_ge(unit_done, n + 1 + 4 * sem_i)
                            dve.tensor_tensor(act_f[:, s % 2, :], silu_g[:, s % 2, :], prod[:, 2 * (s % 2) + 1, :],
                                              ALU.mult).then_inc(evac, 1)
                            dve.wait_ge(ahi_ready, j + 1 + 2 * sem_i)
                            if tail:
                                hi, dst = a_hi[:, FT - 2 + u // 2, :], a_lo[:, FT - 2 + u // 2, :]
                            else:
                                hi, dst = (t[:, bass.ds(i * 2 + u // 2, 1), :].rearrange("p a c -> p (a c)")
                                           for t in (a_hi, a_lo))
                            dve.tensor_tensor(dst, act_f[:, s % 2, :], hi.bitcast(F32), ALU.subtract)\
                                .then_inc(a_ready, 1)
                            dve.wait_ge(a_ready, j + 1 + 2 * sem_i)

                with dve.Fori(0, FT // 2 - 1) as i:
                    pair(i)
                pair(0, tail=True)
                for m in range(KT):
                    for half in range(2):
                        split(n0 + 2 * FT + 2 * m + half + 2)
                    residual(m, s0 + FT + m, n0 + 2 * FT + 2 * m + 2, 0.5)

            split(0)
            split(1)
            for k in range(KT):
                dve.wait_ge(x_turned, k + 1)
                dve.tensor_copy(x[:, k, :], prod[:, k % 4, :]).then_inc(x_in, 1)
            norm(0)
            ffn_dve(0)

            norm(1)
            dve.wait_ge(ev_in, 16 * 3)
            link(dve.tensor_copy(ubuf[:], cbuf[:].bitcast(I32)))
            link(dve.tensor_scalar(ubuf[:], ubuf[:], freq[:], None, ALU.mult))
            magic = 1.5 * 2.0 ** 23
            for unit_2pi, parts in ((4096.0, 7), (1.0, 6)):
                link(dve.tensor_scalar(cbuf[:], ubuf[:], float(1.0 / (2 * np.pi * unit_2pi)), magic, ALU.mult, ALU.add))
                link(dve.tensor_scalar(cbuf[:], cbuf[:], magic, None, ALU.subtract))
                for part in pi_parts(2 * np.pi * unit_2pi, parts):
                    link(dve.scalar_tensor_tensor(ubuf[:], cbuf[:], -part, ubuf[:], ALU.mult, ALU.add))
            link(dve.tensor_scalar(ubuf[:], ubuf[:], 3.141592, -3.141592, ALU.min, ALU.max))
            dve.tensor_copy(sinT[:], ubuf[:]).then_inc(ang_ready, 1)
            link(dve.scalar_tensor_tensor(cosT[:], ubuf[:], -1.0, ubuf[:], ALU.mult, ALU.max))
            dve.tensor_scalar(cosT[:], cosT[:], -1.0, float(np.float32(np.pi / 2)), ALU.mult, ALU.add)\
                .then_inc(ang_ready, 1)

            def ev_extra_dve(u):
                for kind, b, j in extras[u]:
                    w = (b + 1) * P
                    if kind == "idx":
                        q = (b - 1) * HEADS + j
                        dve.wait_ge(relu_done, q + 1)
                        wcol = w_idx[:, b, j:j + 1]
                        if j == 0:
                            ins = dve.tensor_scalar(score[:, b, 0:w], relu_s[:, q % 2, 0:w], wcol, None, ALU.mult)
                        else:
                            ins = dve.scalar_tensor_tensor(score[:, b, 0:w], relu_s[:, q % 2, 0:w], wcol,
                                                           score[:, b, 0:w], ALU.mult, ALU.add)
                        ins.then_inc(idx_added, 1)
                        dve.wait_ge(idx_added, q + 1)
                        if j == HEADS - 1:
                            link(dve.tensor_tensor(score[:, b, b * P:w], score[:, b, b * P:w], const["neg_future"],
                                                   ALU.add))
                    else:
                        link(dve.max(top8[:], score[:, b, 0:w]))
                        link(dve.match_replace(score[:, b, 0:w], top8[:], score[:, b, 0:w], MARK))

            def ev_side_dve(u):
                kind, m = EV_UNITS[u]
                if kind == "ik":
                    dve.wait_ge(rot_done, 1)
                    dve.wait_ge(trig_ready, 2)
                    dve.tensor_scalar(w_idx[:].rearrange("p t h -> p (t h)"), misc[:, 2, 0:TT * HEADS],
                                      float((HEADS * HD) ** -0.5), None, ALU.mult)
                    dve.tensor_tensor(ubuf[:], misc[:, 1, :], sinT[:], ALU.mult)
                    link(dve.tensor_tensor(ik[:], misc[:, 0, :], cosT[:], ALU.mult))
                    dve.tensor_tensor(ik[:], ik[:], ubuf[:], ALU.add).then_inc(roped, 1)
                elif kind in ROPED:
                    dst = {"iq": iq, "q": qT, "k": kT}[kind][:, m, :]
                    dve.wait_ge(rot_done, u + 1)
                    link(dve.tensor_tensor(ubuf[:], misc[:, 0, :], sinT[:], ALU.mult))
                    dve.wait_ge(cos_part, u)
                    dve.tensor_tensor(dst, dst, ubuf[:], ALU.add).then_inc(roped, 1)
                elif kind == "v":
                    dve.wait_ge(rot_done, u + 1)
                    dve.tensor_copy(vtok[:, :, m, :], tiles(misc[:, 0, :])).then_inc(roped, 1)

            for u in range(len(EV_UNITS)):
                kind, m = EV_UNITS[u]
                n, s = EV_N + u, EV_S + u
                bank = prod[:, 2 * (s % 2), :]
                split(n + 2)
                dve.wait_ge(unit_done, n + 1)
                if kind in ("ik", "iq", "k", "q", "v"):
                    dve.wait_ge(took, u + 1)
                    dve.sem_inc(evac, 1)
                elif kind == "c":
                    dve.tensor_copy(cbuf[:], bank).then_inc(evac, 1)
                elif kind == "x":
                    dve.wait_ge(evac, s)
                    dve.tensor_tensor(ubuf[:], cbuf[:], bank, ALU.mult).then_inc(evac, 1)
                    dve.wait_ge(evac, s + 1)
                    link(dve.tensor_scalar(cbuf[:], ubuf[:], ev_conv[:, m, 2:3], None, ALU.mult))
                    for j in (1, 2):
                        link(dve.scalar_tensor_tensor(cbuf[:, j:T], ubuf[:, 0:T - j], ev_conv[:, m, 2 - j:3 - j],
                                                      cbuf[:, j:T], ALU.mult, ALU.add))
                else:
                    dve.tensor_tensor(act_f[:, m % 2, :], cbuf[:], bank, ALU.mult).then_inc(evac, 1)
                    dve.wait_ge(evac, s + 1)
                    dve.wait_ge(emhi, m + 1)
                    dve.tensor_tensor(emix_lo[:, m, :], act_f[:, m % 2, :], emix_hi[:, m, :].bitcast(F32), ALU.subtract)\
                        .then_inc(emix_ready, 1)
                if u >= 1:
                    ev_side_dve(u - 1)
                    ev_extra_dve(u - 1)
            ev_extra_dve(len(EV_UNITS) - 1)
            for kind, b, j in extras["rest"]:
                w = (b + 1) * P
                link(dve.max(top8[:], score[:, b, 0:w]))
                link(dve.match_replace(score[:, b, 0:w], top8[:], score[:, b, 0:w], MARK))
            link(dve.tensor_copy(score[:, 0, 0:P], const["neg_future"]))
            for b in range(1, TT):
                w = (b + 1) * P
                link(dve.tensor_scalar(score[:, b, 0:w], score[:, b, 0:w], SPLIT, NEG, ALU.is_gt, ALU.mult))

            Q = TT * HEADS
            for q in range(Q + 2):
                if q < Q:
                    b, i = q // HEADS, q % 2
                    w = (b + 1) * P
                    dve.wait_ge(logit_mm, q + 1)
                    if q >= 2:
                        dve.wait_ge(exp_done, q - 1)
                    link(dve.tensor_tensor_reduce(relu_s[:, i, 0:w], misc[:, i, 0:w], score[:, b, 0:w], HD ** -0.5,
                                                  NEG, ALU.add, ALU.max, amax[:, i:i + 1]))
                    dve.tensor_scalar(amax_n[:, i:i + 1], amax[:, i:i + 1], -1.0, None, ALU.mult).then_inc(masked, 1)
                if 1 <= q <= Q:
                    i, w = (q - 1) % 2, ((q - 1) // HEADS + 1) * P
                    dve.wait_ge(exp_done, q)
                    link(dve.reciprocal(arcp[:, i:i + 1], asum[:, i:i + 1]))
                    dve.tensor_scalar(probs[:, i, 0:w], probs[:, i, 0:w], arcp[:, i:i + 1], None, ALU.mult)\
                        .then_inc(probs_ready, 1)
                if q >= 2:
                    b, h = (q - 2) // HEADS, (q - 2) % HEADS
                    r = slice(HD * (h % 2), HD * (h % 2) + HD)
                    dve.wait_ge(pv_done, q - 1)
                    dve.tensor_copy(y_f[r, h // 2, b * P:(b + 1) * P], misc[r, 3, 0:P]).then_inc(y_taken, 1)
            dve.wait_ge(emhi, 5)
            dve.tensor_tensor(emix_lo[:, 4:8, :], y_f[:], emix_hi[:, 4:8, :].bitcast(F32), ALU.subtract)\
                .then_inc(emix_ready, 1)
            for m in range(KT):
                split(EVO_N + m + 2)
                residual(m, EVO_S + m, EVO_N + m + 1, 1.0)
            norm(2)
            ffn_dve(1)
            norm(3)
            ffn_dve(2)
            norm(4)

            def bc(ap):
                return ap.unsqueeze(1).broadcast_to([P, TT, HEADS])

            def prep_dve(j):
                if j == 4:
                    dve.wait_ge(ba_turned, 1)
                    dve.wait_ge(od_in, 16 * 4)
                    dve.tensor_copy(ba_tok[:], misc[:, 0, 0:TT * 16].rearrange("p (t c) -> p t c", t=TT))\
                        .then_inc(ba_tok_in, 1)
                    dve.wait_ge(ba_tok_in, 1)
                    link(dve.tensor_tensor(gt2[:], ba_tok[:, :, HEADS:2 * HEADS], bc(dtb[:]), ALU.add))
                    dve.scalar_tensor_tensor(gt1[:], gt2[:], -1.0, gt2[:], ALU.mult, ALU.max).then_inc(ba_tok_in, 1)
                    dve.wait_ge(ba_tok_in, 2)
                    link(dve.tensor_scalar(gt2[:], gt2[:], 0.0, None, ALU.max))
                    dve.wait_ge(gate_exp, 1)
                    link(dve.tensor_scalar(beta[:], beta[:], 1.0, None, ALU.add))
                    link(dve.reciprocal(beta[:], beta[:]))
                    dve.wait_ge(gate_exp, 2)
                    link(dve.tensor_tensor(gt2[:], gt2[:], gt1[:], ALU.add))
                    dve.scalar_tensor_tensor(g_tok[:], gt2[:], -1.0, bc(alog[:]), ALU.mult, ALU.mult)\
                        .then_inc(g_ready, 1)
                if j == 14:
                    dve.wait_ge(gcum_mm, 1)
                    dve.tensor_copy(g_cum[:].rearrange("p t h -> p (t h)"), misc[:, 1, 0:TT * HEADS])\
                        .then_inc(g_cum_in, 1)
                    dve.wait_ge(gate_exp, 3)
                    link(dve.tensor_tensor(beg[:], beg[:], beta[:], ALU.mult))

            M = [tiles(misc[:, i, :]) for i in range(4)]

            def col(t, g):
                return t[:, :, g:g + 1].broadcast_to([P, TT, P])

            def same(m):
                return m.unsqueeze(1).broadcast_to([P, TT, P])

            def stage_dve(g, name):
                if name == "norm":
                    if g >= 1:
                        dve.wait_ge(out_mm, TT * g)
                    dve.tensor_copy(g_b[:], col(g_tok, g)).then_inc(gb_ready, 1)
                    dve.wait_ge(qk_rstd, g + 1)
                    dve.scalar_tensor_tensor(qc[:, g % 2, :], qc[:, g % 2, :], float(P ** -0.5), silu_g[:, 0, :],
                                             ALU.mult, ALU.mult)
                    dve.tensor_tensor(kn[:].rearrange("p t c -> p (t c)"), kc[:, g % 2, :], silu_g[:, 1, :], ALU.mult)\
                        .then_inc(qk_ready, 1)
                elif name == "decay":
                    dve.wait_ge(grow_mm, g + 1)
                    dve.wait_ge(e_row_ready, g + 1)
                    link(dve.tensor_tensor(a_mat[:], M[2], col(g_cum, g), ALU.subtract))
                    dve.tensor_scalar(dec_t[:], a_mat[:], 0.0, None, ALU.min)
                    dve.tensor_scalar(dec_a[:], a_mat[:], 0.0, None, ALU.max).then_inc(dif_ready, 1)
                elif name == "gram":
                    dve.wait_ge(gram_mm, g + 1)
                    dve.wait_ge(dec_ready, g + 1)
                    dve.tensor_tensor(a_mat[:], M[0], dec_a[:], ALU.mult).then_inc(a_made, 1)
                    dve.tensor_tensor(intra_t[:], M[1], dec_t[:], ALU.mult).then_inc(a_made, 1)
                    dve.tensor_tensor(v_beta[:], M[3], col(beta, g), ALU.mult).then_inc(a_made, 1)
                    dve.tensor_tensor(k_beg[:], M[2], col(beg, g), ALU.mult).then_inc(a_made, 1)
                    dve.tensor_tensor(k_dec[:], M[2], dec_t[:, :, P - 1:P].broadcast_to([P, TT, P]), ALU.mult)\
                        .then_inc(a_made, 1)
                elif name == "turn1":
                    dve.wait_ge(b_made, LEVELS * g + 1)
                    dve.tensor_tensor(t_inv[:], same(const["ident"]), b_lvl[:, 1], ALU.subtract).then_inc(tu_ready, 1)
                    dve.wait_ge(b1_turned, g + 1)
                    dve.tensor_tensor(u_inv[:], same(const["ident"]), M[0], ALU.subtract).then_inc(tu_ready, 1)
                elif name[0] == "t":
                    l = int(name[1:])
                    dve.wait_ge(t_mm, (LEVELS - 1) * g + l - 1)
                    if l < LEVELS:
                        dve.tensor_tensor(t_inv[:], t_inv[:], M[1], ALU.subtract).then_inc(tu_ready, 1)
                    dve.tensor_tensor(u_inv[:], u_inv[:], M[2], ALU.subtract).then_inc(tu_ready, 1)
                elif name[:3] == "new":
                    t = int(name[3:])
                    dve.wait_ge(vnew_mm, TT * g + t + 1)
                    dve.tensor_copy(v_new[:, t % 2, :], M[1][:, t, :]).then_inc(vnew_ready, 1)
                elif name[:3] == "out" and name != f"out{TT - 1}":
                    t = int(name[3:])
                    dve.wait_ge(state_mm, (TT - 1) * g + t + 1)
                    if t == 0:
                        dve.tensor_copy(state[:, 1, :], M[3][:, t, :]).then_inc(state_ready, 1)
                    else:
                        dve.wait_ge(state_ready, (TT - 1) * g + t)
                        dve.scalar_tensor_tensor(state[:, (t + 1) % 2, :], state[:, t % 2, :], e_row[:, t, P - 1:P],
                                                 M[3][:, t, :], ALU.mult, ALU.add).then_inc(state_ready, 1)
                elif name == "fin":
                    dve.wait_ge(o_rstd, g + 1)
                    link(dve.scalar_tensor_tensor(act_f[:, 0, :], misc[:, 2, :], o_gain[:], rstd[:], ALU.mult, ALU.mult))
                    dve.tensor_tensor(act_f[:, 0, :], act_f[:, 0, :], zs[:, g % 2, :], ALU.mult).then_inc(o_f, 1)
                    dve.wait_ge(ohi, g + 1)
                    dve.tensor_tensor(omix_lo[:, g, :], act_f[:, 0, :], omix_hi[:, g, :].bitcast(F32), ALU.subtract)\
                        .then_inc(omix_ready, 1)

            for u in range(len(OD_UNITS)):
                n, s = OD_N + u, OD_S + u
                bank = prod[:, 2 * (s % 2), :]
                head, part = divmod(u - 1, 4)
                if u >= 1:
                    for k in range(KT):
                        slot = part * KT + k
                        if head == 0:
                            prep_dve(slot)
                        elif 0 <= slot - SHIFT < len(STAGES):
                            stage_dve(head - 1, STAGES[slot - SHIFT])
                split(n + 2)
                dve.wait_ge(unit_done, n + 1)
                if u == 0:
                    dve.wait_ge(ba_taken, 1)
                    dve.sem_inc(evac, 1)
                    dve.wait_ge(od_in, 16 * 4)
                    continue
                kind, h = OD_UNITS[u]
                dst = {"q": qc, "k": kc, "v": vc, "z": zs}[kind][:, h % 2, :]
                if kind == "z":
                    dve.tensor_copy(dst, bank).then_inc(evac, 1)
                else:
                    c = "qkv".index(kind) * HEADS + h
                    link(dve.tensor_scalar(dst, bank, od_conv[:, c, 3:4], None, ALU.mult))
                    for j in (1, 2, 3):
                        ins = dve.scalar_tensor_tensor(dst[:, j:T], bank[:, 0:T - j], od_conv[:, c, 3 - j:4 - j],
                                                       dst[:, j:T], ALU.mult, ALU.add)
                        if j < 3:
                            link(ins)
                    ins.then_inc(evac, 1)
            for name in STAGES:
                stage_dve(HEADS - 1, name)
            for m in range(KT):
                split(ODO_N + m + 2)
                residual(m, ODO_S + m, ODO_N + m + 1, 1.0)
            norm(5)
            ffn_dve(3)
            norm(6, dst=y_out)

        @block.gpsimd
        def _(pool):
            def same(m):
                return m.unsqueeze(1).broadcast_to([P, TT, P])

            pool.wait_ge(trig_ready, 2)
            for u, (kind, m) in enumerate(EV_UNITS):
                if kind in ROPED:
                    dst = {"iq": iq, "q": qT, "k": kT}[kind][:, m, :]
                    pool.wait_ge(took, u + 1)
                    pool.tensor_tensor(dst, roped_in[:, u % 2, :], cosT[:], ALU.mult).then_inc(cos_part, 1)
            for g in range(HEADS):
                pool.wait_ge(dec_exp, g + 1)
                pool.tensor_tensor(dec_t[:], dec_t[:], same(const["tri"]), ALU.mult)
                pool.tensor_tensor(dec_a[:], dec_a[:], beta[:, :, g:g + 1].broadcast_to([P, TT, P]), ALU.mult)\
                    .then_inc(dec_ready, 1)
                pool.wait_ge(qk_ready, g + 1)
                for l in range(1, LEVELS + 1):
                    if l == 1:
                        pool.wait_ge(a_made, 5 * g + 1)
                    if l >= 3:
                        if l == 3:
                            pool.wait_ge(tu_ready, TU * g + 2)
                        else:
                            pool.wait_ge(y_mm, (LEVELS - 1) * g + l - 3)
                    pool.tensor_tensor(b_lvl[:, l % 2], a_mat[:], same(const[f"level{l}"]), ALU.mult).then_inc(b_made, 1)
                    if l == 1:
                        pool.tensor_tensor(q_dec[:].rearrange("p t c -> p (t c)"), qc[:, g % 2, :],
                                           e_row[:].rearrange("p t c -> p (t c)"), ALU.mult).then_inc(qdec_ready, 1)


def shape_constants():
    i, j = np.indices((P, P))
    rot = np.zeros((P, P), np.float32)
    half = HD // 8
    for m in range(P):
        if m % HD < half:
            rot[m + half, m] = -1.0
        elif m % HD < 2 * half:
            rot[m - half, m] = 1.0
    c = {
        "ident": i == j, "ones": np.ones((P, P)), "tri": i <= j, "neg_future": np.where(j > i, NEG, 0.0),
        "rot": rot, "dup": (i == j % HD) & (i < HD),
        "dup_rot": np.where(i < HD, np.tile(rot[:, :HD], (1, 2)), 0.0),
    }
    for l in range(1, LEVELS + 1):
        s = 2 ** (l - 1)
        c[f"level{l}"] = (i // (2 * s) == j // (2 * s)) & (i // s % 2 == 1) & (j // s % 2 == 0)
    return np.ascontiguousarray(np.stack([np.asarray(c[n], np.float32) for n in CONSTS], axis=1))


def rope_frequencies():
    f = np.float32(500000.0) ** (-np.arange(0, HD // 4, 2, dtype=np.float32) / np.float32(HD // 4))
    row = np.arange(P) % HD
    return np.where(row < HD // 4, f[row % (HD // 8)], 0.0).astype(np.float32)[:, None]


def kernel(x, positions, norm_gain, ffn_w_gate, ffn_w_up, ffn_w_down, ev_w_in, ev_conv_w, ev_w_out,
           od_w_in, od_conv_w, od_a_log, od_dt_bias, od_o_gain, od_w_out, final_gain):
    import concourse.bacc as bacc
    from concourse.bass_utils import run_bass_kernel_spmd

    (x, positions, norm_gain, ffn_w_gate, ffn_w_up, ffn_w_down, ev_w_in, ev_conv_w, ev_w_out, od_w_in, od_conv_w,
     od_a_log, od_dt_bias, od_o_gain, od_w_out, final_gain) = (np.asarray(a) for a in (
         x, positions, norm_gain, ffn_w_gate, ffn_w_up, ffn_w_down, ev_w_in, ev_conv_w, ev_w_out, od_w_in, od_conv_w,
         od_a_log, od_dt_bias, od_o_gain, od_w_out, final_gain))

    def unit(w, cols):
        u = np.zeros((w.shape[0] // P, P, P), w.dtype)
        at = 0
        for lo, n in cols:
            u[:, :, at:at + n] = w[:, lo:lo + n].reshape(-1, P, n)
            at += n
        return u.transpose(1, 0, 2).reshape(P, -1)

    w8 = np.empty((ROWS8, P, KT * P), x.dtype)
    wd = np.empty((NFFN * 2 * KT, P, HALF * P), x.dtype)
    for f in range(NFFN):
        gate, up, down = (w[f // 2, f % 2] for w in (ffn_w_gate, ffn_w_up, ffn_w_down))
        for j in range(FT):
            w8[GU_ROW[f] + 2 * j] = unit(gate, [(j * P, P)])
            w8[GU_ROW[f] + 2 * j + 1] = unit(up, [(j * P, P)])
        for m in range(KT):
            for half in range(2):
                wd[f * 2 * KT + 2 * m + half] = unit(down[half * HALF * P:(half + 1) * HALF * P], [(m * P, P)])
    at = {"b": 0, "c": T, "x": 2 * T, "q": 3 * T, "k": 4 * T, "v": 5 * T, "iq": 6 * T}
    for u, (kind, m) in enumerate(EV_UNITS):
        w8[EV0 + u] = unit(ev_w_in[0], [(7 * T, HD + HEADS)] if kind == "ik" else [(at[kind] + m * P, P)])
    at = {"q": 0, "k": D, "v": 2 * D, "z": 3 * D}
    for u, (kind, h) in enumerate(OD_UNITS):
        w8[OD0 + u] = unit(od_w_in[0], [(4 * D, 2 * HEADS)] if kind == "ba" else [(at[kind] + h * P, P)])
    for m in range(KT):
        w8[EVO0 + m] = unit(ev_w_out[0], [(m * P, P)])
        w8[ODO0 + m] = unit(od_w_out[0], [(m * P, P)])
    gains = np.concatenate([norm_gain.reshape(6, KT, P), final_gain.reshape(1, KT, P)]).transpose(2, 0, 1)

    inputs = {
        "x": x.reshape(T, D), "pos": positions.reshape(1, T), "w8": w8, "wd": wd, "gains": gains,
        "consts": shape_constants(), "eps": np.full((P, 1), EPS, np.float32), "freq": rope_frequencies(),
        "ev_conv": ev_conv_w[0].reshape(3, 4, P).transpose(2, 1, 0),
        "od_conv": od_conv_w[0].reshape(4, 3 * HEADS, P).transpose(2, 1, 0),
        "alog": od_a_log.reshape(1, HEADS), "dtb": od_dt_bias.reshape(1, HEADS), "o_gain": od_o_gain.reshape(P, 1),
    }
    nc = bacc.Bacc("TRN2", target_bir_lowering=False, num_devices=1)
    arrays, aps = {}, {}
    for name, a in inputs.items():
        arrays[f"in_{name}"] = np.ascontiguousarray(a)
        aps[name] = nc.dram_tensor(f"in_{name}", a.shape, mybir.dt.from_np(a.dtype), kind="ExternalInput").ap()
    out = nc.dram_tensor("out", (T, D), F32, kind="ExternalOutput").ap()
    program(nc, aps, out)
    got = run_bass_kernel_spmd(nc, [arrays], core_ids=[0]).results[0]["out"]
    return got.reshape(1, T, D)
```

```python
from contextlib import ExitStack

import numpy as np

import concourse.bass as bass
from concourse import mybir

F32 = mybir.dt.float32
F32R = mybir.dt.float32r
I32 = mybir.dt.int32
ALU = mybir.AluOpType
ACT = mybir.ActivationFunctionType
AX = mybir.AxisListType

P = 128
D = 1024
T = 512
KT = D // P
TT = T // P
DFF = 2816
FT = DFF // P
HALF = FT // 2
NFFN = 4
EPS = 1e-6
HEADS = 8
HD = 64
TOPK = T // 4
ROUNDS = TOPK // 8
LEVELS = 7
NEG = -3.0e38
MARK = -3.3e38
SPLIT = -3.15e38

EV_UNITS = [("ik", 0)] + [("iq", m) for m in range(4)] + [("k", m) for m in range(4)] + [("q", m) for m in range(4)] \
    + [("v", m) for m in range(4)] + [(w, m) for m in range(4) for w in "cxb"]
OD_UNITS = [("ba", 0)] + [(w, h) for h in range(HEADS) for w in "qkv"] + [("z", h) for h in range(HEADS)]
ROPED = ("iq", "k", "q")

FFN_UNITS, FFN_STEPS = 2 * FT + 2 * KT, FT + KT
EV_N, EV_S = FFN_UNITS, FFN_STEPS
EVO_N, EVO_S = EV_N + len(EV_UNITS), EV_S + len(EV_UNITS)
F1_N, F1_S = EVO_N + KT, EVO_S + KT
F2_N, F2_S = F1_N + FFN_UNITS, F1_S + FFN_STEPS
OD_N, OD_S = F2_N + FFN_UNITS, F2_S + FFN_STEPS
ODO_N, ODO_S = OD_N + len(OD_UNITS), OD_S + len(OD_UNITS)
F3_N, F3_S = ODO_N + KT, ODO_S + KT
FFN_AT = [(0, 0), (F1_N, F1_S), (F2_N, F2_S), (F3_N, F3_S)]
N_END = F3_N + FFN_UNITS
GU0, EV0 = 0, 2 * FT
EVO0 = EV0 + len(EV_UNITS)
GU1 = EVO0 + KT
GU2 = GU1 + 2 * FT
OD0 = GU2 + 2 * FT
ODO0 = OD0 + len(OD_UNITS)
GU3 = ODO0 + KT
GU_ROW = [GU0, GU1, GU2, GU3]
ROWS8 = GU3 + 2 * FT

CONSTS = ["ident", "ones", "tri", "neg_future", "rot", "dup", "dup_rot"] + [f"level{l}" for l in range(1, LEVELS + 1)]


def unit_width(n):
    for n0, _ in FFN_AT:
        if n0 + 2 * FT <= n < n0 + FFN_UNITS:
            return HALF * P
    return KT * P


def ev_extras():
    idx = [("idx", b, h) for b in range(1, TT) for h in range(HEADS)]
    top = [("top", b, r) for b in range(1, TT) for r in range(ROUNDS)]
    out = {}
    for u in range(len(EV_UNITS)):
        for k in (1, 4, 6):
            if u >= 6 and idx:
                out[u * KT + k] = [idx.pop(0)]
        for k in (2, 5, 7):
            if u >= 9 and top:
                out[u * KT + k] = [top.pop(0)]
    assert not idx and not top
    return out


ATT_UNIT = 18


def attention_slots():
    slots = (len(EV_UNITS) - ATT_UNIT) * KT
    out = {}
    for q in range(Q_ITEMS + 2):
        out.setdefault(ATT_UNIT * KT + q * slots // (Q_ITEMS + 2), []).append(q)
    return out


CHAIN1 = ["square", "norm", "decay", "mask", "gram", "turn1"] \
    + [f"{w}{l}" for l in range(2, LEVELS + 1) for w in ("y", "t")]
CHAIN2 = ["w"] + [f"{w}{t}" for t in range(TT) for w in ("new", "out")] + ["osquare", "osum", "fin"]


def delta_slots():
    per = 3 * KT
    out = {}
    for g in range(HEADS):
        for at, chain in ((per * (g + 1) + SHIFT1, CHAIN1), (per * (g + 2) + SHIFT2, CHAIN2)):
            for i, name in enumerate(chain):
                out.setdefault(at + i * per // len(chain), []).append((g, name))
    assert max(out) < 4 * HEADS * KT
    return out


SHIFT1 = 6
SHIFT2 = 8
TU = 2 * LEVELS - 1
TM = 2 * (LEVELS - 1) - 1
N_SIDE = 17
Q_ITEMS = TT * HEADS


def norm_of(f):
    return (0, 2, 3, 5)[f]


def pi_parts(value, count, bits=7):
    parts = []
    for _ in range(count):
        scale = 2.0 ** (np.floor(np.log2(value)) - bits + 1)
        parts.append(float(np.floor(value / scale) * scale))
        value -= parts[-1]
    return parts


def program(nc, A, out):
    with ExitStack() as ctx:
        def sem(name):
            return ctx.enter_context(nc.semaphore(name))

        def sb(name, shape, dt=F32):
            return nc.alloc_sbuf_tensor(name, [P] + shape, dt)

        x = sb("x", [KT, T])
        h_hi, h_lo = sb("h_hi", [KT, T], F32R), sb("h_lo", [KT, T], F32R)
        raw = sb("raw", [4, HALF * P])
        w_hi, w_lo = sb("w_hi", [2, HALF * P], F32R), sb("w_lo", [2, HALF * P], F32R)
        consts = sb("consts", [len(CONSTS), P])
        gains = sb("gains", [7, KT])
        eps = sb("eps", [1])
        silu_g = sb("silu_g", [2, T])
        act_f = sb("act_f", [2, T])
        sq = sb("sq", [2, T])
        sq_acc = sb("sq_acc", [T])
        rstd = sb("rstd", [T])
        hf = sb("hf", [2, T])
        const = {name: consts[:, i, :] for i, name in enumerate(CONSTS)}

        region = nc.sbuf_base
        region0 = (region + 31) // 32 * 32
        region_end = nc.sbuf_usable_end

        class Plan:
            def __init__(self):
                self.at = region0

            def __call__(self, name, shape, dt=F32):
                t = nc.alloc_sbuf_tensor_at(name, [P] + shape, dt, offset=self.at)
                self.at += int(np.prod(shape)) * 4
                self.at = (self.at + 31) // 32 * 32
                assert self.at <= region_end, (name, self.at, region_end)
                return t

        io = Plan()
        x_rows = io("x_rows", [TT, D])
        ffn = Plan()
        a_hi, a_lo = ffn("a_hi", [FT, T], F32R), ffn("a_lo", [FT, T], F32R)

        ev = Plan()
        emix_hi, emix_lo = ev("emix_hi", [KT, T], F32R), ev("emix_lo", [KT, T], F32R)
        iq, qT, kT = ev("iq", [4, T]), ev("qT", [4, T]), ev("kT", [4, T])
        ik = ev("ik", [T])
        vtok = ev("vtok", [TT, 4, P])
        y_f = iq
        cosT, sinT = ev("cosT", [T]), ev("sinT", [T])
        roped_in = hf
        cbuf, ubuf = ev("cbuf", [T]), ev("ubuf", [T])
        score = ev("score", [TT - 1, T])
        relu_s = ev("relu_s", [2, T])
        probs = silu_g
        probsT = ev("probsT", [2, TT, P])
        w_idx = ev("w_idx", [TT, HEADS])
        top8 = ev("top8", [8])
        amax, asum = ev("amax", [2]), ev("asum", [2])
        amax_n, arcp = ev("amax_n", [2]), ev("arcp", [2])
        ev_conv = ev("ev_conv", [4, 3])
        freq = ev("freq", [1])

        od = Plan()
        omix_hi, omix_lo = od("omix_hi", [KT, T], F32R), od("omix_lo", [KT, T], F32R)
        o_n = nc.alloc_sbuf_tensor_at("o_n", [P, KT, T], F32, offset=region0 + KT * T * 4)
        qc, kc, vc = (od(n, [2, T]) for n in ("qc", "kc", "vc"))
        kn = od("kn", [TT, P])
        g_b = od("g_b", [TT, P])
        dec_t, dec_a = od("dec_t", [TT, P]), od("dec_a", [TT, P])
        a_mat = od("a_mat", [TT, P])
        b_lvl = od("b_lvl", [2, TT, P])
        t_inv = od("t_inv", [TT, P])
        y_lvl = g_b
        u_inv, e_row, intra_t = (od(n, [2, TT, P]) for n in ("u_inv", "e_row", "intra_t"))
        v_beta, k_beg, k_dec = (od(n, [2, TT, P]) for n in ("v_beta", "k_beg", "k_dec"))
        q_dec = nc.alloc_sbuf_tensor_at("q_dec", [P, 2, TT, P], F32, offset=region0 + 5 * T * 4)
        neg_w = nc.alloc_sbuf_tensor_at("neg_w", [P, TT, P], F32, offset=region0 + 7 * T * 4)
        pre = hf[:, 1, :]
        state, v_new = od("state", [2, P]), od("v_new", [2, P])
        g_tok, g_cum = od("g_tok", [TT, HEADS]), od("g_cum", [TT, HEADS])
        beta, beg = od("beta", [TT, HEADS]), od("beg", [TT, HEADS])
        ba_tok = od("ba_tok", [TT, 2 * HEADS])
        gt1, gt2 = od("gt1", [TT, HEADS]), od("gt2", [TT, HEADS])
        alog, dtb = od("alog", [HEADS]), od("dtb", [HEADS])
        od_conv = od("od_conv", [3 * HEADS, 4])
        o_gain = od("o_gain", [1])

        fin = Plan()
        y_out = fin("y_out", [KT, T])
        y_rows = fin("y_rows", [2, D])

        prod = nc.alloc_psum_tensor("prod", [P, 4, T], F32)
        misc = nc.alloc_psum_tensor("misc", [P, 4, T], F32)

        def tiles(ap):
            return ap.rearrange("p (t c) -> p t c", t=TT)

        setup_in = sem("setup_in")
        raw_in = [sem(f"raw_in{i}") for i in range(4)]
        hi_ready, lo_ready, unit_done, evac = sem("hi_ready"), sem("lo_ready"), sem("unit_done"), sem("evac")
        x_turned, x_in = sem("x_turned"), sem("x_in")
        sq_ready, acc_done, sum_done, rstd_ready = sem("sq_ready"), sem("acc_done"), sem("sum_done"), sem("rstd_ready")
        hhi_ready, h_ready, y_made = sem("hhi_ready"), sem("h_ready"), sem("y_made")
        gate_scaled, silu_done, a_scaled = sem("gate_scaled"), sem("silu_done"), sem("a_scaled")
        ahi_ready, a_ready = sem("ahi_ready"), sem("a_ready")
        act_seq, dve_seq, pool_seq = sem("act_seq"), sem("dve_seq"), sem("pool_seq")
        ev_in, od_in = sem("ev_in"), sem("od_in")
        ang_ready, trig_ready = sem("ang_ready"), sem("trig_ready")
        rot_done, cos_part, roped = sem("rot_done"), sem("cos_part"), sem("roped")
        idx_mm, relu_done, idx_added = sem("idx_mm"), sem("relu_done"), sem("idx_added")
        y_conv, emhi, emix_ready = sem("y_conv"), sem("emhi"), sem("emix_ready")
        logit_mm, masked, exp_done, probs_ready = sem("logit_mm"), sem("masked"), sem("exp_done"), sem("probs_ready")
        turned, probsT_ready, pv_done, y_taken = sem("turned"), sem("probsT_ready"), sem("pv_done"), sem("y_taken")
        conv_done, act_done, state_mm = sem("conv_done"), sem("act_done"), sem("state_mm")
        ba_turned, ba_tok_in, gate_exp = sem("ba_turned"), sem("ba_tok_in"), sem("gate_exp")
        g_ready, gcum_mm, g_cum_in, gate_in = sem("g_ready"), sem("gcum_mm"), sem("g_cum_in"), sem("gate_in")
        qk_sq, qk_sum, qk_rstd, qk_ready = sem("qk_sq"), sem("qk_sum"), sem("qk_rstd"), sem("qk_ready")
        gb_ready, grow_mm, dif_ready, dec_exp = sem("gb_ready"), sem("grow_mm"), sem("dif_ready"), sem("dec_exp")
        dec_ready, gram_mm, a_made = sem("dec_ready"), sem("gram_mm"), sem("a_made")
        b_made, b1_turned, tu_ready = sem("b_made"), sem("b1_turned"), sem("tu_ready")
        y_mm, y_ready, t_mm = sem("y_mm"), sem("y_ready"), sem("t_mm")
        w_mm, w_ready = sem("w_mm"), sem("w_ready")
        vnew_mm, vnew_ready, out_mm, state_ready = sem("vnew_mm"), sem("vnew_ready"), sem("out_mm"), sem("state_ready")
        o_sq, o_sum, o_rstd, on_ready = (sem(n) for n in ("o_sq", "o_sum", "o_rstd", "on_ready"))
        gated, ohi, omix_ready = sem("gated"), sem("ohi"), sem("omix_ready")
        qdec_ready, e_row_ready = sem("qdec_ready"), sem("e_row_ready")
        y_turned, y_rows_in, stored = sem("y_turned"), sem("y_rows_in"), [sem("stored0"), sem("stored1")]
        SETUP = 4

        block = ctx.enter_context(nc.Block())
        extras = ev_extras()
        att_slots = attention_slots()
        od_slots = delta_slots()

        @block.sync
        def _(sp):
            def load(n, src, i=0):
                if n >= 4:
                    sp.wait_ge(lo_ready, n - 3 + 4 * i)
                sp.dma_start(raw[:, n % 4, 0:unit_width(n)], src).then_inc(raw_in[n % 4], 16)

            def ffn_loads(f):
                n0, row0 = FFN_AT[f][0], GU_ROW[f]
                for u in range(4):
                    load(n0 + u, A["w8"][row0 + u])
                with sp.Fori(1, 2 * FT // 4) as i:
                    for u in range(4):
                        row = i * 4 + (row0 + u)
                        sp.wait_ge(lo_ready, i * 4 + (n0 + u - 3))
                        sp.dma_start(raw[:, (n0 + u) % 4, 0:KT * P],
                                     A["w8"][bass.ds(row, 1)].rearrange("a p c -> (a p) c")).then_inc(raw_in[(n0 + u) % 4], 16)
                with sp.Fori(0, 2 * KT // 4) as i:
                    for u in range(4):
                        n = n0 + 2 * FT + u
                        row = i * 4 + (f * 2 * KT + u)
                        sp.wait_ge(lo_ready, i * 4 + (n - 3))
                        sp.dma_start(raw[:, n % 4, :],
                                     A["wd"][bass.ds(row, 1)].rearrange("a p c -> (a p) c")).then_inc(raw_in[n % 4], 16)

            sp.dma_start(x_rows[:], A["x"].rearrange("(t p) d -> p t d", p=P)).then_inc(setup_in, 16)
            sp.dma_start(consts[:], A["consts"]).then_inc(setup_in, 16)
            sp.dma_start(gains[:], A["gains"]).then_inc(setup_in, 16)
            sp.dma_start(eps[:], A["eps"]).then_inc(setup_in, 16)
            ffn_loads(0)
            for u in range(4):
                load(EV_N + u, A["w8"][EV0 + u])
            sp.wait_ge(evac, FFN_STEPS)
            sp.dma_start(ev_conv[:], A["ev_conv"]).then_inc(ev_in, 16)
            sp.dma_start(freq[:], A["freq"]).then_inc(ev_in, 16)
            sp.dma_start(cbuf[:].bitcast(I32), A["pos"].broadcast_to([P, T])).then_inc(ev_in, 16)
            for u in range(4, len(EV_UNITS) + KT):
                load(EV_N + u, A["w8"][EV0 + u])
            ffn_loads(1)
            ffn_loads(2)
            for u in range(4):
                load(OD_N + u, A["w8"][OD0 + u])
            sp.wait_ge(evac, OD_S)
            sp.dma_start(alog[:], A["alog"].broadcast_to([P, HEADS])).then_inc(od_in, 16)
            sp.dma_start(dtb[:], A["dtb"].broadcast_to([P, HEADS])).then_inc(od_in, 16)
            sp.dma_start(od_conv[:], A["od_conv"]).then_inc(od_in, 16)
            sp.dma_start(o_gain[:], A["o_gain"]).then_inc(od_in, 16)
            for u in range(4, len(OD_UNITS) + KT):
                load(OD_N + u, A["w8"][OD0 + u])
            ffn_loads(3)
            for t in range(TT):
                sp.wait_ge(y_rows_in, t + 1)
                sp.dma_start(out[t * P:(t + 1) * P, :], y_rows[:, t % 2, :]).then_inc(stored[t % 2], 16)
            sp.wait_ge(stored[0], 16 * TT // 2)
            sp.wait_ge(stored[1], 16 * TT // 2)

        @block.tensor
        def _(pe):
            def unit(n, bank, k0, acts, first, last, i=0, between=None, wait_k=None):
                pe.wait_ge(lo_ready, n + 1 + 4 * i)
                tiles_n = unit_width(n) // P
                for k in range(tiles_n):
                    if wait_k is not None:
                        wait_k(k)
                    hi, lo = acts(k0 + k)
                    wh = w_hi[:, n % 2, k * P:(k + 1) * P]
                    wl = w_lo[:, n % 2, k * P:(k + 1) * P]
                    pe.matmul(bank, wh, hi, start=first and k == 0, stop=False)
                    pe.matmul(bank, wh, lo, start=False, stop=False)
                    ins = pe.matmul(bank, wl, hi, start=False, stop=last and k == tiles_n - 1)
                    if k == tiles_n - 1:
                        ins.then_inc(unit_done, 1)
                    if between is not None:
                        between(k)

            def h_act(k):
                return h_hi[:, k, :], h_lo[:, k, :]

            def a_act(k):
                return a_hi[:, k, :], a_lo[:, k, :]

            def bank_free(s, i=0):
                if not isinstance(i, int):
                    pe.wait_ge(evac, i * 2 + (s - 1))
                elif s >= 2:
                    pe.wait_ge(evac, s - 1)

            def square_sum(r):
                pe.wait_ge(acc_done, 6 * (r + 1))
                pe.matmul(misc[:, 0, :], const["ones"], sq_acc[:], start=True, stop=False)
                pe.wait_ge(sq_ready, 8 * (r + 1))
                pe.matmul(misc[:, 0, :], const["ones"], sq[:, 1, :], start=False, stop=True).then_inc(sum_done, 1)

            def first_unit(r, n, bank):
                unit(n, bank, 0, h_act, True, True, wait_k=lambda k: pe.wait_ge(h_ready, 8 * r + k + 1),
                     between=lambda k: square_sum(r) if k == KT - 1 else None)

            def ffn_pe(f):
                n0, s0 = FFN_AT[f]

                def pairs(i, first):
                    for u in range(4):
                        s = s0 + u // 2
                        if u % 2 == 0:
                            bank_free(s, i)
                        bank = prod[:, 2 * (s % 2) + u % 2, :]
                        if first and u == 0:
                            first_unit(norm_of(f), n0, bank)
                        else:
                            unit(n0 + u, bank, 0, h_act, True, True, i)

                pairs(0, True)
                with pe.Fori(1, FT // 2) as i:
                    pairs(i, False)
                for m in range(KT):
                    s = s0 + FT + m
                    bank_free(s)
                    for half in range(2):
                        unit(n0 + 2 * FT + 2 * m + half, prod[:, 2 * (s % 2), :], half * HALF, a_act,
                             half == 0, half == 1,
                             wait_k=(lambda k, half=half: pe.wait_ge(a_ready, FT * f + half * HALF + k + 1))
                             if m == 0 else None)

            def out_pe(n0, s0, acts, wait_k):
                for m in range(KT):
                    bank_free(s0 + m)
                    unit(n0 + m, prod[:, 2 * ((s0 + m) % 2), :], 0, acts, True, True,
                         wait_k=wait_k if m == 0 else None)

            pe.wait_ge(setup_in, 16 * SETUP)
            for k in range(KT):
                if k >= 4:
                    pe.wait_ge(x_in, k - 3)
                for t in range(TT):
                    ins = pe.transpose(prod[:, k % 4, t * P:(t + 1) * P], x_rows[:, t, k * P:(k + 1) * P], const["ident"])
                ins.then_inc(x_turned, 1)
            pe.wait_ge(x_in, KT)
            ffn_pe(0)

            def idx_pe(b, h):
                q = (b - 1) * HEADS + h
                if b == 1 and h == 0:
                    pe.wait_ge(roped, 5)
                if q >= 2:
                    pe.wait_ge(relu_done, q - 1)
                r = slice(HD * (h % 2), HD * (h % 2) + HD)
                w = (b + 1) * P
                pe.matmul(prod[:, 1 + 2 * (q % 2), 0:w], iq[r, h // 2, b * P:(b + 1) * P], ik[r, 0:w],
                          start=True, stop=True).then_inc(idx_mm, 1)

            def ev_extra_pe(slot):
                for kind, b, j in extras.get(slot, []):
                    if kind == "idx":
                        idx_pe(b, j)

            def ev_side_pe(u):
                kind, m = EV_UNITS[u]
                if kind == "ik":
                    pe.wait_ge(evac, EV_S + 1)
                    pe.wait_ge(rstd_ready, 2)
                    pe.matmul(misc[:, 0, :], const["dup"], roped_in[:, 0, :], start=True, stop=True)
                    pe.matmul(misc[:, 1, :], const["dup_rot"], roped_in[:, 0, :], start=True, stop=True)
                    for t in range(TT):
                        ins = pe.matmul(misc[:, 2, t * HEADS:(t + 1) * HEADS], roped_in[:, 0, t * P:(t + 1) * P],
                                        const["ident"][:, HD:HD + HEADS], start=True, stop=True)
                    ins.then_inc(rot_done, 1)
                elif kind in ROPED:
                    pe.wait_ge(evac, EV_S + u + 1)
                    pe.wait_ge(roped, u)
                    pe.matmul(misc[:, 0, :], const["rot"], roped_in[:, u % 2, :], start=True, stop=True)\
                        .then_inc(rot_done, 1)
                elif kind == "v":
                    pe.wait_ge(evac, EV_S + u + 1)
                    pe.wait_ge(roped, u)
                    for t in range(TT):
                        ins = pe.transpose(misc[:, 0, t * P:(t + 1) * P], roped_in[:, u % 2, t * P:(t + 1) * P],
                                           const["ident"])
                    ins.then_inc(rot_done, 1)

            def att(q):
                return q // HEADS, q % HEADS, slice(HD * (q % 2), HD * (q % 2) + HD)

            def att_logits(q):
                b, h, r = att(q)
                if q == 0:
                    pe.wait_ge(roped, N_SIDE)
                if q >= 2:
                    pe.wait_ge(masked, q - 1)
                w = (b + 1) * P
                pe.matmul(misc[:, q % 2, 0:w], qT[r, h // 2, b * P:(b + 1) * P], kT[r, h // 2, 0:w],
                          start=True, stop=True).then_inc(logit_mm, 1)

            def att_turn(q):
                b = q // HEADS
                pe.wait_ge(probs_ready, q + 1)
                if q >= 1:
                    pe.wait_ge(probsT_ready, q)
                for c in range(b + 1):
                    ins = pe.transpose(misc[:, 2, c * P:(c + 1) * P], probs[:, q % 2, c * P:(c + 1) * P], const["ident"])
                ins.then_inc(turned, 1)

            def att_pv(q):
                b, h, r = att(q)
                pe.wait_ge(probsT_ready, q + 1)
                if q >= 1:
                    pe.wait_ge(y_taken, q)
                for c in range(b + 1):
                    ins = pe.matmul(misc[r, 3, 0:P], vtok[:, c, h // 2, r.start:r.stop], probsT[:, q % 2, c, :],
                                    start=c == 0, stop=c == b)
                ins.then_inc(pv_done, 1)

            def att_pe(q):
                if q < Q_ITEMS:
                    att_logits(q)
                if 1 <= q <= Q_ITEMS:
                    att_turn(q - 1)
                if q >= 2:
                    att_pv(q - 2)

            for u in range(len(EV_UNITS)):
                s = EV_S + u
                bank_free(s)
                if u == 0:
                    first_unit(1, EV_N, prod[:, 2 * (s % 2), :])
                    continue

                def between(k, u=u):
                    for q in att_slots.get(u * KT + k, []):
                        att_pe(q)
                    if k == 3:
                        ev_side_pe(u - 1)
                    ev_extra_pe(u * KT + k)

                unit(EV_N + u, prod[:, 2 * (s % 2), :], 0, h_act, True, True, between=between)
            out_pe(EVO_N, EVO_S, lambda k: (emix_hi[:, k, :], emix_lo[:, k, :]),
                   lambda k: pe.wait_ge(emix_ready, k + 1))
            ffn_pe(1)
            ffn_pe(2)

            def prep_pe(j):
                if j == 2:
                    pe.wait_ge(evac, OD_S + 1)
                    pe.wait_ge(rstd_ready, 5)
                    for t in range(TT):
                        ins = pe.matmul(misc[:, 0, t * 16:(t + 1) * 16], hf[:, 0, t * P:(t + 1) * P],
                                        const["ident"][:, 0:16], start=True, stop=True)
                    ins.then_inc(ba_turned, 1)
                if j == 12:
                    pe.wait_ge(g_ready, 1)
                    pe.matmul(misc[:, 1, 0:TT * HEADS], const["tri"], g_tok[:].rearrange("p t h -> p (t h)"),
                              start=True, stop=True).then_inc(gcum_mm, 1)

            def each(dst, lhs, rhs, start=True, stop=True):
                for t in range(TT):
                    ins = pe.matmul(dst[:, t, :], lhs[:, t, :], rhs[:, t, :], start=start, stop=stop)
                return ins

            M = [tiles(misc[:, i, :]) for i in range(4)]
            X = [tiles(prod[:, i, :]) for i in (1, 3)]

            def stage_pe(g, name):
                tri4 = const["tri"]
                L = g * (LEVELS - 1)
                i = g % 2
                if name == "norm":
                    pe.wait_ge(qk_sq, g + 1)
                    if g >= 1:
                        pe.wait_ge(tu_ready, TU * g)
                    pe.matmul(misc[:, 0, :], const["ones"], sq[:, 0, :], start=True, stop=True)
                    pe.matmul(misc[:, 1, :], const["ones"], sq[:, 1, :], start=True, stop=True).then_inc(qk_sum, 1)
                    pe.wait_ge(gb_ready, g + 1)
                    for t in range(TT):
                        ins = pe.matmul(M[2][:, t, :], g_b[:, t, :], tri4, start=True, stop=True)
                    ins.then_inc(grow_mm, 1)
                elif name == "gram":
                    pe.wait_ge(qk_ready, g + 1)
                    pe.wait_ge(dif_ready, g + 1)
                    each(M[0], kn, kn)
                    each(M[1], kn, tiles(qc[:, g % 2, :]))
                    for t in range(TT):
                        pe.transpose(M[2][:, t, :], kn[:, t, :], const["ident"])
                    for t in range(TT):
                        ins = pe.transpose(M[3][:, t, :], vc[:, g % 2, t * P:(t + 1) * P], const["ident"])
                    ins.then_inc(gram_mm, 1)
                elif name == "turn1":
                    pe.wait_ge(b_made, LEVELS * g + 1)
                    pe.wait_ge(a_made, 5 * (g + 1))
                    for t in range(TT):
                        ins = pe.transpose(M[0][:, t, :], b_lvl[:, 1, t, :], const["ident"])
                    ins.then_inc(b1_turned, 1)
                elif name[0] == "y":
                    l = int(name[1:])
                    pe.wait_ge(b_made, LEVELS * g + l)
                    pe.wait_ge(tu_ready, TU * g + 2 * (l - 1) - (l > 2))
                    each(M[3], b_lvl[:, l % 2], u_inv[:, i]).then_inc(y_mm, 1)
                elif name[0] == "t":
                    l = int(name[1:])
                    pe.wait_ge(y_ready, L + l - 1)
                    pe.wait_ge(tu_ready, TU * g + 2 * (l - 1))
                    each(M[2], t_inv, y_lvl).then_inc(t_mm, 1)
                    if l < LEVELS:
                        each(M[1], y_lvl, t_inv).then_inc(t_mm, 1)
                elif name == "w":
                    pe.wait_ge(tu_ready, TU * (g + 1))
                    if g >= 1:
                        pe.wait_ge(o_rstd, g)
                    each(X[1], k_beg[:, i], u_inv[:, i]).then_inc(w_mm, 1)
                elif name[:3] == "new":
                    t = int(name[3:])
                    if t == 0:
                        pe.wait_ge(w_ready, g + 1)
                    else:
                        pe.wait_ge(state_ready, (TT - 1) * g + t)
                    ins = pe.matmul(X[1][:, t, :], u_inv[:, i, t, :], v_beta[:, i, t, :], start=True, stop=t == 0)
                    if t:
                        ins = pe.matmul(X[1][:, t, :], neg_w[:, t, :], state[:, t % 2, :], start=False, stop=True)
                    ins.then_inc(vnew_mm, 1)
                elif name[:3] == "out":
                    t = int(name[3:])
                    pe.wait_ge(vnew_ready, TT * g + t + 1)
                    if t == 0:
                        pe.wait_ge(qdec_ready, g + 1)
                        if g >= 1:
                            pe.wait_ge(on_ready, g)
                    if t < TT - 1:
                        pe.matmul(X[1][:, t, :], k_dec[:, i, t, :], v_new[:, t % 2, :], start=True, stop=True)\
                            .then_inc(state_mm, 1)
                    if t:
                        pe.matmul(X[0][:, t, :], state[:, t % 2, :], q_dec[:, i, t, :], start=True, stop=False)
                    pe.matmul(X[0][:, t, :], v_new[:, t % 2, :], intra_t[:, i, t, :], start=t == 0, stop=True)\
                        .then_inc(out_mm, 1)
                elif name == "osum":
                    pe.wait_ge(o_sq, g + 1)
                    pe.matmul(prod[:, 3, :], const["ones"], sq_acc[:], start=True, stop=True).then_inc(o_sum, 1)

            for u in range(len(OD_UNITS)):
                s = OD_S + u
                bank_free(s)
                if u == 0:
                    first_unit(4, OD_N, prod[:, 2 * (s % 2), :])
                    continue

                def between(k, u=u):
                    slot = (u - 1) * KT + k
                    prep_pe(slot)
                    for g, name in od_slots.get(slot, []):
                        stage_pe(g, name)

                unit(OD_N + u, prod[:, 2 * (s % 2), :], 0, h_act, True, True, between=between)
            out_pe(ODO_N, ODO_S, lambda k: (omix_hi[:, k, :], omix_lo[:, k, :]),
                   lambda k: pe.wait_ge(omix_ready, k + 1))
            ffn_pe(3)

            square_sum(6)
            for t in range(TT):
                if t == 0:
                    pe.wait_ge(y_made, KT)
                if t >= 2:
                    pe.wait_ge(y_rows_in, t - 1)
                for k in range(KT):
                    ins = pe.transpose(prod[:, 2 * (t % 2) + k // 4, (k % 4) * P:(k % 4 + 1) * P],
                                       y_out[:, k, t * P:(t + 1) * P], const["ident"])
                ins.then_inc(y_turned, 1)

        @block.scalar
        def _(act):
            seq = [0]

            def link(ins):
                seq[0] += 1
                ins.then_inc(act_seq, 1)
                act.wait_ge(act_seq, seq[0])

            def split(n, i=0):
                if n >= N_END:
                    return
                act.wait_ge(raw_in[n % 4], 16 * (n // 4 + 1) + 16 * i)
                if n >= 2:
                    act.wait_ge(unit_done, n - 1 + 4 * i)
                w = unit_width(n)
                act.activation(w_hi[:, n % 2, 0:w], raw[:, n % 4, 0:w], ACT.Copy).then_inc(hi_ready, 1)

            def tile(r, m, ready, count):
                act.wait_ge(ready, count)
                if r < 6:
                    act.activation(h_hi[:, m, :], x[:, m, :], ACT.Copy, scale=gains[:, r, m:m + 1])\
                        .then_inc(hhi_ready, 1)
                if m >= 2:
                    act.wait_ge(acc_done, 6 * r + max(m - 2, 1))
                act.activation(sq[:, m % 2, :], x[:, m, :], ACT.Square).then_inc(sq_ready, 1)

            def norm(r):
                act.wait_ge(sum_done, r + 1)
                link(act.activation(rstd[:], misc[:, 0, :], ACT.Ln, bias=eps[:], scale=1.0 / D))
                act.activation(rstd[:], rstd[:], ACT.Exp, scale=-0.5).then_inc(rstd_ready, 1)

            def ffn_act(f):
                n0, s0 = FFN_AT[f]

                def pair(i, tail=False):
                    for u in range(4):
                        n, s = n0 + u, s0 + u // 2
                        if tail:
                            split(n0 + 2 * FT - 4 + u + 2)
                            j = FT - 2 + u // 2
                            sem_i, jj = FT // 2 - 1, j
                        else:
                            split(n + 2, i)
                            sem_i = i
                            jj = None
                        if u % 2 == 1:
                            act.wait_ge(a_scaled, FT * f + u // 2 + 1 + 2 * sem_i)
                            dst = a_hi[:, jj, :] if tail else \
                                a_hi[:, bass.ds(i * 2 + u // 2, 1), :].rearrange("p a c -> p (a c)")
                            act.activation(dst, act_f[:, s % 2, :], ACT.Copy).then_inc(ahi_ready, 1)
                        else:
                            act.wait_ge(gate_scaled, FT * f + u // 2 + 1 + 2 * sem_i)
                            act.activation(silu_g[:, s % 2, :], silu_g[:, s % 2, :], ACT.Silu).then_inc(silu_done, 1)

                with act.Fori(0, FT // 2 - 1) as i:
                    pair(i)
                pair(0, tail=True)
                for m in range(KT):
                    for half in range(2):
                        split(n0 + 2 * FT + 2 * m + half + 2)
                    tile(norm_of(f) + 1, m, evac, s0 + FT + m + 1)

            act.wait_ge(setup_in, 16 * SETUP)
            split(0)
            split(1)
            for k in range(KT):
                tile(0, k, x_in, k + 1)
            norm(0)
            ffn_act(0)
            norm(1)

            for i in range(2):
                act.wait_ge(ang_ready, i + 1)
                act.activation((sinT, cosT)[i][:], (sinT, cosT)[i][:], ACT.Sin).then_inc(trig_ready, 1)

            def ev_extra_act(slot):
                for kind, b, j in extras.get(slot, []):
                    if kind == "idx":
                        q = (b - 1) * HEADS + j
                        act.wait_ge(idx_mm, q + 1)
                        if q >= 2:
                            act.wait_ge(idx_added, q - 1)
                        act.activation(relu_s[:, q % 2, 0:(b + 1) * P], prod[:, 1 + 2 * (q % 2), 0:(b + 1) * P], ACT.Relu)\
                            .then_inc(relu_done, 1)

            def att_act(q):
                if q < Q_ITEMS:
                    act.wait_ge(masked, q + 1)
                    if q >= 2:
                        act.wait_ge(turned, q - 1)
                    w = (q // HEADS + 1) * P
                    act.activation(probs[:, q % 2, 0:w], relu_s[:, q % 2, 0:w], ACT.Exp, bias=amax_n[:, q % 2:q % 2 + 1],
                                   accum_out=asum[:, q % 2:q % 2 + 1]).then_inc(exp_done, 1)
                if 1 <= q <= Q_ITEMS:
                    c = (q - 1) // HEADS + 1
                    act.wait_ge(turned, q)
                    if q >= 3:
                        act.wait_ge(pv_done, q - 2)
                    act.activation(probsT[:, (q - 1) % 2, 0:c, :], tiles(misc[:, 2, :])[:, 0:c, :], ACT.Copy)\
                        .then_inc(probsT_ready, 1)

            for u in range(1, len(EV_UNITS) + 1):
                kind, m = EV_UNITS[u - 1]
                for k in range(KT):
                    for q in att_slots.get(u * KT + k, []):
                        att_act(q)
                    if k == 0:
                        split(EV_N + u + 1)
                    if k == 3 and kind == "b":
                        act.wait_ge(y_conv, m + 1)
                        act.activation(emix_hi[:, m, :], act_f[:, m % 2, :], ACT.Copy).then_inc(emhi, 1)
                    ev_extra_act(u * KT + k)
            act.wait_ge(y_taken, Q_ITEMS)
            for m in range(4):
                act.activation(emix_hi[:, 4 + m, :], y_f[:, m, :], ACT.Copy).then_inc(emhi, 1)
            for m in range(KT):
                split(EVO_N + m + 2)
                tile(2, m, evac, EVO_S + m + 1)
            norm(2)
            ffn_act(1)
            norm(3)
            ffn_act(2)
            norm(4)

            def prep_act(j):
                if j == 4:
                    act.wait_ge(ba_tok_in, 1)
                    act.activation(beta[:], ba_tok[:, :, 0:HEADS], ACT.Exp, scale=-1.0).then_inc(gate_exp, 1)
                    act.wait_ge(ba_tok_in, 2)
                    link(act.activation(gt1[:], gt1[:], ACT.Exp, scale=-1.0))
                    link(act.activation(gt1[:], gt1[:], ACT.Ln, bias=1.0))
                    act.activation(alog[:], alog[:], ACT.Exp).then_inc(gate_exp, 1)
                if j == 14:
                    act.wait_ge(g_cum_in, 1)
                    act.activation(beg[:], g_cum[:], ACT.Exp).then_inc(gate_exp, 1)

            M = [tiles(misc[:, i, :]) for i in range(4)]
            X = [tiles(prod[:, i, :]) for i in (1, 3)]

            def stage_act(g, name):
                L = g * (LEVELS - 1)
                i = g % 2
                if name == "square":
                    act.wait_ge(act_done, 3 * (g + 1))
                    act.activation(sq[:, 0, :], qc[:, i, :], ACT.Square)
                    act.activation(sq[:, 1, :], kc[:, i, :], ACT.Square).then_inc(qk_sq, 1)
                elif name == "norm":
                    act.wait_ge(qk_sum, g + 1)
                    act.activation(silu_g[:, 0, :], misc[:, 0, :], ACT.Ln, bias=eps[:])
                    link(act.activation(silu_g[:, 1, :], misc[:, 1, :], ACT.Ln, bias=eps[:]))
                    act.activation(silu_g[:, 0, :], silu_g[:, 0, :], ACT.Exp, scale=-0.5)
                    act.activation(silu_g[:, 1, :], silu_g[:, 1, :], ACT.Exp, scale=-0.5).then_inc(qk_rstd, 1)
                elif name == "decay":
                    act.wait_ge(grow_mm, g + 1)
                    act.activation(e_row[:, i], M[2], ACT.Exp).then_inc(e_row_ready, 1)
                elif name == "mask":
                    act.wait_ge(dif_ready, g + 1)
                    act.activation(dec_t[:], dec_t[:], ACT.Exp)
                    act.activation(dec_a[:], dec_a[:], ACT.Exp, scale=-1.0).then_inc(dec_exp, 1)
                elif name[0] == "y":
                    l = int(name[1:])
                    act.wait_ge(y_mm, L + l - 1)
                    act.activation(y_lvl[:], M[3], ACT.Copy).then_inc(y_ready, 1)
                elif name == "w":
                    act.wait_ge(w_mm, g + 1)
                    act.activation(neg_w[:], X[1], ACT.Copy, scale=-1.0).then_inc(w_ready, 1)
                elif name == "osquare":
                    act.wait_ge(out_mm, TT * (g + 1))
                    act.activation(sq_acc[:], prod[:, 1, :], ACT.Square).then_inc(o_sq, 1)
                elif name == "osum":
                    act.wait_ge(o_sum, g + 1)
                    link(act.activation(act_f[:, 1, :], prod[:, 3, :], ACT.Ln, bias=eps[:], scale=1.0 / P))
                    act.activation(act_f[:, 1, :], act_f[:, 1, :], ACT.Exp, scale=-0.5).then_inc(o_rstd, 1)

            for u in range(1, len(OD_UNITS) + 1):
                kind, h = OD_UNITS[u - 1]
                for k in range(KT):
                    slot = (u - 1) * KT + k
                    prep_act(slot)
                    for g, name in od_slots.get(slot, []):
                        stage_act(g, name)
                    if k == 0:
                        split(OD_N + u + 1)
                    if k == 2 and kind == "z":
                        act.wait_ge(evac, OD_S + u)
                        act.activation(hf[:, h % 2, :], hf[:, h % 2, :], ACT.Silu).then_inc(act_done, 1)
                    if k == 5 and kind == "z":
                        act.wait_ge(gated, h + 1)
                        act.activation(omix_hi[:, h, :], act_f[:, 0, :], ACT.Copy).then_inc(ohi, 1)
                    if k == 5 and kind in "qkv":
                        dst = {"q": qc, "k": kc, "v": vc}[kind][:, h % 2, :]
                        act.wait_ge(conv_done, u - 1)
                        act.activation(dst, dst, ACT.Silu).then_inc(act_done, 1)
            for m in range(KT):
                split(ODO_N + m + 2)
                tile(5, m, evac, ODO_S + m + 1)
            norm(5)
            ffn_act(3)
            norm(6)
            for t in range(TT):
                act.wait_ge(y_turned, t + 1)
                if t >= 2:
                    act.wait_ge(stored[t % 2], 16 * (t // 2))
                act.activation(y_rows[:, t % 2, :].rearrange("p (a c) -> p a c", a=2),
                               prod[:, 2 * (t % 2):2 * (t % 2) + 2, :], ACT.Copy).then_inc(y_rows_in, 1)

        @block.vector
        def _(dve):
            seq = [0]

            def link(ins):
                seq[0] += 1
                ins.then_inc(dve_seq, 1)
                dve.wait_ge(dve_seq, seq[0])

            def split(n, i=0):
                if n >= N_END:
                    return
                w = unit_width(n)
                dve.wait_ge(hi_ready, n + 1 + 4 * i)
                dve.tensor_tensor(w_lo[:, n % 2, 0:w], raw[:, n % 4, 0:w], w_hi[:, n % 2, 0:w].bitcast(F32),
                                  ALU.subtract).then_inc(lo_ready, 1)

            def lo(r, m):
                dve.wait_ge(hhi_ready, 8 * r + m + 1)
                dve.scalar_tensor_tensor(h_lo[:, m, :], x[:, m, :], gains[:, r, m:m + 1], h_hi[:, m, :].bitcast(F32),
                                         ALU.mult, ALU.subtract).then_inc(h_ready, 1)

            def residual(m, s, n_units, scale):
                dve.wait_ge(unit_done, n_units)
                dve.scalar_tensor_tensor(x[:, m, :], prod[:, 2 * (s % 2), :], scale, x[:, m, :], ALU.mult, ALU.add)\
                    .then_inc(evac, 1)

            def ffn_dve(f):
                n0, s0 = FFN_AT[f]

                def pair(i, tail=False):
                    for u in range(4):
                        n, s = n0 + u, s0 + u // 2
                        sem_i = FT // 2 - 1 if tail else i
                        if tail:
                            split(n0 + 2 * FT - 4 + u + 2)
                        else:
                            split(n + 2, i)
                        j = FT * f + u // 2
                        if u % 2 == 0:
                            dve.wait_ge(unit_done, n + 1 + 4 * sem_i)
                            if u == 0 and not tail:
                                dve.wait_ge(rstd_ready, norm_of(f) + 1)
                            dve.tensor_tensor(silu_g[:, s % 2, :], prod[:, 2 * (s % 2), :], rstd[:], ALU.mult)\
                                .then_inc(gate_scaled, 1)
                        else:
                            dve.wait_ge(silu_done, j + 1 + 2 * sem_i)
                            dve.wait_ge(unit_done, n + 1 + 4 * sem_i)
                            dve.tensor_tensor(act_f[:, s % 2, :], silu_g[:, s % 2, :], prod[:, 2 * (s % 2) + 1, :],
                                              ALU.mult).then_inc(evac, 1)
                            dve.wait_ge(evac, s + 1 + 2 * sem_i)
                            dve.tensor_tensor(act_f[:, s % 2, :], act_f[:, s % 2, :], rstd[:], ALU.mult)\
                                .then_inc(a_scaled, 1)
                            dve.wait_ge(ahi_ready, j + 1 + 2 * sem_i)
                            if tail:
                                hi, dst = a_hi[:, FT - 2 + u // 2, :], a_lo[:, FT - 2 + u // 2, :]
                            else:
                                hi, dst = (t[:, bass.ds(i * 2 + u // 2, 1), :].rearrange("p a c -> p (a c)")
                                           for t in (a_hi, a_lo))
                            dve.tensor_tensor(dst, act_f[:, s % 2, :], hi.bitcast(F32), ALU.subtract)\
                                .then_inc(a_ready, 1)
                            dve.wait_ge(a_ready, j + 1 + 2 * sem_i)

                with dve.Fori(0, FT // 2 - 1) as i:
                    pair(i)
                pair(0, tail=True)
                for m in range(KT):
                    for half in range(2):
                        split(n0 + 2 * FT + 2 * m + half + 2)
                    residual(m, s0 + FT + m, n0 + 2 * FT + 2 * m + 2, 0.5)
                    if f < NFFN - 1:
                        lo(norm_of(f) + 1, m)

            split(0)
            split(1)
            for k in range(KT):
                dve.wait_ge(x_turned, k + 1)
                dve.tensor_copy(x[:, k, :], prod[:, k % 4, :]).then_inc(x_in, 1)
                if k:
                    lo(0, k - 1)
            lo(0, KT - 1)
            ffn_dve(0)

            dve.wait_ge(ev_in, 16 * 3)
            link(dve.tensor_copy(ubuf[:], cbuf[:].bitcast(I32)))
            link(dve.tensor_scalar(ubuf[:], ubuf[:], freq[:], None, ALU.mult))
            magic = 1.5 * 2.0 ** 23
            for unit_2pi, parts in ((4096.0, 7), (1.0, 6)):
                link(dve.tensor_scalar(cbuf[:], ubuf[:], float(1.0 / (2 * np.pi * unit_2pi)), magic, ALU.mult, ALU.add))
                link(dve.tensor_scalar(cbuf[:], cbuf[:], magic, None, ALU.subtract))
                for part in pi_parts(2 * np.pi * unit_2pi, parts):
                    link(dve.scalar_tensor_tensor(ubuf[:], cbuf[:], -part, ubuf[:], ALU.mult, ALU.add))
            link(dve.tensor_scalar(ubuf[:], ubuf[:], 3.141592, -3.141592, ALU.min, ALU.max))
            dve.tensor_copy(sinT[:], ubuf[:]).then_inc(ang_ready, 1)
            link(dve.scalar_tensor_tensor(cosT[:], ubuf[:], -1.0, ubuf[:], ALU.mult, ALU.max))
            dve.tensor_scalar(cosT[:], cosT[:], -1.0, float(np.float32(np.pi / 2)), ALU.mult, ALU.add)\
                .then_inc(ang_ready, 1)

            def ev_extra_dve(items):
                for kind, b, j in items:
                    w = (b + 1) * P
                    if kind == "idx":
                        q = (b - 1) * HEADS + j
                        dve.wait_ge(relu_done, q + 1)
                        wcol = w_idx[:, b, j:j + 1]
                        if j == 0:
                            ins = dve.tensor_scalar(score[:, b - 1, 0:w], relu_s[:, q % 2, 0:w], wcol, None, ALU.mult)
                        else:
                            ins = dve.scalar_tensor_tensor(score[:, b - 1, 0:w], relu_s[:, q % 2, 0:w], wcol,
                                                           score[:, b - 1, 0:w], ALU.mult, ALU.add)
                        ins.then_inc(idx_added, 1)
                        dve.wait_ge(idx_added, q + 1)
                        if j == HEADS - 1:
                            link(dve.tensor_tensor(score[:, b - 1, b * P:w], score[:, b - 1, b * P:w], const["neg_future"],
                                                   ALU.add))
                    else:
                        link(dve.max(top8[:], score[:, b - 1, 0:w]))
                        link(dve.match_replace(score[:, b - 1, 0:w], top8[:], score[:, b - 1, 0:w], MARK))
                        if j == ROUNDS - 1:
                            link(dve.tensor_scalar(score[:, b - 1, 0:w], score[:, b - 1, 0:w], SPLIT, NEG,
                                                   ALU.is_gt, ALU.mult))

            def ev_side_dve(u):
                kind, m = EV_UNITS[u]
                if kind == "ik":
                    dve.wait_ge(rot_done, 1)
                    dve.wait_ge(trig_ready, 2)
                    dve.tensor_scalar(w_idx[:].rearrange("p t h -> p (t h)"), misc[:, 2, 0:TT * HEADS],
                                      float((HEADS * HD) ** -0.5), None, ALU.mult)
                    dve.tensor_tensor(ubuf[:], misc[:, 1, :], sinT[:], ALU.mult)
                    link(dve.tensor_tensor(ik[:], misc[:, 0, :], cosT[:], ALU.mult))
                    dve.tensor_tensor(ik[:], ik[:], ubuf[:], ALU.add).then_inc(roped, 1)
                elif kind in ROPED:
                    dst = {"iq": iq, "q": qT, "k": kT}[kind][:, m, :]
                    dve.wait_ge(rot_done, u + 1)
                    link(dve.tensor_tensor(ubuf[:], misc[:, 0, :], sinT[:], ALU.mult))
                    dve.wait_ge(cos_part, u)
                    dve.tensor_tensor(dst, dst, ubuf[:], ALU.add).then_inc(roped, 1)
                elif kind == "v":
                    dve.wait_ge(rot_done, u + 1)
                    dve.tensor_copy(vtok[:, :, m, :], tiles(misc[:, 0, :])).then_inc(roped, 1)

            def att_dve(q):
                if q < Q_ITEMS:
                    b, i = q // HEADS, q % 2
                    w = (b + 1) * P
                    dve.wait_ge(logit_mm, q + 1)
                    if q >= 2:
                        dve.wait_ge(exp_done, q - 1)
                    mask = score[:, b - 1, 0:w] if b else const["neg_future"]
                    link(dve.tensor_tensor_reduce(relu_s[:, i, 0:w], misc[:, i, 0:w], mask, HD ** -0.5,
                                                  NEG, ALU.add, ALU.max, amax[:, i:i + 1]))
                    dve.tensor_scalar(amax_n[:, i:i + 1], amax[:, i:i + 1], -1.0, None, ALU.mult).then_inc(masked, 1)
                if 1 <= q <= Q_ITEMS:
                    i, w = (q - 1) % 2, ((q - 1) // HEADS + 1) * P
                    dve.wait_ge(exp_done, q)
                    link(dve.reciprocal(arcp[:, i:i + 1], asum[:, i:i + 1]))
                    dve.tensor_scalar(probs[:, i, 0:w], probs[:, i, 0:w], arcp[:, i:i + 1], None, ALU.mult)\
                        .then_inc(probs_ready, 1)
                if q >= 2:
                    b, h = (q - 2) // HEADS, (q - 2) % HEADS
                    r = slice(HD * (h % 2), HD * (h % 2) + HD)
                    dve.wait_ge(pv_done, q - 1)
                    dve.tensor_copy(y_f[r, h // 2, b * P:(b + 1) * P], misc[r, 3, 0:P]).then_inc(y_taken, 1)

            def ev_finish(u, k):
                kind, m = EV_UNITS[u]
                bank = prod[:, 2 * ((EV_S + u) % 2), :]
                if k == 0:
                    dve.wait_ge(unit_done, EV_N + u + 1)
                    if u == 0:
                        dve.wait_ge(rstd_ready, 2)
                    if kind in ("ik", "iq", "k", "q", "v"):
                        if u >= 2:
                            dve.wait_ge(rot_done, u - 1)
                            dve.wait_ge(roped, u - 1)
                        dve.tensor_tensor(roped_in[:, u % 2, :], bank, rstd[:], ALU.mult).then_inc(evac, 1)
                    elif kind == "c":
                        dve.tensor_tensor(cbuf[:], bank, rstd[:], ALU.mult).then_inc(evac, 1)
                    elif kind == "x":
                        dve.tensor_tensor(ubuf[:], cbuf[:], bank, ALU.mult).then_inc(evac, 1)
                    else:
                        dve.tensor_tensor(act_f[:, m % 2, :], cbuf[:], bank, ALU.mult).then_inc(evac, 1)
                elif k == 1:
                    split(EV_N + u + 2)
                elif kind == "c" and k == 2:
                    dve.wait_ge(evac, EV_S + u + 1)
                    link(dve.tensor_tensor(cbuf[:], cbuf[:], rstd[:], ALU.mult))
                elif kind == "x" and k == 2:
                    dve.wait_ge(evac, EV_S + u + 1)
                    link(dve.tensor_scalar(cbuf[:], ubuf[:], ev_conv[:, m, 2:3], None, ALU.mult))
                elif kind == "x" and k in (4, 6):
                    j = k // 2 - 1
                    link(dve.scalar_tensor_tensor(cbuf[:, j:T], ubuf[:, 0:T - j], ev_conv[:, m, 2 - j:3 - j],
                                                  cbuf[:, j:T], ALU.mult, ALU.add))
                elif kind == "b" and k == 2:
                    dve.wait_ge(evac, EV_S + u + 1)
                    dve.tensor_tensor(act_f[:, m % 2, :], act_f[:, m % 2, :], rstd[:], ALU.mult).then_inc(y_conv, 1)
                elif kind == "b" and k == 5:
                    dve.wait_ge(emhi, m + 1)
                    dve.tensor_tensor(emix_lo[:, m, :], act_f[:, m % 2, :], emix_hi[:, m, :].bitcast(F32), ALU.subtract)\
                        .then_inc(emix_ready, 1)
                    dve.wait_ge(emix_ready, m + 1)
                elif k == 5:
                    ev_side_dve(u)

            for u in range(1, len(EV_UNITS) + 1):
                for k in range(KT):
                    for q in att_slots.get(u * KT + k, []):
                        att_dve(q)
                    ev_finish(u - 1, k)
                    ev_extra_dve([e for e in extras.get(u * KT + k - 1, []) if e[0] == "idx"])
                    ev_extra_dve([e for e in extras.get(u * KT + k, []) if e[0] == "top"])
            for m in range(4):
                dve.wait_ge(emhi, 5 + m)
                dve.tensor_tensor(emix_lo[:, 4 + m, :], y_f[:, m, :], emix_hi[:, 4 + m, :].bitcast(F32), ALU.subtract)\
                    .then_inc(emix_ready, 1)
            for m in range(KT):
                split(EVO_N + m + 2)
                residual(m, EVO_S + m, EVO_N + m + 1, 1.0)
                lo(2, m)
            ffn_dve(1)
            ffn_dve(2)

            def bc(ap):
                return ap.unsqueeze(1).broadcast_to([P, TT, HEADS])

            def prep_dve(j):
                if j == 4:
                    dve.wait_ge(ba_turned, 1)
                    dve.wait_ge(od_in, 16 * 4)
                    dve.tensor_copy(ba_tok[:], misc[:, 0, 0:TT * 16].rearrange("p (t c) -> p t c", t=TT))\
                        .then_inc(ba_tok_in, 1)
                    dve.wait_ge(ba_tok_in, 1)
                    link(dve.tensor_tensor(gt2[:], ba_tok[:, :, HEADS:2 * HEADS], bc(dtb[:]), ALU.add))
                    dve.scalar_tensor_tensor(gt1[:], gt2[:], -1.0, gt2[:], ALU.mult, ALU.max).then_inc(ba_tok_in, 1)
                    dve.wait_ge(ba_tok_in, 2)
                    link(dve.tensor_scalar(gt2[:], gt2[:], 0.0, None, ALU.max))
                    dve.wait_ge(gate_exp, 1)
                    link(dve.tensor_scalar(beta[:], beta[:], 1.0, None, ALU.add))
                    link(dve.reciprocal(beta[:], beta[:]))
                    dve.wait_ge(gate_exp, 2)
                    link(dve.tensor_tensor(gt2[:], gt2[:], gt1[:], ALU.add))
                    dve.scalar_tensor_tensor(g_tok[:], gt2[:], -1.0, bc(alog[:]), ALU.mult, ALU.mult)\
                        .then_inc(g_ready, 1)
                if j == 14:
                    dve.wait_ge(gcum_mm, 1)
                    dve.tensor_copy(g_cum[:].rearrange("p t h -> p (t h)"), misc[:, 1, 0:TT * HEADS])\
                        .then_inc(g_cum_in, 1)
                    dve.wait_ge(gate_exp, 3)
                    link(dve.tensor_tensor(beg[:], beg[:], beta[:], ALU.mult))

            M = [tiles(misc[:, i, :]) for i in range(4)]

            def col(t, g):
                return t[:, :, g:g + 1].broadcast_to([P, TT, P])

            def same(m):
                return m.unsqueeze(1).broadcast_to([P, TT, P])

            X = [tiles(prod[:, i, :]) for i in (1, 3)]

            def stage_dve(g, name):
                i = g % 2
                if name == "square":
                    if g == 0:
                        dve.wait_ge(g_ready, 1)
                    dve.tensor_copy(g_b[:], col(g_tok, g)).then_inc(gb_ready, 1)
                elif name == "decay":
                    dve.wait_ge(qk_rstd, g + 1)
                    dve.scalar_tensor_tensor(qc[:, g % 2, :], qc[:, g % 2, :], float(P ** -0.5), silu_g[:, 0, :],
                                             ALU.mult, ALU.mult)
                    dve.tensor_tensor(kn[:].rearrange("p t c -> p (t c)"), kc[:, g % 2, :], silu_g[:, 1, :], ALU.mult)\
                        .then_inc(qk_ready, 1)
                    dve.wait_ge(grow_mm, g + 1)
                    dve.wait_ge(e_row_ready, g + 1)
                    link(dve.tensor_tensor(a_mat[:], M[2], col(g_cum, g), ALU.subtract))
                    dve.tensor_scalar(dec_t[:], a_mat[:], 0.0, None, ALU.min)
                    dve.tensor_scalar(dec_a[:], a_mat[:], 0.0, None, ALU.max).then_inc(dif_ready, 1)
                elif name == "gram":
                    dve.wait_ge(gram_mm, g + 1)
                    dve.wait_ge(dec_ready, g + 1)
                    dve.tensor_tensor(a_mat[:], M[0], dec_a[:], ALU.mult).then_inc(a_made, 1)
                    dve.tensor_tensor(intra_t[:, i], M[1], dec_t[:], ALU.mult).then_inc(a_made, 1)
                    dve.tensor_tensor(v_beta[:, i], M[3], col(beta, g), ALU.mult).then_inc(a_made, 1)
                    dve.tensor_tensor(k_beg[:, i], M[2], col(beg, g), ALU.mult).then_inc(a_made, 1)
                    dve.tensor_tensor(k_dec[:, i], M[2], dec_t[:, :, P - 1:P].broadcast_to([P, TT, P]), ALU.mult)\
                        .then_inc(a_made, 1)
                elif name == "turn1":
                    dve.wait_ge(b_made, LEVELS * g + 1)
                    dve.tensor_tensor(t_inv[:], same(const["ident"]), b_lvl[:, 1], ALU.subtract).then_inc(tu_ready, 1)
                    dve.wait_ge(b1_turned, g + 1)
                    dve.tensor_tensor(u_inv[:, i], same(const["ident"]), M[0], ALU.subtract).then_inc(tu_ready, 1)
                elif name[0] == "t":
                    l = int(name[1:])
                    dve.wait_ge(t_mm, TM * g + 2 * l - 3)
                    dve.tensor_tensor(u_inv[:, i], u_inv[:, i], M[2], ALU.subtract).then_inc(tu_ready, 1)
                    if l < LEVELS:
                        dve.wait_ge(t_mm, TM * g + 2 * l - 2)
                        dve.tensor_tensor(t_inv[:], t_inv[:], M[1], ALU.subtract).then_inc(tu_ready, 1)
                elif name[:3] == "new":
                    t = int(name[3:])
                    dve.wait_ge(vnew_mm, TT * g + t + 1)
                    dve.tensor_copy(v_new[:, t % 2, :], X[1][:, t, :]).then_inc(vnew_ready, 1)
                elif name[:3] == "out" and name != f"out{TT - 1}":
                    t = int(name[3:])
                    dve.wait_ge(state_mm, (TT - 1) * g + t + 1)
                    if t == 0:
                        dve.tensor_copy(state[:, 1, :], X[1][:, t, :]).then_inc(state_ready, 1)
                    else:
                        dve.wait_ge(state_ready, (TT - 1) * g + t)
                        dve.scalar_tensor_tensor(state[:, (t + 1) % 2, :], state[:, t % 2, :], e_row[:, i, t, P - 1:P],
                                                 X[1][:, t, :], ALU.mult, ALU.add).then_inc(state_ready, 1)
                elif name == "fin":
                    dve.wait_ge(o_rstd, g + 1)
                    dve.scalar_tensor_tensor(o_n[:, g, :], prod[:, 1, :], o_gain[:], act_f[:, 1, :], ALU.mult, ALU.mult)\
                        .then_inc(on_ready, 1)

            def od_finish(u, k):
                kind, h = OD_UNITS[u]
                bank = prod[:, 2 * ((OD_S + u) % 2), :]
                if k == 0:
                    dve.wait_ge(unit_done, OD_N + u + 1)
                    if u == 0:
                        dve.wait_ge(rstd_ready, 5)
                        dve.wait_ge(od_in, 16 * 4)
                    dst = {"ba": hf[:, 0, :], "z": hf[:, h % 2, :]}.get(kind, pre)
                    dve.tensor_tensor(dst, bank, rstd[:], ALU.mult).then_inc(evac, 1)
                elif k == 1:
                    split(OD_N + u + 2)
                elif kind == "z" and k == 4:
                    dve.wait_ge(act_done, 3 * HEADS + h + 1)
                    dve.wait_ge(on_ready, h + 1)
                    dve.tensor_tensor(act_f[:, 0, :], hf[:, h % 2, :], o_n[:, h, :], ALU.mult).then_inc(gated, 1)
                elif kind == "z" and k == 7:
                    dve.wait_ge(ohi, h + 1)
                    dve.tensor_tensor(omix_lo[:, h, :], act_f[:, 0, :], omix_hi[:, h, :].bitcast(F32), ALU.subtract)\
                        .then_inc(omix_ready, 1)
                    dve.wait_ge(omix_ready, h + 1)
                elif kind in "qkv" and 2 <= k <= 4:
                    dst = {"q": qc, "k": kc, "v": vc}[kind][:, h % 2, :]
                    c = "qkv".index(kind) * HEADS + h
                    if k == 2:
                        dve.wait_ge(evac, OD_S + u + 1)
                        link(dve.tensor_scalar(dst, pre, od_conv[:, c, 3:4], None, ALU.mult))
                    j = k - 1
                    ins = dve.scalar_tensor_tensor(dst[:, j:T], pre[:, 0:T - j], od_conv[:, c, 3 - j:4 - j],
                                                   dst[:, j:T], ALU.mult, ALU.add)
                    if j < 3:
                        link(ins)
                    else:
                        ins.then_inc(conv_done, 1)
                        dve.wait_ge(conv_done, u)

            for u in range(1, len(OD_UNITS) + 1):
                for k in range(KT):
                    slot = (u - 1) * KT + k
                    prep_dve(slot)
                    for g, name in od_slots.get(slot, []):
                        stage_dve(g, name)
                    od_finish(u - 1, k)
            for m in range(KT):
                split(ODO_N + m + 2)
                residual(m, ODO_S + m, ODO_N + m + 1, 1.0)
                lo(5, m)
            ffn_dve(3)
            dve.wait_ge(rstd_ready, 7)
            for k in range(KT):
                dve.scalar_tensor_tensor(y_out[:, k, :], x[:, k, :], gains[:, 6, k:k + 1], rstd[:], ALU.mult, ALU.mult)\
                    .then_inc(y_made, 1)

        @block.gpsimd
        def _(pool):
            def same(m):
                return m.unsqueeze(1).broadcast_to([P, TT, P])

            def add_squares(r):
                for m in range(1, 7):
                    pool.wait_ge(sq_ready, 8 * r + m + 1)
                    a = sq[:, 0, :] if m == 1 else sq_acc[:]
                    if m == 1 and r:
                        pool.wait_ge(sum_done, r)
                    pool.tensor_tensor(sq_acc[:], a, sq[:, m % 2, :], ALU.add).then_inc(acc_done, 1)
                    pool.wait_ge(acc_done, 6 * r + m)

            add_squares(0)
            add_squares(1)
            pool.wait_ge(trig_ready, 2)
            for u, (kind, m) in enumerate(EV_UNITS):
                if kind in ROPED:
                    dst = {"iq": iq, "q": qT, "k": kT}[kind][:, m, :]
                    pool.wait_ge(evac, EV_S + u + 1)
                    pool.tensor_tensor(dst, roped_in[:, u % 2, :], cosT[:], ALU.mult).then_inc(cos_part, 1)
            for r in (2, 3, 4):
                add_squares(r)
            for g in range(HEADS):
                pool.wait_ge(dec_exp, g + 1)
                pool.tensor_tensor(dec_t[:], dec_t[:], same(const["tri"]), ALU.mult)
                pool.tensor_tensor(dec_a[:], dec_a[:], beta[:, :, g:g + 1].broadcast_to([P, TT, P]), ALU.mult)\
                    .then_inc(dec_ready, 1)
                pool.wait_ge(qk_ready, g + 1)
                for l in range(1, LEVELS + 1):
                    if l == 1:
                        pool.wait_ge(a_made, 5 * g + 1)
                    if l >= 3:
                        if l == 3:
                            pool.wait_ge(tu_ready, TU * g + 2)
                        else:
                            pool.wait_ge(y_mm, (LEVELS - 1) * g + l - 3)
                    pool.tensor_tensor(b_lvl[:, l % 2], a_mat[:], same(const[f"level{l}"]), ALU.mult).then_inc(b_made, 1)
                    if l == 1:
                        pool.tensor_tensor(q_dec[:, g % 2].rearrange("p t c -> p (t c)"), qc[:, g % 2, :],
                                           e_row[:, g % 2].rearrange("p t c -> p (t c)"), ALU.mult).then_inc(qdec_ready, 1)
            for r in (5, 6):
                add_squares(r)


def shape_constants():
    i, j = np.indices((P, P))
    rot = np.zeros((P, P), np.float32)
    half = HD // 8
    for m in range(P):
        if m % HD < half:
            rot[m + half, m] = -1.0
        elif m % HD < 2 * half:
            rot[m - half, m] = 1.0
    c = {
        "ident": i == j, "ones": np.ones((P, P)), "tri": i <= j, "neg_future": np.where(j > i, NEG, 0.0),
        "rot": rot, "dup": (i == j % HD) & (i < HD),
        "dup_rot": np.where(i < HD, np.tile(rot[:, :HD], (1, 2)), 0.0),
    }
    for l in range(1, LEVELS + 1):
        s = 2 ** (l - 1)
        c[f"level{l}"] = (i // (2 * s) == j // (2 * s)) & (i // s % 2 == 1) & (j // s % 2 == 0)
    return np.ascontiguousarray(np.stack([np.asarray(c[n], np.float32) for n in CONSTS], axis=1))


def rope_frequencies():
    f = np.float32(500000.0) ** (-np.arange(0, HD // 4, 2, dtype=np.float32) / np.float32(HD // 4))
    row = np.arange(P) % HD
    return np.where(row < HD // 4, f[row % (HD // 8)], 0.0).astype(np.float32)[:, None]


def kernel(x, positions, norm_gain, ffn_w_gate, ffn_w_up, ffn_w_down, ev_w_in, ev_conv_w, ev_w_out,
           od_w_in, od_conv_w, od_a_log, od_dt_bias, od_o_gain, od_w_out, final_gain):
    import concourse.bacc as bacc
    from concourse.bass_utils import run_bass_kernel_spmd

    (x, positions, norm_gain, ffn_w_gate, ffn_w_up, ffn_w_down, ev_w_in, ev_conv_w, ev_w_out, od_w_in, od_conv_w,
     od_a_log, od_dt_bias, od_o_gain, od_w_out, final_gain) = (np.asarray(a) for a in (
         x, positions, norm_gain, ffn_w_gate, ffn_w_up, ffn_w_down, ev_w_in, ev_conv_w, ev_w_out, od_w_in, od_conv_w,
         od_a_log, od_dt_bias, od_o_gain, od_w_out, final_gain))

    def unit(w, cols):
        u = np.zeros((w.shape[0] // P, P, P), w.dtype)
        at = 0
        for lo, n in cols:
            u[:, :, at:at + n] = w[:, lo:lo + n].reshape(-1, P, n)
            at += n
        return u.transpose(1, 0, 2).reshape(P, -1)

    w8 = np.empty((ROWS8, P, KT * P), x.dtype)
    wd = np.empty((NFFN * 2 * KT, P, HALF * P), x.dtype)
    for f in range(NFFN):
        gate, up, down = (w[f // 2, f % 2] for w in (ffn_w_gate, ffn_w_up, ffn_w_down))
        for j in range(FT):
            w8[GU_ROW[f] + 2 * j] = unit(gate, [(j * P, P)])
            w8[GU_ROW[f] + 2 * j + 1] = unit(up, [(j * P, P)])
        for m in range(KT):
            for half in range(2):
                wd[f * 2 * KT + 2 * m + half] = unit(down[half * HALF * P:(half + 1) * HALF * P], [(m * P, P)])
    at = {"b": 0, "c": T, "x": 2 * T, "q": 3 * T, "k": 4 * T, "v": 5 * T, "iq": 6 * T}
    for u, (kind, m) in enumerate(EV_UNITS):
        w8[EV0 + u] = unit(ev_w_in[0], [(7 * T, HD + HEADS)] if kind == "ik" else [(at[kind] + m * P, P)])
    at = {"q": 0, "k": D, "v": 2 * D, "z": 3 * D}
    for u, (kind, h) in enumerate(OD_UNITS):
        w8[OD0 + u] = unit(od_w_in[0], [(4 * D, 2 * HEADS)] if kind == "ba" else [(at[kind] + h * P, P)])
    for m in range(KT):
        w8[EVO0 + m] = unit(ev_w_out[0], [(m * P, P)])
        w8[ODO0 + m] = unit(od_w_out[0], [(m * P, P)])
    gains = np.concatenate([norm_gain.reshape(6, KT, P), final_gain.reshape(1, KT, P)]).transpose(2, 0, 1)

    inputs = {
        "x": x.reshape(T, D), "pos": positions.reshape(1, T), "w8": w8, "wd": wd, "gains": gains,
        "consts": shape_constants(), "eps": np.full((P, 1), EPS, np.float32), "freq": rope_frequencies(),
        "ev_conv": ev_conv_w[0].reshape(3, 4, P).transpose(2, 1, 0),
        "od_conv": od_conv_w[0].reshape(4, 3 * HEADS, P).transpose(2, 1, 0),
        "alog": od_a_log.reshape(1, HEADS), "dtb": od_dt_bias.reshape(1, HEADS), "o_gain": od_o_gain.reshape(P, 1),
    }
    nc = bacc.Bacc("TRN2", target_bir_lowering=False, num_devices=1)
    arrays, aps = {}, {}
    for name, a in inputs.items():
        arrays[f"in_{name}"] = np.ascontiguousarray(a)
        aps[name] = nc.dram_tensor(f"in_{name}", a.shape, mybir.dt.from_np(a.dtype), kind="ExternalInput").ap()
    out = nc.dram_tensor("out", (T, D), F32, kind="ExternalOutput").ap()
    program(nc, aps, out)
    got = run_bass_kernel_spmd(nc, [arrays], core_ids=[0]).results[0]["out"]
    return got.reshape(1, T, D)
```

```python
from contextlib import ExitStack

import numpy as np

import concourse.bass as bass
from concourse import mybir

F32 = mybir.dt.float32
F32R = mybir.dt.float32r
I32 = mybir.dt.int32
ALU = mybir.AluOpType
ACT = mybir.ActivationFunctionType

P = 128
D = 1024
T = 512
KT = D // P
TT = T // P
DFF = 2816
FT = DFF // P
HALF = FT // 2
NFFN = 4
EPS = 1e-6
HEADS = 8
HD = 64
TOPK = T // 4
ROUNDS = TOPK // 8
LEVELS = 7
NEG = -3.0e38
MARK = -3.3e38
SPLIT = -3.15e38

EV_UNITS = [("ik", 0)] + [("iq", m) for m in range(4)] + [("k", m) for m in range(4)] + [("q", m) for m in range(4)] \
    + [("v", m) for m in range(4)] + [(w, m) for m in range(4) for w in "cxb"]
OD_UNITS = [("ba", 0)] + [(w, h) for h in range(HEADS) for w in "qkv"] + [("z", h) for h in range(HEADS)]
ROPED = ("iq", "k", "q")

FFN_UNITS, FFN_STEPS = 2 * FT + 2 * KT, FT + KT
EV_N, EV_S = FFN_UNITS, FFN_STEPS
EVO_N, EVO_S = EV_N + len(EV_UNITS), EV_S + len(EV_UNITS)
F1_N, F1_S = EVO_N + KT, EVO_S + KT
F2_N, F2_S = F1_N + FFN_UNITS, F1_S + FFN_STEPS
OD_N, OD_S = F2_N + FFN_UNITS, F2_S + FFN_STEPS
ODO_N, ODO_S = OD_N + len(OD_UNITS), OD_S + len(OD_UNITS)
F3_N, F3_S = ODO_N + KT, ODO_S + KT
FFN_AT = [(0, 0), (F1_N, F1_S), (F2_N, F2_S), (F3_N, F3_S)]
N_END = F3_N + FFN_UNITS
GU0, EV0 = 0, 2 * FT
EVO0 = EV0 + len(EV_UNITS)
GU1 = EVO0 + KT
GU2 = GU1 + 2 * FT
OD0 = GU2 + 2 * FT
ODO0 = OD0 + len(OD_UNITS)
GU3 = ODO0 + KT
GU_ROW = [GU0, GU1, GU2, GU3]
ROWS8 = GU3 + 2 * FT

CONSTS = ["ident", "ones", "tri", "neg_future", "rot", "dup", "dup_rot"] + [f"level{l}" for l in range(1, LEVELS + 1)]


def unit_width(n):
    for n0, _ in FFN_AT:
        if n0 + 2 * FT <= n < n0 + FFN_UNITS:
            return HALF * P
    return KT * P


def ev_extras():
    idx = [("idx", b, h) for b in range(1, TT) for h in range(HEADS)]
    top = [("top", b, r) for b in range(1, TT) for r in range(ROUNDS)]
    out = {}
    for u in range(len(EV_UNITS)):
        for k in (1, 4, 6):
            if u >= 6 and idx:
                out[u * KT + k] = [idx.pop(0)]
        for k in (2, 5, 7):
            if u >= 9 and top:
                out[u * KT + k] = [top.pop(0)]
    assert not idx and not top
    return out


POOL_UNIT = 14

ATT_SLOT = 17 * KT + 6
ATT_STEPS = {"logits": 0, "scale": 2, "turn": 4, "values": 6}


def attention_slots():
    slots = len(EV_UNITS) * KT - ATT_SLOT - max(ATT_STEPS.values())
    out = {}
    for q in range(Q_ITEMS):
        for step, at in ATT_STEPS.items():
            out.setdefault(ATT_SLOT + q * slots // Q_ITEMS + at, []).append((step, q))
    for steps in out.values():
        steps.sort(key=lambda e: e[1])
    return out


CHAIN1 = {"spread": -17, "decay": -13, "mask": -11, "squareq": -12, "normq": -9, "scaleq": -6,
          "squarek": -4, "normk": -3, "scalek": 0, "gram": 4, "turn1": 7}
CHAIN1.update({"y2": 11, "t2": 13, "y3": 15, "t3": 17, "y4": 18, "t4": 20, "y5": 21, "t5": 22, "y6": 24, "t6": 25,
               "y7": 26, "t7": 27})
CHAIN2 = {"w": 9, "new0": 11, "out0": 13, "new1": 15, "out1": 17, "new2": 19, "out2": 21, "new3": 23, "out3": 25,
          "osquare": 26, "osum": 29, "fin": 33}
TAP_SLOTS = (2, 3, 4, 6)
FIRST = 4


def delta_slots():
    per = 3 * KT
    out = {}
    for g in range(HEADS):
        for behind, chain in ((2, CHAIN2), (1, CHAIN1)):
            for name, at in chain.items():
                out.setdefault(per * (g + behind) + FIRST + at, []).append((g, name))
    for stages in out.values():
        stages.sort(key=lambda e: e[0])
    assert max(out) < 4 * HEADS * KT
    return out


TU = 2 * LEVELS - 1
TM = 2 * (LEVELS - 1) - 1
N_SIDE = 17
Q_ITEMS = TT * HEADS


def norm_of(f):
    return (0, 2, 3, 5)[f]


def half_blocks(m, level, odd):
    s = 2 ** (level - 1)
    if len(m.shape) == 2:
        return m.rearrange("p (b o s) -> p b o s", o=2, s=s)[:, :, odd, :]
    return m.rearrange("p t (b o s) -> p (t b) o s", o=2, s=s)[:, :, odd, :]


def pi_parts(value, count, bits=7):
    parts = []
    for _ in range(count):
        scale = 2.0 ** (np.floor(np.log2(value)) - bits + 1)
        parts.append(float(np.floor(value / scale) * scale))
        value -= parts[-1]
    return parts


def program(nc, A, out):
    with ExitStack() as ctx:
        def sem(name):
            return ctx.enter_context(nc.semaphore(name))

        def sb(name, shape, dt=F32):
            return nc.alloc_sbuf_tensor(name, [P] + shape, dt)

        x = sb("x", [KT, T])
        h_at = (nc.sbuf_base + 31) // 32 * 32
        h_hi, h_lo = sb("h_hi", [KT, T], F32R), sb("h_lo", [KT, T], F32R)
        y_feat = nc.alloc_sbuf_tensor_at("y_feat", [P, KT, T], F32, offset=h_at)
        y_rows = nc.alloc_sbuf_tensor_at("y_rows", [P, TT, D], F32, offset=h_at + KT * T * 4)
        rstd_row = sb("rstd_row", [TT])
        raw = sb("raw", [4, HALF * P])
        w_hi, w_lo = sb("w_hi", [2, HALF * P], F32R), sb("w_lo", [2, HALF * P], F32R)
        consts = sb("consts", [len(CONSTS), P])
        gains = sb("gains", [7, KT])
        freq = sb("freq", [1])
        eps, warm = sb("eps", [1]), sb("warm", [1])
        silu_g = sb("silu_g", [2, T])
        act_f = sb("act_f", [2, T])
        sq = sb("sq", [2, T])
        sq_acc = sb("sq_acc", [T])
        rstd = sb("rstd", [T])
        hf = sb("hf", [2, T])
        const = {name: consts[:, i, :] for i, name in enumerate(CONSTS)}

        region = nc.sbuf_base
        region0 = (region + 31) // 32 * 32
        region_end = nc.sbuf_usable_end

        class Plan:
            def __init__(self):
                self.at = region0

            def __call__(self, name, shape, dt=F32):
                t = nc.alloc_sbuf_tensor_at(name, [P] + shape, dt, offset=self.at)
                self.at += int(np.prod(shape)) * 4
                self.at = (self.at + 31) // 32 * 32
                assert self.at <= region_end, (name, self.at, region_end)
                return t

        io = Plan()
        x_rows = io("x_rows", [TT, D])
        ffn = Plan()
        a_hi, a_lo = ffn("a_hi", [FT, T], F32R), ffn("a_lo", [FT, T], F32R)

        ev = Plan()
        emix_hi, emix_lo = ev("emix_hi", [KT, T], F32R), ev("emix_lo", [KT, T], F32R)
        iq, qT, kT = ev("iq", [4, T]), ev("qT", [4, T]), ev("kT", [4, T])
        ik = ev("ik", [T])
        vtok = ev("vtok", [TT, 4, P])
        y_f = iq
        cosT, sinT = ev("cosT", [T]), ev("sinT", [T])
        roped_in = hf
        cbuf, ubuf = ev("cbuf", [T]), ev("ubuf", [T])
        score = ev("score", [TT - 1, T])
        relu_s = ev("relu_s", [2, T])
        probs = silu_g
        probsT = ev("probsT", [2, TT, P])
        w_idx = ev("w_idx", [TT, HEADS])
        top8 = ev("top8", [8])
        amax, asum = ev("amax", [2]), ev("asum", [2])
        amax_n, arcp = ev("amax_n", [2]), ev("arcp", [2])
        ev_conv = ev("ev_conv", [4, 3])

        od = Plan()
        omix_hi, omix_lo = od("omix_hi", [KT, T], F32R), od("omix_lo", [KT, T], F32R)
        o_n = nc.alloc_sbuf_tensor_at("o_n", [P, KT, T], F32, offset=region0 + KT * T * 4)
        qc, kc, vc = (od(n, [2, T]) for n in ("qc", "kc", "vc"))
        kn = od("kn", [TT, P])
        g_b = kn
        e_row = od("e_row", [TT, P])
        dec_t, dec_a = od("dec_t", [TT, P]), od("dec_a", [TT, P])
        a_mat = od("a_mat", [TT, P])
        b_lvl = od("b_lvl", [2, TT, P])
        t_inv = od("t_inv", [TT, P])
        y_lvl = od("y_lvl", [TT, P])
        u_inv, intra_t = (od(n, [2, TT, P]) for n in ("u_inv", "intra_t"))
        e_last = od("e_last", [2, TT, 1])
        v_beta, k_beg, k_dec = (od(n, [2, TT, P]) for n in ("v_beta", "k_beg", "k_dec"))
        q_dec = nc.alloc_sbuf_tensor_at("q_dec", [P, 2, TT, P], F32, offset=region0 + 5 * T * 4)
        neg_w = nc.alloc_sbuf_tensor_at("neg_w", [P, TT, P], F32, offset=region0 + 7 * T * 4)
        pre = hf[:, 1, :]
        state, v_new = od("state", [2, P]), od("v_new", [2, P])
        g_tok, g_cum = od("g_tok", [TT, HEADS]), od("g_cum", [TT, HEADS])
        beta, beg = od("beta", [TT, HEADS]), od("beg", [TT, HEADS])
        ba_tok = od("ba_tok", [TT, 2 * HEADS])
        gt1, gt2 = od("gt1", [TT, HEADS]), od("gt2", [TT, HEADS])
        alog, dtb = od("alog", [HEADS]), od("dtb", [HEADS])
        od_conv = od("od_conv", [3 * HEADS, 4])
        o_gain = od("o_gain", [1])

        prod = nc.alloc_psum_tensor("prod", [P, 4, T], F32)
        misc = nc.alloc_psum_tensor("misc", [P, 4, T], F32)

        def tiles(ap):
            return ap.rearrange("p (t c) -> p t c", t=TT)

        setup_in, consts_in = sem("setup_in"), sem("consts_in")
        raw_in = [sem(f"raw_in{i}") for i in range(4)]
        hi_ready, lo_ready, unit_done, evac = sem("hi_ready"), sem("lo_ready"), sem("unit_done"), sem("evac")
        x_turned, x_in = sem("x_turned"), sem("x_in")
        sq_ready, acc_done, sum_done, rstd_ready = sem("sq_ready"), sem("acc_done"), sem("sum_done"), sem("rstd_ready")
        hhi_ready, h_ready, y_made = sem("hhi_ready"), sem("h_ready"), sem("y_made")
        gate_scaled, silu_done, a_scaled = sem("gate_scaled"), sem("silu_done"), sem("a_scaled")
        ahi_ready, a_ready = sem("ahi_ready"), sem("a_ready")
        act_seq, dve_seq = sem("act_seq"), sem("dve_seq")
        ev_in, conv_in, od_in = sem("ev_in"), sem("conv_in"), sem("od_in")
        ang_ready, trig_ready = sem("ang_ready"), sem("trig_ready")
        rot_done, cos_part, roped = sem("rot_done"), sem("cos_part"), sem("roped")
        idx_mm, relu_done, idx_added = sem("idx_mm"), sem("relu_done"), sem("idx_added")
        y_conv, emhi, emix_ready = sem("y_conv"), sem("emhi"), sem("emix_ready")
        logit_mm, masked, exp_done = sem("logit_mm"), sem("masked"), sem("exp_done")
        arcp_ready, probs_ready = sem("arcp_ready"), sem("probs_ready")
        turned, probsT_ready, pv_done, y_taken = sem("turned"), sem("probsT_ready"), sem("pv_done"), sem("y_taken")
        conv_done, act_done, state_mm = sem("conv_done"), sem("act_done"), sem("state_mm")
        ba_turned, ba_tok_in, gate_exp = sem("ba_turned"), sem("ba_tok_in"), sem("gate_exp")
        g_ready, gcum_mm, g_cum_in = sem("g_ready"), sem("gcum_mm"), sem("g_cum_in")
        qk_sq, qk_sum, qk_rstd, qk_ready = sem("qk_sq"), sem("qk_sum"), sem("qk_rstd"), sem("qk_ready")
        gb_ready, grow_mm, dif_ready, dec_exp = sem("gb_ready"), sem("grow_mm"), sem("dif_ready"), sem("dec_exp")
        dec_ready, kk_mm, gram_mm, a_made = sem("dec_ready"), sem("kk_mm"), sem("gram_mm"), sem("a_made")
        b_made, b1_turned, tu_ready = sem("b_made"), sem("b1_turned"), sem("tu_ready")
        y_mm, y_ready, t_mm = sem("y_mm"), sem("y_ready"), sem("t_mm")
        w_mm, w_ready = sem("w_mm"), sem("w_ready")
        vnew_mm, vnew_ready, out_mm, state_ready = sem("vnew_mm"), sem("vnew_ready"), sem("out_mm"), sem("state_ready")
        o_sq, o_sum, o_rstd, on_ready = (sem(n) for n in ("o_sq", "o_sum", "o_rstd", "on_ready"))
        gated, ohi, omix_ready = sem("gated"), sem("ohi"), sem("omix_ready")
        qdec_ready, e_row_ready = sem("qdec_ready"), sem("e_row_ready")
        y_turned, y_rows_in, stored = sem("y_turned"), sem("y_rows_in"), sem("stored")
        y_scaled_v, y_scaled_s = sem("y_scaled_v"), sem("y_scaled_s")
        SETUP = 4

        block = ctx.enter_context(nc.Block())
        extras = ev_extras()
        att_slots = attention_slots()
        od_slots = delta_slots()

        @block.sync
        def _(sp):
            def load(n, src, i=0):
                if n >= 4:
                    sp.wait_ge(lo_ready, n - 3 + 4 * i)
                sp.dma_start(raw[:, n % 4, 0:unit_width(n)], src).then_inc(raw_in[n % 4], 16)

            def ffn_loads(f, first=0):
                n0, row0 = FFN_AT[f][0], GU_ROW[f]
                for u in range(first, 4):
                    load(n0 + u, A["w8"][row0 + u])
                with sp.Fori(1, 2 * FT // 4) as i:
                    for u in range(4):
                        row = i * 4 + (row0 + u)
                        sp.wait_ge(lo_ready, i * 4 + (n0 + u - 3))
                        sp.dma_start(raw[:, (n0 + u) % 4, 0:KT * P],
                                     A["w8"][bass.ds(row, 1)].rearrange("a p c -> (a p) c")).then_inc(raw_in[(n0 + u) % 4], 16)
                with sp.Fori(0, 2 * KT // 4) as i:
                    for u in range(4):
                        n = n0 + 2 * FT + u
                        row = i * 4 + (f * 2 * KT + u)
                        sp.wait_ge(lo_ready, i * 4 + (n - 3))
                        sp.dma_start(raw[:, n % 4, :],
                                     A["wd"][bass.ds(row, 1)].rearrange("a p c -> (a p) c")).then_inc(raw_in[n % 4], 16)

            sp.dma_start(const["ident"], A["consts"][:, 0, :]).then_inc(setup_in, 16)
            sp.dma_start(x_rows[:], A["x"].rearrange("(t p) d -> p t d", p=P)).then_inc(setup_in, 16)
            sp.dma_start(gains[:], A["gains"]).then_inc(setup_in, 16)
            sp.dma_start(eps[:], A["eps"]).then_inc(setup_in, 16)
            for u in range(4):
                load(u, A["w8"][GU_ROW[0] + u])
                if u == 1:
                    sp.dma_start(consts[:, 1:, :], A["consts"][:, 1:, :]).then_inc(consts_in, 16)
            sp.dma_start(freq[:], A["freq"]).then_inc(ev_in, 16)
            sp.dma_start(hf[:, 1, :].bitcast(I32), A["pos"].broadcast_to([P, T])).then_inc(ev_in, 16)
            ffn_loads(0, 4)
            for u in range(4):
                load(EV_N + u, A["w8"][EV0 + u])
            sp.wait_ge(evac, FFN_STEPS)
            sp.dma_start(ev_conv[:], A["ev_conv"]).then_inc(conv_in, 16)
            for u in range(4, len(EV_UNITS) + KT):
                load(EV_N + u, A["w8"][EV0 + u])
            ffn_loads(1)
            ffn_loads(2)
            for u in range(4):
                load(OD_N + u, A["w8"][OD0 + u])
            sp.wait_ge(evac, OD_S)
            sp.dma_start(alog[:], A["alog"].broadcast_to([P, HEADS])).then_inc(od_in, 16)
            sp.dma_start(dtb[:], A["dtb"].broadcast_to([P, HEADS])).then_inc(od_in, 16)
            sp.dma_start(od_conv[:], A["od_conv"]).then_inc(od_in, 16)
            sp.dma_start(o_gain[:], A["o_gain"]).then_inc(od_in, 16)
            for u in range(4, len(OD_UNITS) + KT):
                load(OD_N + u, A["w8"][OD0 + u])
            ffn_loads(3)
            for i in range(TT // 2):
                for t, scaled in ((i, y_scaled_v), (TT // 2 + i, y_scaled_s)):
                    sp.wait_ge(scaled, i + 1)
                    sp.dma_start(out[t * P:(t + 1) * P, :], y_rows[:, t, :]).then_inc(stored, 16)
            sp.wait_ge(stored, 16 * TT)

        @block.tensor
        def _(pe):
            def unit(n, bank, k0, acts, first, last, i=0, between=None, wait_k=None):
                pe.wait_ge(lo_ready, n + 1 + 4 * i)
                tiles_n = unit_width(n) // P
                for k in range(tiles_n):
                    if wait_k is not None:
                        wait_k(k)
                    hi, lo = acts(k0 + k)
                    wh = w_hi[:, n % 2, k * P:(k + 1) * P]
                    wl = w_lo[:, n % 2, k * P:(k + 1) * P]
                    pe.matmul(bank, wh, hi, start=first and k == 0, stop=False)
                    pe.matmul(bank, wh, lo, start=False, stop=False)
                    ins = pe.matmul(bank, wl, hi, start=False, stop=last and k == tiles_n - 1)
                    if k == tiles_n - 1:
                        ins.then_inc(unit_done, 1)
                    if between is not None:
                        between(k)

            def h_act(k):
                return h_hi[:, k, :], h_lo[:, k, :]

            def a_act(k):
                return a_hi[:, k, :], a_lo[:, k, :]

            def bank_free(s, i=0):
                if not isinstance(i, int):
                    pe.wait_ge(evac, i * 2 + (s - 1))
                elif s >= 2:
                    pe.wait_ge(evac, s - 1)

            def square_sum(r):
                if r == 0:
                    pe.wait_ge(consts_in, 16)
                pe.wait_ge(acc_done, 6 * (r + 1))
                pe.matmul(misc[:, 0, :], const["ones"], sq_acc[:], start=True, stop=False)
                pe.wait_ge(sq_ready, 8 * (r + 1))
                pe.matmul(misc[:, 0, :], const["ones"], sq[:, 1, :], start=False, stop=True).then_inc(sum_done, 1)

            def first_unit(r, n, bank):
                unit(n, bank, 0, h_act, True, True, wait_k=lambda k: pe.wait_ge(h_ready, 8 * r + k + 1),
                     between=lambda k: square_sum(r) if k == KT - 1 else None)

            def turn_y(m):
                pe.wait_ge(y_made, m + 1)
                if m >= 3:
                    pe.wait_ge(y_rows_in, m - 2)
                for t in range(TT):
                    ins = pe.transpose(misc[:, 1 + m % 3, t * P:(t + 1) * P], y_feat[:, m, t * P:(t + 1) * P],
                                       const["ident"])
                ins.then_inc(y_turned, 1)

            def ffn_pe(f):
                n0, s0 = FFN_AT[f]

                def pairs(i, first):
                    for u in range(4):
                        s = s0 + u // 2
                        if u % 2 == 0:
                            bank_free(s, i)
                        bank = prod[:, 2 * (s % 2) + u % 2, :]
                        if first and u == 0:
                            first_unit(norm_of(f), n0, bank)
                        else:
                            unit(n0 + u, bank, 0, h_act, True, True, i)

                pairs(0, True)
                with pe.Fori(1, FT // 2) as i:
                    pairs(i, False)
                for m in range(KT):
                    s = s0 + FT + m
                    bank_free(s)
                    for half in range(2):
                        if f == NFFN - 1 and m >= 2 and half == 1:
                            turn_y(m - 2)
                        unit(n0 + 2 * FT + 2 * m + half, prod[:, 2 * (s % 2), :], half * HALF, a_act,
                             half == 0, half == 1,
                             wait_k=(lambda k, half=half: pe.wait_ge(a_ready, FT * f + half * HALF + k + 1))
                             if m == 0 else None)

            def out_pe(n0, s0, acts, wait_k):
                for m in range(KT):
                    bank_free(s0 + m)
                    unit(n0 + m, prod[:, 2 * ((s0 + m) % 2), :], 0, acts, True, True,
                         wait_k=wait_k if m == 0 else None)

            pe.wait_ge(setup_in, 16 * SETUP)
            for k in range(KT):
                if k >= 4:
                    pe.wait_ge(x_in, k - 3)
                for t in range(TT):
                    ins = pe.transpose(prod[:, k % 4, t * P:(t + 1) * P], x_rows[:, t, k * P:(k + 1) * P], const["ident"])
                ins.then_inc(x_turned, 1)
            pe.wait_ge(x_in, KT)
            ffn_pe(0)

            def idx_pe(b, h):
                q = (b - 1) * HEADS + h
                if b == 1 and h == 0:
                    pe.wait_ge(roped, 5)
                if q >= 2:
                    pe.wait_ge(relu_done, q - 1)
                r = slice(HD * (h % 2), HD * (h % 2) + HD)
                w = (b + 1) * P
                pe.matmul(prod[:, 1 + 2 * (q % 2), 0:w], iq[r, h // 2, b * P:(b + 1) * P], ik[r, 0:w],
                          start=True, stop=True).then_inc(idx_mm, 1)

            def ev_extra_pe(slot):
                for kind, b, j in extras.get(slot, []):
                    if kind == "idx":
                        idx_pe(b, j)

            def ev_side_pe(u):
                kind, m = EV_UNITS[u]
                if kind == "ik":
                    pe.wait_ge(evac, EV_S + 1)
                    pe.wait_ge(rstd_ready, 2)
                    pe.matmul(misc[:, 0, :], const["dup"], roped_in[:, 0, :], start=True, stop=True)
                    pe.matmul(misc[:, 1, :], const["dup_rot"], roped_in[:, 0, :], start=True, stop=True)
                    for t in range(TT):
                        ins = pe.matmul(misc[:, 2, t * HEADS:(t + 1) * HEADS], roped_in[:, 0, t * P:(t + 1) * P],
                                        const["ident"][:, HD:HD + HEADS], start=True, stop=True)
                    ins.then_inc(rot_done, 1)
                elif kind in ROPED:
                    pe.wait_ge(evac, EV_S + u + 1)
                    pe.wait_ge(roped, u)
                    pe.matmul(misc[:, 0, :], const["rot"], roped_in[:, u % 2, :], start=True, stop=True)\
                        .then_inc(rot_done, 1)
                elif kind == "v":
                    pe.wait_ge(evac, EV_S + u + 1)
                    pe.wait_ge(roped, u)
                    for t in range(TT):
                        ins = pe.transpose(misc[:, 0, t * P:(t + 1) * P], roped_in[:, u % 2, t * P:(t + 1) * P],
                                           const["ident"])
                    ins.then_inc(rot_done, 1)

            def att(q):
                return q // HEADS, q % HEADS, slice(HD * (q % 2), HD * (q % 2) + HD)

            def att_logits(q):
                b, h, r = att(q)
                if q == 0:
                    pe.wait_ge(roped, N_SIDE)
                if q >= 2:
                    pe.wait_ge(masked, q - 1)
                w = (b + 1) * P
                pe.matmul(misc[:, q % 2, 0:w], qT[r, h // 2, b * P:(b + 1) * P], kT[r, h // 2, 0:w],
                          start=True, stop=True).then_inc(logit_mm, 1)

            def att_turn(q):
                b = q // HEADS
                pe.wait_ge(probs_ready, q + 1)
                if q >= 1:
                    pe.wait_ge(probsT_ready, q)
                for c in range(b + 1):
                    ins = pe.transpose(misc[:, 2, c * P:(c + 1) * P], probs[:, q % 2, c * P:(c + 1) * P], const["ident"])
                ins.then_inc(turned, 1)

            def att_pv(q):
                b, h, r = att(q)
                pe.wait_ge(probsT_ready, q + 1)
                if q >= 1:
                    pe.wait_ge(y_taken, q)
                for c in range(b + 1):
                    ins = pe.matmul(misc[r, 3, 0:P], vtok[:, c, h // 2, r.start:r.stop], probsT[:, q % 2, c, :],
                                    start=c == 0, stop=c == b)
                ins.then_inc(pv_done, 1)

            def att_pe(step, q):
                if step == "logits":
                    att_logits(q)
                elif step == "turn":
                    att_turn(q)
                elif step == "values":
                    att_pv(q)

            for u in range(len(EV_UNITS)):
                s = EV_S + u
                bank_free(s)
                if u == 0:
                    first_unit(1, EV_N, prod[:, 2 * (s % 2), :])
                    continue

                def between(k, u=u):
                    for step, q in att_slots.get(u * KT + k, []):
                        att_pe(step, q)
                    if k == (7 if u == 1 else 3):
                        ev_side_pe(u - 1)
                    ev_extra_pe(u * KT + k)

                unit(EV_N + u, prod[:, 2 * (s % 2), :], 0, h_act, True, True, between=between)
            out_pe(EVO_N, EVO_S, lambda k: (emix_hi[:, k, :], emix_lo[:, k, :]),
                   lambda k: pe.wait_ge(emix_ready, k + 1))
            ffn_pe(1)
            ffn_pe(2)

            def prep_pe(j):
                if j == 2:
                    pe.wait_ge(evac, OD_S + 1)
                    pe.wait_ge(rstd_ready, 5)
                    for t in range(TT):
                        ins = pe.matmul(misc[:, 0, t * 16:(t + 1) * 16], hf[:, 0, t * P:(t + 1) * P],
                                        const["ident"][:, 0:16], start=True, stop=True)
                    ins.then_inc(ba_turned, 1)
                if j == 12:
                    pe.wait_ge(g_ready, 1)
                    pe.matmul(misc[:, 1, 0:TT * HEADS], const["tri"], g_tok[:].rearrange("p t h -> p (t h)"),
                              start=True, stop=True).then_inc(gcum_mm, 1)

            def each(dst, lhs, rhs, cut=lambda m: m):
                for t in range(TT):
                    ins = pe.matmul(cut(dst[:, t, :]), lhs[:, t, :], cut(rhs[:, t, :]), start=True, stop=True)
                return ins

            M = [tiles(misc[:, i, :]) for i in range(4)]
            X = [tiles(prod[:, i, :]) for i in (1, 3)]

            def stage_pe(g, name):
                L = g * (LEVELS - 1)
                i = g % 2
                if name == "decay":
                    if g >= 1:
                        pe.wait_ge(tu_ready, TU * (g - 1) + 2)
                    pe.wait_ge(gb_ready, g + 1)
                    for t in range(TT):
                        ins = pe.matmul(M[0][:, t, :], g_b[:, t, :], const["tri"], start=True, stop=True)
                    ins.then_inc(grow_mm, 1)
                elif name in ("normq", "normk"):
                    j = "qk".index(name[-1])
                    pe.wait_ge(qk_sq, 2 * g + j + 1)
                    if j == 0:
                        pe.wait_ge(dif_ready, g + 1)
                    else:
                        pe.wait_ge(qk_rstd, 2 * g + 1)
                    pe.matmul(misc[:, 0, :], const["ones"], sq[:, j, :], start=True, stop=True).then_inc(qk_sum, 1)
                elif name == "gram":
                    pe.wait_ge(qk_ready, 2 * g + 2)
                    pe.wait_ge(act_done, 3 * g + 3)
                    if g >= 1:
                        pe.wait_ge(tu_ready, TU * g)
                    each(M[0], kn, kn).then_inc(kk_mm, 1)
                    each(M[1], kn, tiles(qc[:, g % 2, :]))
                    for t in range(TT):
                        pe.transpose(M[2][:, t, :], kn[:, t, :], const["ident"])
                    for t in range(TT):
                        ins = pe.transpose(M[3][:, t, :], vc[:, g % 2, t * P:(t + 1) * P], const["ident"])
                    ins.then_inc(gram_mm, 1)
                elif name == "turn1":
                    pe.wait_ge(b_made, LEVELS * g + 1)
                    pe.wait_ge(a_made, 5 * g + 1)
                    for t in range(TT):
                        ins = pe.transpose(M[0][:, t, :], b_lvl[:, 1, t, :], const["ident"])
                    ins.then_inc(b1_turned, 1)
                elif name[0] == "y":
                    l = int(name[1:])
                    pe.wait_ge(b_made, LEVELS * g + l)
                    pe.wait_ge(tu_ready, TU * g + 2 * (l - 1) - (l > 2))
                    if l == 2:
                        pe.wait_ge(a_made, 5 * g + 2)
                    each(M[3], b_lvl[:, l % 2], u_inv[:, i]).then_inc(y_mm, 1)
                    if l > 2:
                        for t in range(TT):
                            ins = pe.transpose(M[1][:, t, :], u_inv[:, i, t, :], const["ident"])
                        ins.then_inc(t_mm, 1)
                elif name[0] == "t":
                    l = int(name[1:])
                    pe.wait_ge(y_ready, L + l - 1)
                    if l == 2:
                        pe.wait_ge(a_made, 5 * (g + 1))
                    pe.wait_ge(tu_ready, TU * g + 2 * (l - 1))
                    each(M[2], t_inv, y_lvl, lambda m: half_blocks(m, l, 1)).then_inc(t_mm, 1)
                elif name == "w":
                    pe.wait_ge(tu_ready, TU * (g + 1))
                    if g >= 1:
                        pe.wait_ge(o_rstd, g)
                    each(X[1], k_beg[:, i], u_inv[:, i]).then_inc(w_mm, 1)
                elif name[:3] == "new":
                    t = int(name[3:])
                    if t == 0:
                        pe.wait_ge(w_ready, g + 1)
                    else:
                        pe.wait_ge(state_ready, (TT - 1) * g + t)
                    ins = pe.matmul(X[1][:, t, :], u_inv[:, i, t, :], v_beta[:, i, t, :], start=True, stop=t == 0)
                    if t:
                        ins = pe.matmul(X[1][:, t, :], neg_w[:, t, :], state[:, t % 2, :], start=False, stop=True)
                    ins.then_inc(vnew_mm, 1)
                elif name[:3] == "out":
                    t = int(name[3:])
                    pe.wait_ge(vnew_ready, TT * g + t + 1)
                    if t == 0:
                        pe.wait_ge(qdec_ready, g + 1)
                        if g >= 1:
                            pe.wait_ge(on_ready, g)
                    if t < TT - 1:
                        pe.matmul(X[1][:, t, :], k_dec[:, i, t, :], v_new[:, t % 2, :], start=True, stop=True)\
                            .then_inc(state_mm, 1)
                    if t:
                        pe.matmul(X[0][:, t, :], state[:, t % 2, :], q_dec[:, i, t, :], start=True, stop=False)
                    pe.matmul(X[0][:, t, :], v_new[:, t % 2, :], intra_t[:, i, t, :], start=t == 0, stop=True)\
                        .then_inc(out_mm, 1)
                elif name == "osum":
                    pe.wait_ge(o_sq, g + 1)
                    pe.matmul(prod[:, 3, :], const["ones"], sq_acc[:], start=True, stop=True).then_inc(o_sum, 1)

            for u in range(len(OD_UNITS)):
                s = OD_S + u
                bank_free(s)
                if u == 0:
                    first_unit(4, OD_N, prod[:, 2 * (s % 2), :])
                    continue

                def between(k, u=u):
                    slot = (u - 1) * KT + k
                    prep_pe(slot)
                    for g, name in od_slots.get(slot, []):
                        stage_pe(g, name)

                unit(OD_N + u, prod[:, 2 * (s % 2), :], 0, h_act, True, True, between=between)
            out_pe(ODO_N, ODO_S, lambda k: (omix_hi[:, k, :], omix_lo[:, k, :]),
                   lambda k: pe.wait_ge(omix_ready, k + 1))
            ffn_pe(3)

            turn_y(KT - 2)
            for t in range(TT):
                a = slice(t * P, (t + 1) * P)
                pe.wait_ge(acc_done, 6 * 7)
                pe.matmul(misc[:, 0, t:t + 1], sq_acc[:, a], const["ones"][:, 0:1], start=True, stop=False)
                pe.wait_ge(sq_ready, 8 * 7)
                ins = pe.matmul(misc[:, 0, t:t + 1], sq[:, 1, a], const["ones"][:, 0:1], start=False, stop=True)
            ins.then_inc(sum_done, 1)
            turn_y(KT - 1)

        @block.scalar
        def _(act):
            seq = [0]

            def link(ins):
                seq[0] += 1
                ins.then_inc(act_seq, 1)
                act.wait_ge(act_seq, seq[0])

            def split(n, i=0):
                if n >= N_END:
                    return
                act.wait_ge(raw_in[n % 4], 16 * (n // 4 + 1) + 16 * i)
                if n >= 2:
                    act.wait_ge(unit_done, n - 1 + 4 * i)
                w = unit_width(n)
                act.activation(w_hi[:, n % 2, 0:w], raw[:, n % 4, 0:w], ACT.Copy).then_inc(hi_ready, 1)

            def tile(r, m, ready, count):
                if m == KT - 1:
                    act.activation(warm[:], eps[:], ACT.Ln)
                act.wait_ge(ready, count)
                hi(r, m)
                square(r, m)

            def hi(r, m):
                if r < 6:
                    act.activation(h_hi[:, m, :], x[:, m, :], ACT.Copy, scale=gains[:, r, m:m + 1])\
                        .then_inc(hhi_ready, 1)

            def square(r, m):
                if m >= 2:
                    act.wait_ge(acc_done, 6 * r + max(m - 2, 1))
                act.activation(sq[:, m % 2, :], x[:, m, :], ACT.Square).then_inc(sq_ready, 1)

            def norm(r):
                act.wait_ge(sum_done, r + 1)
                link(act.activation(rstd[:], misc[:, 0, :], ACT.Ln, bias=eps[:], scale=1.0 / D))
                act.activation(rstd[:], rstd[:], ACT.Exp, scale=-0.5).then_inc(rstd_ready, 1)

            def ffn_act(f):
                n0, s0 = FFN_AT[f]

                def pair(i, tail=False):
                    for u in range(4):
                        n, s = n0 + u, s0 + u // 2
                        if tail:
                            split(n0 + 2 * FT - 4 + u + 2)
                            j = FT - 2 + u // 2
                            sem_i, jj = FT // 2 - 1, j
                        else:
                            split(n + 2, i)
                            sem_i = i
                            jj = None
                        if u % 2 == 1:
                            act.wait_ge(a_scaled, FT * f + u // 2 + 1 + 2 * sem_i)
                            dst = a_hi[:, jj, :] if tail else \
                                a_hi[:, bass.ds(i * 2 + u // 2, 1), :].rearrange("p a c -> p (a c)")
                            act.activation(dst, act_f[:, s % 2, :], ACT.Copy).then_inc(ahi_ready, 1)
                        else:
                            act.wait_ge(gate_scaled, FT * f + u // 2 + 1 + 2 * sem_i)
                            act.activation(silu_g[:, s % 2, :], silu_g[:, s % 2, :], ACT.Silu).then_inc(silu_done, 1)

                with act.Fori(0, FT // 2 - 1) as i:
                    pair(i)
                pair(0, tail=True)
                for m in range(KT):
                    for half in range(2):
                        split(n0 + 2 * FT + 2 * m + half + 2)
                    tile(norm_of(f) + 1, m, evac, s0 + FT + m + 1)

            act.wait_ge(setup_in, 16 * SETUP)
            for k in range(KT):
                act.wait_ge(x_in, k + 1)
                hi(0, k)
                if k in (0, 1):
                    split(k)
            for k in range(KT):
                square(0, k)
            norm(0)
            ffn_act(0)
            norm(1)

            act.wait_ge(ang_ready, 1)
            for i in range(2):
                act.activation((sinT, cosT)[i][:], hf[:, i, :], ACT.Sin).then_inc(trig_ready, 1)

            def ev_extra_act(slot):
                for kind, b, j in extras.get(slot, []):
                    if kind == "idx":
                        q = (b - 1) * HEADS + j
                        act.wait_ge(idx_mm, q + 1)
                        if q >= 2:
                            act.wait_ge(idx_added, q - 1)
                        act.activation(relu_s[:, q % 2, 0:(b + 1) * P], prod[:, 1 + 2 * (q % 2), 0:(b + 1) * P], ACT.Relu)\
                            .then_inc(relu_done, 1)

            def att_act(step, q):
                if step == "logits":
                    act.wait_ge(masked, q + 1)
                    if q >= 2:
                        act.wait_ge(turned, q - 1)
                    w = (q // HEADS + 1) * P
                    act.activation(probs[:, q % 2, 0:w], relu_s[:, q % 2, 0:w], ACT.Exp, bias=amax_n[:, q % 2:q % 2 + 1],
                                   accum_out=asum[:, q % 2:q % 2 + 1]).then_inc(exp_done, 1)
                elif step == "scale":
                    i, w = q % 2, (q // HEADS + 1) * P
                    act.wait_ge(arcp_ready, q + 1)
                    act.activation(probs[:, i, 0:w], probs[:, i, 0:w], ACT.Copy, scale=arcp[:, i:i + 1])\
                        .then_inc(probs_ready, 1)
                elif step == "values":
                    b, h = q // HEADS, q % HEADS
                    r = slice(HD * (h % 2), HD * (h % 2) + HD)
                    act.wait_ge(pv_done, q + 1)
                    act.activation(y_f[r, h // 2, b * P:(b + 1) * P], misc[r, 3, 0:P], ACT.Copy).then_inc(y_taken, 1)
                elif step == "turn":
                    c = q // HEADS + 1
                    act.wait_ge(turned, q + 1)
                    if q >= 2:
                        act.wait_ge(pv_done, q - 1)
                    act.activation(probsT[:, q % 2, 0:c, :], tiles(misc[:, 2, :])[:, 0:c, :], ACT.Copy)\
                        .then_inc(probsT_ready, 1)

            for u in range(1, len(EV_UNITS) + 1):
                kind, m = EV_UNITS[u - 1]
                for k in range(KT):
                    for step, q in att_slots.get(u * KT + k, []):
                        att_act(step, q)
                    if k == 0:
                        split(EV_N + u + 1)
                    if k == 3 and kind == "b":
                        act.wait_ge(y_conv, m + 1)
                        act.activation(emix_hi[:, m, :], act_f[:, m % 2, :], ACT.Copy).then_inc(emhi, 1)
                    ev_extra_act(u * KT + k)
            act.wait_ge(y_taken, Q_ITEMS)
            for m in range(4):
                act.activation(emix_hi[:, 4 + m, :], y_f[:, m, :], ACT.Copy).then_inc(emhi, 1)
            for m in range(KT):
                split(EVO_N + m + 2)
                tile(2, m, evac, EVO_S + m + 1)
            norm(2)
            ffn_act(1)
            norm(3)
            ffn_act(2)
            norm(4)

            def prep_act(j):
                if j == 4:
                    act.wait_ge(ba_tok_in, 1)
                    act.activation(beta[:], ba_tok[:, :, 0:HEADS], ACT.Exp, scale=-1.0).then_inc(gate_exp, 1)
                    act.wait_ge(ba_tok_in, 2)
                    link(act.activation(gt1[:], gt1[:], ACT.Exp, scale=-1.0))
                    link(act.activation(gt1[:], gt1[:], ACT.Ln, bias=1.0))
                    act.activation(alog[:], alog[:], ACT.Exp).then_inc(gate_exp, 1)
                if j == 14:
                    act.wait_ge(g_cum_in, 1)
                    act.activation(beg[:], g_cum[:], ACT.Exp).then_inc(gate_exp, 1)

            M = [tiles(misc[:, i, :]) for i in range(4)]
            X = [tiles(prod[:, i, :]) for i in (1, 3)]

            def stage_act(g, name):
                L = g * (LEVELS - 1)
                i = g % 2
                if name in ("squareq", "squarek"):
                    j = "qk".index(name[-1])
                    act.wait_ge(act_done, 3 * g + j + 1)
                    act.activation(sq[:, j, :], (qc, kc)[j][:, i, :], ACT.Square).then_inc(qk_sq, 1)
                elif name in ("normq", "normk"):
                    j = "qk".index(name[-1])
                    act.wait_ge(qk_sum, 2 * g + j + 1)
                    link(act.activation(silu_g[:, j, :], misc[:, 0, :], ACT.Ln, bias=eps[:]))
                    act.activation(silu_g[:, j, :], silu_g[:, j, :], ACT.Exp, scale=-0.5).then_inc(qk_rstd, 1)
                elif name == "decay":
                    act.wait_ge(grow_mm, g + 1)
                    if g >= 1:
                        act.wait_ge(qdec_ready, g)
                    act.activation(e_row[:], M[0], ACT.Exp).then_inc(e_row_ready, 1)
                elif name == "mask":
                    act.wait_ge(dif_ready, g + 1)
                    act.activation(dec_t[:], dec_t[:], ACT.Exp)
                    act.activation(dec_a[:], dec_a[:], ACT.Exp, scale=-1.0).then_inc(dec_exp, 1)
                elif name[0] == "y":
                    l = int(name[1:])
                    act.wait_ge(y_mm, L + l - 1)
                    act.activation(y_lvl[:], M[3], ACT.Copy).then_inc(y_ready, 1)
                elif name == "w":
                    act.wait_ge(w_mm, g + 1)
                    act.activation(neg_w[:], X[1], ACT.Copy, scale=-1.0).then_inc(w_ready, 1)
                elif name == "osquare":
                    act.wait_ge(out_mm, TT * (g + 1))
                    act.activation(sq_acc[:], prod[:, 1, :], ACT.Square).then_inc(o_sq, 1)
                elif name == "osum":
                    act.wait_ge(o_sum, g + 1)
                    link(act.activation(act_f[:, 1, :], prod[:, 3, :], ACT.Ln, bias=eps[:], scale=1.0 / P))
                    act.activation(act_f[:, 1, :], act_f[:, 1, :], ACT.Exp, scale=-0.5).then_inc(o_rstd, 1)

            for u in range(1, len(OD_UNITS) + 1):
                kind, h = OD_UNITS[u - 1]
                for k in range(KT):
                    slot = (u - 1) * KT + k
                    prep_act(slot)
                    for g, name in od_slots.get(slot, []):
                        stage_act(g, name)
                    if k == 0:
                        split(OD_N + u + 1)
                    if k == 2 and kind == "z":
                        act.wait_ge(evac, OD_S + u)
                        act.activation(hf[:, h % 2, :], hf[:, h % 2, :], ACT.Silu).then_inc(act_done, 1)
                    if k == 5 and kind == "z":
                        act.wait_ge(gated, h + 1)
                        act.activation(omix_hi[:, h, :], act_f[:, 0, :], ACT.Copy).then_inc(ohi, 1)
                    if k == 7 and kind in "qkv":
                        dst = {"q": qc, "k": kc, "v": vc}[kind][:, h % 2, :]
                        act.wait_ge(conv_done, u - 1)
                        act.activation(dst, dst, ACT.Silu).then_inc(act_done, 1)
            for m in range(KT):
                split(ODO_N + m + 2)
                tile(5, m, evac, ODO_S + m + 1)
            norm(5)
            ffn_act(3)
            act.wait_ge(sum_done, 7)
            link(act.activation(rstd_row[:], misc[:, 0, 0:TT], ACT.Ln, bias=eps[:], scale=1.0 / D))
            act.activation(rstd_row[:], rstd_row[:], ACT.Exp, scale=-0.5).then_inc(rstd_ready, 1)
            act.wait_ge(rstd_ready, 7)
            act.wait_ge(y_rows_in, KT)
            for t in range(TT // 2, TT):
                act.activation(y_rows[:, t, :], y_rows[:, t, :], ACT.Copy, scale=rstd_row[:, t:t + 1]).then_inc(y_scaled_s, 1)

        @block.vector
        def _(dve):
            seq = [0]

            def link(ins):
                seq[0] += 1
                ins.then_inc(dve_seq, 1)
                dve.wait_ge(dve_seq, seq[0])

            def split(n, i=0):
                if n >= N_END:
                    return
                w = unit_width(n)
                dve.wait_ge(hi_ready, n + 1 + 4 * i)
                dve.tensor_tensor(w_lo[:, n % 2, 0:w], raw[:, n % 4, 0:w], w_hi[:, n % 2, 0:w].bitcast(F32),
                                  ALU.subtract).then_inc(lo_ready, 1)

            def lo(r, m):
                dve.wait_ge(hhi_ready, 8 * r + m + 1)
                dve.scalar_tensor_tensor(h_lo[:, m, :], x[:, m, :], gains[:, r, m:m + 1], h_hi[:, m, :].bitcast(F32),
                                         ALU.mult, ALU.subtract).then_inc(h_ready, 1)

            def residual(m, s, n_units, scale):
                dve.wait_ge(unit_done, n_units)
                dve.scalar_tensor_tensor(x[:, m, :], prod[:, 2 * (s % 2), :], scale, x[:, m, :], ALU.mult, ALU.add)\
                    .then_inc(evac, 1)

            def angles(m):
                pos, ang = hf[:, 1, :], hf[:, 0, :]
                magic = 1.5 * 2.0 ** 23
                if m == 0:
                    dve.wait_ge(ev_in, 16 * 2)
                    link(dve.tensor_copy(ang, pos.bitcast(I32)))
                    link(dve.tensor_scalar(ang, ang, freq[:], None, ALU.mult))
                elif m < 7:
                    unit_2pi, count = ((4096.0, 7), (1.0, 6))[(m - 1) // 3]
                    parts = pi_parts(2 * np.pi * unit_2pi, count)
                    if (m - 1) % 3 == 0:
                        link(dve.tensor_scalar(pos, ang, float(1.0 / (2 * np.pi * unit_2pi)), magic, ALU.mult, ALU.add))
                        link(dve.tensor_scalar(pos, pos, magic, None, ALU.subtract))
                    for part in parts[(m - 1) % 3 * 3:][:3]:
                        link(dve.scalar_tensor_tensor(ang, pos, -part, ang, ALU.mult, ALU.add))
                else:
                    link(dve.tensor_scalar(ang, ang, 3.141592, -3.141592, ALU.min, ALU.max))
                    link(dve.scalar_tensor_tensor(pos, ang, -1.0, ang, ALU.mult, ALU.max))
                    dve.tensor_scalar(pos, pos, -1.0, float(np.float32(np.pi / 2)), ALU.mult, ALU.add)\
                        .then_inc(ang_ready, 1)

            def rows(m):
                dve.wait_ge(y_turned, m + 1)
                dve.tensor_copy(y_rows[:, :, m * P:(m + 1) * P], tiles(misc[:, 1 + m % 3, :])).then_inc(y_rows_in, 1)

            def ffn_dve(f):
                n0, s0 = FFN_AT[f]

                def pair(i, tail=False):
                    for u in range(4):
                        n, s = n0 + u, s0 + u // 2
                        sem_i = FT // 2 - 1 if tail else i
                        if tail:
                            split(n0 + 2 * FT - 4 + u + 2)
                        else:
                            split(n + 2, i)
                        j = FT * f + u // 2
                        if u % 2 == 0:
                            dve.wait_ge(unit_done, n + 1 + 4 * sem_i)
                            if u == 0 and not tail:
                                dve.wait_ge(rstd_ready, norm_of(f) + 1)
                            dve.tensor_tensor(silu_g[:, s % 2, :], prod[:, 2 * (s % 2), :], rstd[:], ALU.mult)\
                                .then_inc(gate_scaled, 1)
                        else:
                            dve.wait_ge(silu_done, j + 1 + 2 * sem_i)
                            dve.wait_ge(unit_done, n + 1 + 4 * sem_i)
                            dve.tensor_tensor(act_f[:, s % 2, :], silu_g[:, s % 2, :], prod[:, 2 * (s % 2) + 1, :],
                                              ALU.mult).then_inc(evac, 1)
                            dve.wait_ge(evac, s + 1 + 2 * sem_i)
                            dve.tensor_tensor(act_f[:, s % 2, :], act_f[:, s % 2, :], rstd[:], ALU.mult)\
                                .then_inc(a_scaled, 1)
                            dve.wait_ge(ahi_ready, j + 1 + 2 * sem_i)
                            if tail:
                                hi, dst = a_hi[:, FT - 2 + u // 2, :], a_lo[:, FT - 2 + u // 2, :]
                            else:
                                hi, dst = (t[:, bass.ds(i * 2 + u // 2, 1), :].rearrange("p a c -> p (a c)")
                                           for t in (a_hi, a_lo))
                            dve.tensor_tensor(dst, act_f[:, s % 2, :], hi.bitcast(F32), ALU.subtract)\
                                .then_inc(a_ready, 1)
                            dve.wait_ge(a_ready, j + 1 + 2 * sem_i)

                with dve.Fori(0, FT // 2 - 1) as i:
                    pair(i)
                pair(0, tail=True)
                for m in range(KT):
                    for half in range(2):
                        split(n0 + 2 * FT + 2 * m + half + 2)
                    if f == NFFN - 1 and m >= 3:
                        rows(m - 3)
                    residual(m, s0 + FT + m, n0 + 2 * FT + 2 * m + 2, 0.5)
                    if f == NFFN - 1:
                        dve.wait_ge(evac, s0 + FT + m + 1)
                        dve.tensor_scalar(y_feat[:, m, :], x[:, m, :], gains[:, 6, m:m + 1], None, ALU.mult)\
                            .then_inc(y_made, 1)
                    if f < NFFN - 1:
                        lo(norm_of(f) + 1, m)
                    if f == 0:
                        angles(m)

            for k in range(KT):
                dve.wait_ge(x_turned, k + 1)
                dve.tensor_copy(x[:, k, :], prod[:, k % 4, :]).then_inc(x_in, 1)
                if k >= 6:
                    split(k - 6)
            for k in range(KT):
                lo(0, k)
            ffn_dve(0)

            def ev_extra_dve(items):
                for kind, b, j in items:
                    w = (b + 1) * P
                    if kind == "idx":
                        q = (b - 1) * HEADS + j
                        dve.wait_ge(relu_done, q + 1)
                        wcol = w_idx[:, b, j:j + 1]
                        if j == 0:
                            ins = dve.tensor_scalar(score[:, b - 1, 0:w], relu_s[:, q % 2, 0:w], wcol, None, ALU.mult)
                        else:
                            ins = dve.scalar_tensor_tensor(score[:, b - 1, 0:w], relu_s[:, q % 2, 0:w], wcol,
                                                           score[:, b - 1, 0:w], ALU.mult, ALU.add)
                        ins.then_inc(idx_added, 1)
                        dve.wait_ge(idx_added, q + 1)
                        if j == HEADS - 1:
                            link(dve.tensor_tensor(score[:, b - 1, b * P:w], score[:, b - 1, b * P:w], const["neg_future"],
                                                   ALU.add))
                    else:
                        link(dve.max(top8[:], score[:, b - 1, 0:w]))
                        link(dve.match_replace(score[:, b - 1, 0:w], top8[:], score[:, b - 1, 0:w], MARK))
                        if j == ROUNDS - 1:
                            link(dve.tensor_scalar(score[:, b - 1, 0:w], score[:, b - 1, 0:w], SPLIT, NEG,
                                                   ALU.is_gt, ALU.mult))

            def ev_side_dve(u):
                kind, m = EV_UNITS[u]
                if kind == "ik":
                    dve.wait_ge(rot_done, 1)
                    dve.wait_ge(trig_ready, 2)
                    dve.tensor_scalar(w_idx[:].rearrange("p t h -> p (t h)"), misc[:, 2, 0:TT * HEADS],
                                      float((HEADS * HD) ** -0.5), None, ALU.mult)
                    dve.tensor_tensor(ubuf[:], misc[:, 1, :], sinT[:], ALU.mult)
                    link(dve.tensor_tensor(ik[:], misc[:, 0, :], cosT[:], ALU.mult))
                    dve.tensor_tensor(ik[:], ik[:], ubuf[:], ALU.add).then_inc(roped, 1)
                elif kind in ROPED:
                    dst = {"iq": iq, "q": qT, "k": kT}[kind][:, m, :]
                    dve.wait_ge(rot_done, u + 1)
                    link(dve.tensor_tensor(ubuf[:], misc[:, 0, :], sinT[:], ALU.mult))
                    dve.wait_ge(cos_part, u)
                    dve.tensor_tensor(dst, dst, ubuf[:], ALU.add).then_inc(roped, 1)
                elif kind == "v":
                    dve.wait_ge(rot_done, u + 1)
                    dve.tensor_copy(vtok[:, :, m, :], tiles(misc[:, 0, :])).then_inc(roped, 1)

            def att_dve(step, q):
                if step == "logits":
                    b, i = q // HEADS, q % 2
                    w = (b + 1) * P
                    dve.wait_ge(logit_mm, q + 1)
                    if q >= 2:
                        dve.wait_ge(exp_done, q - 1)
                    mask = score[:, b - 1, 0:w] if b else const["neg_future"]
                    link(dve.tensor_tensor_reduce(relu_s[:, i, 0:w], misc[:, i, 0:w], mask, HD ** -0.5,
                                                  NEG, ALU.add, ALU.max, amax[:, i:i + 1]))
                    dve.tensor_scalar(amax_n[:, i:i + 1], amax[:, i:i + 1], -1.0, None, ALU.mult).then_inc(masked, 1)
                elif step == "scale":
                    i = q % 2
                    dve.wait_ge(exp_done, q + 1)
                    dve.reciprocal(arcp[:, i:i + 1], asum[:, i:i + 1]).then_inc(arcp_ready, 1)

            def ev_finish(u, k):
                kind, m = EV_UNITS[u]
                bank = prod[:, 2 * ((EV_S + u) % 2), :]
                if k == 0:
                    dve.wait_ge(unit_done, EV_N + u + 1)
                    if u == 0:
                        dve.wait_ge(rstd_ready, 2)
                    if kind in ("ik", "iq", "k", "q", "v"):
                        if u < 2:
                            dve.wait_ge(trig_ready, 2)
                        else:
                            dve.wait_ge(rot_done, u - 1)
                            dve.wait_ge(roped, u - 1)
                        dve.tensor_tensor(roped_in[:, u % 2, :], bank, rstd[:], ALU.mult).then_inc(evac, 1)
                    elif kind == "c":
                        dve.tensor_tensor(cbuf[:], bank, rstd[:], ALU.mult).then_inc(evac, 1)
                    elif kind == "x":
                        dve.tensor_tensor(ubuf[:], cbuf[:], bank, ALU.mult).then_inc(evac, 1)
                    else:
                        dve.tensor_tensor(act_f[:, m % 2, :], cbuf[:], bank, ALU.mult).then_inc(evac, 1)
                elif k == 1:
                    if u + 2 < POOL_UNIT:
                        split(EV_N + u + 2)
                elif kind == "c" and k == 2:
                    dve.wait_ge(evac, EV_S + u + 1)
                    link(dve.tensor_tensor(cbuf[:], cbuf[:], rstd[:], ALU.mult))
                elif kind == "x" and k == 2:
                    dve.wait_ge(evac, EV_S + u + 1)
                    if m == 0:
                        dve.wait_ge(conv_in, 16)
                    link(dve.tensor_scalar(cbuf[:], ubuf[:], ev_conv[:, m, 2:3], None, ALU.mult))
                elif kind == "x" and k in (4, 6):
                    j = k // 2 - 1
                    link(dve.scalar_tensor_tensor(cbuf[:, j:T], ubuf[:, 0:T - j], ev_conv[:, m, 2 - j:3 - j],
                                                  cbuf[:, j:T], ALU.mult, ALU.add))
                elif kind == "b" and k == 2:
                    dve.wait_ge(evac, EV_S + u + 1)
                    dve.tensor_tensor(act_f[:, m % 2, :], act_f[:, m % 2, :], rstd[:], ALU.mult).then_inc(y_conv, 1)
                elif kind == "b" and k == 5:
                    dve.wait_ge(emhi, m + 1)
                    dve.tensor_tensor(emix_lo[:, m, :], act_f[:, m % 2, :], emix_hi[:, m, :].bitcast(F32), ALU.subtract)\
                        .then_inc(emix_ready, 1)
                    dve.wait_ge(emix_ready, m + 1)
                elif k == (7 if u == 0 else 5):
                    ev_side_dve(u)

            for u in range(1, len(EV_UNITS) + 1):
                for k in range(KT):
                    for step, q in att_slots.get(u * KT + k, []):
                        att_dve(step, q)
                    ev_finish(u - 1, k)
                    ev_extra_dve([e for e in extras.get(u * KT + k - 1, []) if e[0] == "idx"])
                    ev_extra_dve([e for e in extras.get(u * KT + k, []) if e[0] == "top"])
            for m in range(4):
                dve.wait_ge(emhi, 5 + m)
                dve.tensor_tensor(emix_lo[:, 4 + m, :], y_f[:, m, :], emix_hi[:, 4 + m, :].bitcast(F32), ALU.subtract)\
                    .then_inc(emix_ready, 1)
            dve.wait_ge(lo_ready, EVO_N + 2)
            for m in range(KT):
                split(EVO_N + m + 2)
                residual(m, EVO_S + m, EVO_N + m + 1, 1.0)
                lo(2, m)
            ffn_dve(1)
            ffn_dve(2)

            def bc(ap):
                return ap.unsqueeze(1).broadcast_to([P, TT, HEADS])

            def prep_dve(j):
                if j == 4:
                    dve.wait_ge(ba_turned, 1)
                    dve.wait_ge(od_in, 16 * 4)
                    dve.tensor_copy(ba_tok[:], misc[:, 0, 0:TT * 16].rearrange("p (t c) -> p t c", t=TT))\
                        .then_inc(ba_tok_in, 1)
                    dve.wait_ge(ba_tok_in, 1)
                    link(dve.tensor_tensor(gt2[:], ba_tok[:, :, HEADS:2 * HEADS], bc(dtb[:]), ALU.add))
                    dve.scalar_tensor_tensor(gt1[:], gt2[:], -1.0, gt2[:], ALU.mult, ALU.max).then_inc(ba_tok_in, 1)
                    dve.wait_ge(ba_tok_in, 2)
                    link(dve.tensor_scalar(gt2[:], gt2[:], 0.0, None, ALU.max))
                    dve.wait_ge(gate_exp, 1)
                    link(dve.tensor_scalar(beta[:], beta[:], 1.0, None, ALU.add))
                    link(dve.reciprocal(beta[:], beta[:]))
                    dve.wait_ge(gate_exp, 2)
                    link(dve.tensor_tensor(gt2[:], gt2[:], gt1[:], ALU.add))
                    dve.scalar_tensor_tensor(g_tok[:], gt2[:], -1.0, bc(alog[:]), ALU.mult, ALU.mult)\
                        .then_inc(g_ready, 1)
                if j == 14:
                    dve.wait_ge(gcum_mm, 1)
                    dve.tensor_copy(g_cum[:].rearrange("p t h -> p (t h)"), misc[:, 1, 0:TT * HEADS])\
                        .then_inc(g_cum_in, 1)
                    dve.wait_ge(gate_exp, 3)
                    link(dve.tensor_tensor(beg[:], beg[:], beta[:], ALU.mult))

            M = [tiles(misc[:, i, :]) for i in range(4)]

            def col(t, g):
                return t[:, :, g:g + 1].broadcast_to([P, TT, P])

            def same(m):
                return m.unsqueeze(1).broadcast_to([P, TT, P])

            X = [tiles(prod[:, i, :]) for i in (1, 3)]

            def stage_dve(g, name):
                i = g % 2
                if name == "spread":
                    if g == 0:
                        dve.wait_ge(g_ready, 1)
                    dve.tensor_copy(g_b[:], col(g_tok, g)).then_inc(gb_ready, 1)
                elif name == "decay":
                    dve.wait_ge(grow_mm, g + 1)
                    dve.wait_ge(e_row_ready, g + 1)
                    link(dve.tensor_tensor(dec_a[:], M[0], col(g_cum, g), ALU.subtract))
                    link(dve.tensor_scalar(dec_t[:], dec_a[:], 0.0, None, ALU.min))
                    dve.tensor_scalar(dec_a[:], dec_a[:], 0.0, None, ALU.max).then_inc(dif_ready, 1)
                elif name == "scaleq":
                    dve.wait_ge(qk_rstd, 2 * g + 1)
                    dve.scalar_tensor_tensor(qc[:, i, :], qc[:, i, :], float(P ** -0.5), silu_g[:, 0, :],
                                             ALU.mult, ALU.mult).then_inc(qk_ready, 1)
                elif name == "scalek":
                    dve.wait_ge(qk_rstd, 2 * g + 2)
                    dve.tensor_tensor(kn[:].rearrange("p t c -> p (t c)"), kc[:, i, :], silu_g[:, 1, :], ALU.mult)\
                        .then_inc(qk_ready, 1)
                elif name == "gram":
                    dve.tensor_copy(e_last[:, i], e_row[:, :, P - 1:P])
                    dve.wait_ge(kk_mm, g + 1)
                    dve.wait_ge(dec_ready, 2 * g + 1)
                    dve.tensor_tensor(a_mat[:], M[0], dec_a[:], ALU.mult).then_inc(a_made, 1)
                    dve.wait_ge(gram_mm, g + 1)
                    dve.tensor_tensor(v_beta[:, i], M[3], col(beta, g), ALU.mult).then_inc(a_made, 1)
                elif name == "turn1":
                    dve.wait_ge(b_made, LEVELS * g + 1)
                    dve.tensor_tensor(t_inv[:], same(const["ident"]), b_lvl[:, 1], ALU.subtract).then_inc(tu_ready, 1)
                    dve.wait_ge(b1_turned, g + 1)
                    dve.tensor_tensor(u_inv[:, i], same(const["ident"]), M[0], ALU.subtract).then_inc(tu_ready, 1)
                    dve.tensor_tensor(k_beg[:, i], M[2], col(beg, g), ALU.mult).then_inc(a_made, 1)
                    dve.wait_ge(dec_ready, 2 * g + 2)
                    dve.tensor_tensor(intra_t[:, i], M[1], dec_t[:], ALU.mult).then_inc(a_made, 1)
                    dve.tensor_tensor(k_dec[:, i], M[2], dec_t[:, :, P - 1:P].broadcast_to([P, TT, P]), ALU.mult)\
                        .then_inc(a_made, 1)
                elif name[0] == "t":
                    l = int(name[1:])
                    dve.wait_ge(t_mm, TM * g + 2 * l - 3)
                    u, du = (half_blocks(m, l, 1) for m in (u_inv[:, i], M[2]))
                    dve.tensor_tensor(u, u, du, ALU.subtract).then_inc(tu_ready, 1)
                elif name[0] == "y" and name != "y2":
                    l = int(name[1:])
                    dve.wait_ge(t_mm, TM * g + 2 * l - 4)
                    tm, tt = (half_blocks(m, l - 1, 0) for m in (t_inv[:], M[1]))
                    dve.tensor_copy(tm, tt).then_inc(tu_ready, 1)
                elif name[:3] == "new":
                    t = int(name[3:])
                    dve.wait_ge(vnew_mm, TT * g + t + 1)
                    dve.tensor_copy(v_new[:, t % 2, :], X[1][:, t, :]).then_inc(vnew_ready, 1)
                elif name[:3] == "out" and name != f"out{TT - 1}":
                    t = int(name[3:])
                    dve.wait_ge(state_mm, (TT - 1) * g + t + 1)
                    if t == 0:
                        dve.tensor_copy(state[:, 1, :], X[1][:, t, :]).then_inc(state_ready, 1)
                    else:
                        dve.wait_ge(state_ready, (TT - 1) * g + t)
                        dve.scalar_tensor_tensor(state[:, (t + 1) % 2, :], state[:, t % 2, :], e_last[:, i, t, :],
                                                 X[1][:, t, :], ALU.mult, ALU.add).then_inc(state_ready, 1)
                elif name == "fin":
                    dve.wait_ge(o_rstd, g + 1)
                    dve.scalar_tensor_tensor(o_n[:, g, :], prod[:, 1, :], o_gain[:], act_f[:, 1, :], ALU.mult, ALU.mult)\
                        .then_inc(on_ready, 1)

            def od_finish(u, k):
                kind, h = OD_UNITS[u]
                bank = prod[:, 2 * ((OD_S + u) % 2), :]
                if k == 0:
                    dve.wait_ge(unit_done, OD_N + u + 1)
                    if u == 0:
                        dve.wait_ge(rstd_ready, 5)
                        dve.wait_ge(od_in, 16 * 4)
                    dst = {"ba": hf[:, 0, :], "z": hf[:, h % 2, :]}.get(kind, pre)
                    dve.tensor_tensor(dst, bank, rstd[:], ALU.mult).then_inc(evac, 1)
                elif k == 1:
                    split(OD_N + u + 2)
                elif kind == "z" and k == 4:
                    dve.wait_ge(act_done, 3 * HEADS + h + 1)
                    dve.wait_ge(on_ready, h + 1)
                    dve.tensor_tensor(act_f[:, 0, :], hf[:, h % 2, :], o_n[:, h, :], ALU.mult).then_inc(gated, 1)
                elif kind == "z" and k == 7:
                    dve.wait_ge(ohi, h + 1)
                    dve.tensor_tensor(omix_lo[:, h, :], act_f[:, 0, :], omix_hi[:, h, :].bitcast(F32), ALU.subtract)\
                        .then_inc(omix_ready, 1)
                    dve.wait_ge(omix_ready, h + 1)
                elif kind in "qkv" and k in TAP_SLOTS:
                    dst = {"q": qc, "k": kc, "v": vc}[kind][:, h % 2, :]
                    c = "qkv".index(kind) * HEADS + h
                    j = TAP_SLOTS.index(k)
                    if j == 0:
                        dve.wait_ge(evac, OD_S + u + 1)
                        link(dve.tensor_scalar(dst, pre, od_conv[:, c, 3:4], None, ALU.mult))
                        return
                    ins = dve.scalar_tensor_tensor(dst[:, j:T], pre[:, 0:T - j], od_conv[:, c, 3 - j:4 - j],
                                                   dst[:, j:T], ALU.mult, ALU.add)
                    if j < 3:
                        link(ins)
                    else:
                        ins.then_inc(conv_done, 1)
                        dve.wait_ge(conv_done, u)

            for u in range(1, len(OD_UNITS) + 1):
                for k in range(KT):
                    slot = (u - 1) * KT + k
                    prep_dve(slot)
                    for g, name in od_slots.get(slot, []):
                        stage_dve(g, name)
                    od_finish(u - 1, k)
            for m in range(KT):
                split(ODO_N + m + 2)
                residual(m, ODO_S + m, ODO_N + m + 1, 1.0)
                lo(5, m)
            ffn_dve(3)
            for m in range(KT - 3, KT):
                rows(m)
            dve.wait_ge(y_rows_in, KT)
            dve.wait_ge(rstd_ready, 7)
            for t in range(TT // 2):
                dve.tensor_scalar(y_rows[:, t, :], y_rows[:, t, :], rstd_row[:, t:t + 1], None, ALU.mult)\
                    .then_inc(y_scaled_v, 1)

        @block.gpsimd
        def _(pool):
            def same(m):
                return m.unsqueeze(1).broadcast_to([P, TT, P])

            def add_squares(r):
                for m in range(1, 7):
                    pool.wait_ge(sq_ready, 8 * r + m + 1)
                    a = sq[:, 0, :] if m == 1 else sq_acc[:]
                    if m == 1 and r:
                        pool.wait_ge(sum_done, r)
                    pool.tensor_tensor(sq_acc[:], a, sq[:, m % 2, :], ALU.add).then_inc(acc_done, 1)
                    pool.wait_ge(acc_done, 6 * r + m)

            add_squares(0)
            add_squares(1)
            pool.wait_ge(trig_ready, 2)
            for u, (kind, m) in enumerate(EV_UNITS):
                if kind in ROPED:
                    dst = {"iq": iq, "q": qT, "k": kT}[kind][:, m, :]
                    pool.wait_ge(evac, EV_S + u + 1)
                    pool.tensor_tensor(dst, roped_in[:, u % 2, :], cosT[:], ALU.mult).then_inc(cos_part, 1)
            pool.wait_ge(lo_ready, EV_N + POOL_UNIT)
            for n in range(EV_N + POOL_UNIT, EVO_N + 2):
                pool.wait_ge(hi_ready, n + 1)
                pool.tensor_tensor(w_lo[:, n % 2, 0:KT * P], raw[:, n % 4, 0:KT * P], w_hi[:, n % 2, 0:KT * P].bitcast(F32),
                                   ALU.subtract).then_inc(lo_ready, 1)
            for r in (2, 3, 4):
                add_squares(r)
            for g in range(HEADS):
                pool.wait_ge(dec_exp, g + 1)
                pool.tensor_tensor(dec_a[:], dec_a[:], beta[:, :, g:g + 1].broadcast_to([P, TT, P]), ALU.mult)\
                    .then_inc(dec_ready, 1)
                pool.tensor_tensor(dec_t[:], dec_t[:], same(const["tri"]), ALU.mult).then_inc(dec_ready, 1)
                pool.wait_ge(qk_ready, 2 * g + 2)
                for l in range(1, LEVELS + 1):
                    if l == 1:
                        pool.wait_ge(a_made, 5 * g + 1)
                    if l >= 3:
                        if l == 3:
                            pool.wait_ge(tu_ready, TU * g + 2)
                        else:
                            pool.wait_ge(y_mm, (LEVELS - 1) * g + l - 3)
                    pool.tensor_tensor(b_lvl[:, l % 2], a_mat[:], same(const[f"level{l}"]), ALU.mult).then_inc(b_made, 1)
                    if l == 2:
                        pool.tensor_tensor(q_dec[:, g % 2].rearrange("p t c -> p (t c)"), qc[:, g % 2, :],
                                           e_row[:].rearrange("p t c -> p (t c)"), ALU.mult).then_inc(qdec_ready, 1)
            for r in (5, 6):
                add_squares(r)


def shape_constants():
    i, j = np.indices((P, P))
    rot = np.zeros((P, P), np.float32)
    half = HD // 8
    for m in range(P):
        if m % HD < half:
            rot[m + half, m] = -1.0
        elif m % HD < 2 * half:
            rot[m - half, m] = 1.0
    c = {
        "ident": i == j, "ones": np.ones((P, P)), "tri": i <= j, "neg_future": np.where(j > i, NEG, 0.0),
        "rot": rot, "dup": (i == j % HD) & (i < HD),
        "dup_rot": np.where(i < HD, np.tile(rot[:, :HD], (1, 2)), 0.0),
    }
    for l in range(1, LEVELS + 1):
        s = 2 ** (l - 1)
        c[f"level{l}"] = (i // (2 * s) == j // (2 * s)) & (i // s % 2 == 1) & (j // s % 2 == 0)
    return np.ascontiguousarray(np.stack([np.asarray(c[n], np.float32) for n in CONSTS], axis=1))


def rope_frequencies():
    f = np.float32(500000.0) ** (-np.arange(0, HD // 4, 2, dtype=np.float32) / np.float32(HD // 4))
    row = np.arange(P) % HD
    return np.where(row < HD // 4, f[row % (HD // 8)], 0.0).astype(np.float32)[:, None]


def kernel(x, positions, norm_gain, ffn_w_gate, ffn_w_up, ffn_w_down, ev_w_in, ev_conv_w, ev_w_out,
           od_w_in, od_conv_w, od_a_log, od_dt_bias, od_o_gain, od_w_out, final_gain):
    import concourse.bacc as bacc
    from concourse.bass_utils import run_bass_kernel_spmd

    (x, positions, norm_gain, ffn_w_gate, ffn_w_up, ffn_w_down, ev_w_in, ev_conv_w, ev_w_out, od_w_in, od_conv_w,
     od_a_log, od_dt_bias, od_o_gain, od_w_out, final_gain) = (np.asarray(a) for a in (
         x, positions, norm_gain, ffn_w_gate, ffn_w_up, ffn_w_down, ev_w_in, ev_conv_w, ev_w_out, od_w_in, od_conv_w,
         od_a_log, od_dt_bias, od_o_gain, od_w_out, final_gain))

    def unit(w, cols):
        u = np.zeros((w.shape[0] // P, P, P), w.dtype)
        at = 0
        for lo, n in cols:
            u[:, :, at:at + n] = w[:, lo:lo + n].reshape(-1, P, n)
            at += n
        return u.transpose(1, 0, 2).reshape(P, -1)

    w8 = np.empty((ROWS8, P, KT * P), x.dtype)
    wd = np.empty((NFFN * 2 * KT, P, HALF * P), x.dtype)
    for f in range(NFFN):
        gate, up, down = (w[f // 2, f % 2] for w in (ffn_w_gate, ffn_w_up, ffn_w_down))
        for j in range(FT):
            w8[GU_ROW[f] + 2 * j] = unit(gate, [(j * P, P)])
            w8[GU_ROW[f] + 2 * j + 1] = unit(up, [(j * P, P)])
        for m in range(KT):
            for half in range(2):
                wd[f * 2 * KT + 2 * m + half] = unit(down[half * HALF * P:(half + 1) * HALF * P], [(m * P, P)])
    at = {"b": 0, "c": T, "x": 2 * T, "q": 3 * T, "k": 4 * T, "v": 5 * T, "iq": 6 * T}
    for u, (kind, m) in enumerate(EV_UNITS):
        w8[EV0 + u] = unit(ev_w_in[0], [(7 * T, HD + HEADS)] if kind == "ik" else [(at[kind] + m * P, P)])
    at = {"q": 0, "k": D, "v": 2 * D, "z": 3 * D}
    for u, (kind, h) in enumerate(OD_UNITS):
        w8[OD0 + u] = unit(od_w_in[0], [(4 * D, 2 * HEADS)] if kind == "ba" else [(at[kind] + h * P, P)])
    for m in range(KT):
        w8[EVO0 + m] = unit(ev_w_out[0], [(m * P, P)])
        w8[ODO0 + m] = unit(od_w_out[0], [(m * P, P)])
    gains = np.concatenate([norm_gain.reshape(6, KT, P), final_gain.reshape(1, KT, P)]).transpose(2, 0, 1)

    inputs = {
        "x": x.reshape(T, D), "pos": positions.reshape(1, T), "w8": w8, "wd": wd, "gains": gains,
        "consts": shape_constants(), "eps": np.full((P, 1), EPS, np.float32), "freq": rope_frequencies(),
        "ev_conv": ev_conv_w[0].reshape(3, 4, P).transpose(2, 1, 0),
        "od_conv": od_conv_w[0].reshape(4, 3 * HEADS, P).transpose(2, 1, 0),
        "alog": od_a_log.reshape(1, HEADS), "dtb": od_dt_bias.reshape(1, HEADS), "o_gain": od_o_gain.reshape(P, 1),
    }
    nc = bacc.Bacc("TRN2", target_bir_lowering=False, num_devices=1)
    arrays, aps = {}, {}
    for name, a in inputs.items():
        arrays[f"in_{name}"] = np.ascontiguousarray(a)
        aps[name] = nc.dram_tensor(f"in_{name}", a.shape, mybir.dt.from_np(a.dtype), kind="ExternalInput").ap()
    out = nc.dram_tensor("out", (T, D), F32, kind="ExternalOutput").ap()
    program(nc, aps, out)
    got = run_bass_kernel_spmd(nc, [arrays], core_ids=[0]).results[0]["out"]
    return got.reshape(1, T, D)
```
